# Optimizing a Trainium2 kernel written in Bass

```python
import math
import jax, jax.numpy as jnp
from jax import lax
import numpy as np

D_MODEL = 2048
BATCH = 1
SEQ = 256
DEPTH = 2
DEC_BATCH = 8
DEC_SEQ = 8
PAST_LEN = 2048
PAGE_SIZE = 128

N_EVEN = (DEPTH + 1) // 2
N_ODD = DEPTH // 2
NORM_EPS = 1e-5
NEG_INF = -1e30

SSD_INNER = D_MODEL
SSD_HEADDIM = 64
SSD_HEADS = SSD_INNER // SSD_HEADDIM
SSD_GROUPS = 4
SSD_STATE = 128
SSD_CONV = 4
SSD_CHUNK = 128
CONV_CH = SSD_INNER + 2 * SSD_GROUPS * SSD_STATE
SC_DIM = D_MODEL
SC_WIDTH = 3
EV_SPLITS = [SSD_INNER, CONV_CH, SSD_HEADS, SC_DIM, SC_DIM, SC_DIM, SC_DIM]
EV_IN = sum(EV_SPLITS)
EV_MIX = SSD_INNER + SC_DIM

ATT_HEADS = 16
KV_HEADS = 4
HEAD_DIM = 128
Q_PER_KV = ATT_HEADS // KV_HEADS
ATT_Q = ATT_HEADS * HEAD_DIM
ATT_KV = KV_HEADS * HEAD_DIM
ATT_IN = 2 * ATT_Q + 2 * ATT_KV
MOBA_BLOCK = 256
MOBA_TOPK = 3
MOBA_QCHUNK = 16
PAGES_PER_BLOCK = MOBA_BLOCK // PAGE_SIZE

N_MEM = 256
CA_HEADS = 4
CA_HEAD_DIM = 128
CA_W = CA_HEADS * CA_HEAD_DIM

kernel_name = 'hybrid_ssd_shortconv_moba_memxattn_step'

def _split(a, sizes):
    return jnp.split(a, [int(s) for s in np.cumsum(sizes)[:-1]], axis=-1)

def _rmsnorm(x, w):
    xf = x.astype(jnp.float32)
    y = xf * lax.rsqrt(jnp.mean(xf * xf, axis=-1, keepdims=True) + NORM_EPS)
    return (y * w.astype(jnp.float32)).astype(x.dtype)

def _alibi_slopes():
    return jnp.asarray(np.array([2.0 ** (-8.0 * (h + 1) / ATT_HEADS) for h in range(ATT_HEADS)], dtype=np.float32))

def _causal_dwconv(x, state, w):
    width = w.shape[0]
    L = x.shape[1]
    xp = jnp.concatenate([state.astype(x.dtype), x], axis=1)
    y = xp[:, 0:L] * w[0]
    for k in range(1, width):
        y = y + xp[:, k:k + L] * w[k]
    return y, xp[:, L:]

def _segsum(a):
    cs = jnp.cumsum(a, axis=-1)
    T = a.shape[-1]
    diff = cs[..., :, None] - cs[..., None, :]
    return jnp.where(jnp.tril(jnp.ones((T, T), bool)), diff, -jnp.inf)

def _ssd_scan(x, dt, a_head, b, c, h0):
    bsz, L, H, P = x.shape
    G, N = b.shape[2], b.shape[3]
    E = H // G
    Q = min(SSD_CHUNK, L)
    Lp = -(-L // Q) * Q
    if Lp != L:
        pw = Lp - L
        x = jnp.pad(x, ((0, 0), (0, pw), (0, 0), (0, 0)))
        dt = jnp.pad(dt, ((0, 0), (0, pw), (0, 0)))
        b = jnp.pad(b, ((0, 0), (0, pw), (0, 0), (0, 0)))
        c = jnp.pad(c, ((0, 0), (0, pw), (0, 0), (0, 0)))
    nc = Lp // Q
    xr = (x * dt[..., None]).reshape(bsz, nc, Q, G, E, P)
    a_t = jnp.moveaxis((dt * a_head).reshape(bsz, nc, Q, G, E), 2, -1)
    br = b.reshape(bsz, nc, Q, G, N)
    cr = c.reshape(bsz, nc, Q, G, N)
    a_cs = jnp.cumsum(a_t, axis=-1)
    lmat = jnp.exp(_segsum(a_t))
    cb = jnp.einsum('bclgn,bcsgn->bcgls', cr, br)
    y_diag = jnp.einsum('bcgls,bcgels,bcsgep->bclgep', cb, lmat, xr)
    decay_states = jnp.exp(a_cs[..., -1:] - a_cs)
    states = jnp.einsum('bclgn,bcgel,bclgep->bcgepn', br, decay_states, xr)
    states = jnp.concatenate([h0.reshape(bsz, 1, G, E, P, N), states], axis=1)
    chunk_a = jnp.pad(a_cs[..., -1], ((0, 0), (1, 0), (0, 0), (0, 0)))
    decay_chunk = jnp.exp(_segsum(jnp.moveaxis(chunk_a, 1, -1)))
    new_states = jnp.einsum('bgezc,bcgepn->bzgepn', decay_chunk, states)
    states_in, h_final = new_states[:, :-1], new_states[:, -1]
    y_off = jnp.einsum('bclgn,bcgepn,bcgel->bclgep', cr, states_in, jnp.exp(a_cs))
    y = (y_diag + y_off).reshape(bsz, Lp, H, P)[:, :L]
    return y, h_final.reshape(bsz, H, P, N)

def _even_mixer(h, w_in, conv_w, conv_b, dt_bias, a_log, d_skip, norm_w, sc_w, w_out, conv_state, ssm_state, sc_state):
    bsz, L, _ = h.shape
    f32 = jnp.float32
    z, xbc, dt_raw, sc_b, sc_c, sc_x, sc_g = _split(h @ w_in, EV_SPLITS)
    xbc, new_conv = _causal_dwconv(xbc, conv_state, conv_w)
    xbc = jax.nn.silu(xbc + conv_b)
    xs, bs, cs = _split(xbc, [SSD_INNER, SSD_GROUPS * SSD_STATE, SSD_GROUPS * SSD_STATE])
    xs = xs.reshape(bsz, L, SSD_HEADS, SSD_HEADDIM).astype(f32)
    bs = bs.reshape(bsz, L, SSD_GROUPS, SSD_STATE).astype(f32)
    cs = cs.reshape(bsz, L, SSD_GROUPS, SSD_STATE).astype(f32)
    dt = jax.nn.softplus(dt_raw.astype(f32) + dt_bias.astype(f32))
    a_head = -jnp.exp(a_log.astype(f32))
    y, new_ssm = _ssd_scan(xs, dt, a_head, bs, cs, ssm_state.astype(f32))
    y = y + d_skip.astype(f32)[:, None] * xs
    y = y.reshape(bsz, L, SSD_INNER).astype(h.dtype) * jax.nn.silu(z)
    y = _rmsnorm(y.reshape(bsz, L, SSD_GROUPS, SSD_INNER // SSD_GROUPS),
                 norm_w.reshape(SSD_GROUPS, SSD_INNER // SSD_GROUPS)).reshape(bsz, L, SSD_INNER)
    u, new_sc = _causal_dwconv(sc_c * sc_x, sc_state, sc_w)
    y_sc = sc_b * u * jax.nn.silu(sc_g)
    out = jnp.concatenate([y, y_sc], axis=-1) @ w_out
    return out, new_conv, new_ssm.astype(ssm_state.dtype), new_sc

def _attn_proj(h, w_in):
    bsz, L, _ = h.shape
    q, k, v, g = _split(h @ w_in, [ATT_Q, ATT_KV, ATT_KV, ATT_Q])
    q = q.reshape(bsz, L, ATT_HEADS, HEAD_DIM) * (HEAD_DIM ** -0.5)
    k = k.reshape(bsz, L, KV_HEADS, HEAD_DIM)
    v = v.reshape(bsz, L, KV_HEADS, HEAD_DIM)
    return q, k, v, g

def _attn_out(o, g, w_out):
    bsz, L = o.shape[0], o.shape[1]
    return (o.reshape(bsz, L, ATT_Q) * jax.nn.silu(g)) @ w_out

def _moba_attend(qg, k_own, v_own, bias_own, k_sel, v_sel, bias_sel):
    s_own = jnp.einsum('bkgqd,bknd->bkgqn', qg, k_own).astype(jnp.float32) + bias_own
    if k_sel is None:
        p = jax.nn.softmax(s_own, axis=-1).astype(v_own.dtype)
        return jnp.einsum('bkgqn,bknd->bkgqd', p, v_own)
    s_sel = jnp.einsum('bkgqd,bkgqjnd->bkgqjn', qg, k_sel).astype(jnp.float32) + bias_sel
    n_own = s_own.shape[-1]
    j, n_blk = s_sel.shape[-2], s_sel.shape[-1]
    s = jnp.concatenate([s_own, s_sel.reshape(s_sel.shape[:-2] + (j * n_blk,))], axis=-1)
    p = jax.nn.softmax(s, axis=-1).astype(v_own.dtype)
    p_sel = p[..., n_own:].reshape(s_sel.shape)
    return (jnp.einsum('bkgqn,bknd->bkgqd', p[..., :n_own], v_own)
            + jnp.einsum('bkgqjn,bkgqjnd->bkgqd', p_sel, v_sel))

def _moba_prompt(q, k, v, slopes):
    bsz, seq = q.shape[0], q.shape[1]
    nb = -(-seq // MOBA_BLOCK)
    sp = nb * MOBA_BLOCK
    padw = ((0, 0), (0, sp - seq), (0, 0), (0, 0))
    q, k, v = jnp.pad(q, padw), jnp.pad(k, padw), jnp.pad(v, padw)
    qg = q.reshape(bsz, sp, KV_HEADS, Q_PER_KV, HEAD_DIM).transpose(0, 2, 3, 1, 4)
    kb = k.reshape(bsz, nb, MOBA_BLOCK, KV_HEADS, HEAD_DIM).transpose(0, 3, 1, 2, 4)
    vb = v.reshape(bsz, nb, MOBA_BLOCK, KV_HEADS, HEAD_DIM).transpose(0, 3, 1, 2, 4)
    slope = slopes.reshape(1, KV_HEADS, Q_PER_KV, 1, 1)
    n_ch = sp // MOBA_QCHUNK

    def to_chunks(a):
        return jnp.moveaxis(a.reshape(a.shape[:3] + (n_ch, MOBA_QCHUNK) + a.shape[4:]), 3, 0)

    xs = [jnp.arange(n_ch), to_chunks(qg)]
    ksel = min(MOBA_TOPK, nb - 1)
    if ksel > 0:
        kmean = jnp.mean(kb.astype(jnp.float32), axis=3)
        gate = jnp.einsum('bkgsd,bknd->bkgsn', qg.astype(jnp.float32), kmean)
        valid = jnp.arange(nb)[None, :] < (jnp.arange(sp) // MOBA_BLOCK)[:, None]
        gate = jnp.where(valid, gate, NEG_INF)
        gval, gidx = lax.top_k(gate, ksel)
        xs += [to_chunks(gidx), to_chunks(gval > 0.5 * NEG_INF)]
    bi = jnp.arange(bsz)[:, None, None, None, None]
    ki = jnp.arange(KV_HEADS)[None, :, None, None, None]

    def chunk_fn(args):
        c, q_c = args[0], args[1]
        qpos = c * MOBA_QCHUNK + jnp.arange(MOBA_QCHUNK)
        ob = (c * MOBA_QCHUNK) // MOBA_BLOCK
        k_own = lax.dynamic_index_in_dim(kb, ob, axis=2, keepdims=False)
        v_own = lax.dynamic_index_in_dim(vb, ob, axis=2, keepdims=False)
        kpos = ob * MOBA_BLOCK + jnp.arange(MOBA_BLOCK)
        dist = (qpos[:, None] - kpos[None, :]).astype(jnp.float32)
        bias_own = jnp.where(dist >= 0, -slope * dist, NEG_INF)
        if ksel > 0:
            idx_c, ok_c = args[2], args[3]
            k_sel = kb[bi, ki, idx_c]
            v_sel = vb[bi, ki, idx_c]
            kpos_sel = idx_c[..., None] * MOBA_BLOCK + jnp.arange(MOBA_BLOCK)
            dist_sel = (qpos[:, None, None] - kpos_sel).astype(jnp.float32)
            bias_sel = jnp.where(ok_c[..., None], -slope[..., None] * dist_sel, NEG_INF)
            return _moba_attend(q_c, k_own, v_own, bias_own, k_sel, v_sel, bias_sel)
        return _moba_attend(q_c, k_own, v_own, bias_own, None, None, None)

    out = lax.map(chunk_fn, tuple(xs))
    out = jnp.moveaxis(out, 0, 3).reshape(bsz, KV_HEADS, Q_PER_KV, sp, HEAD_DIM)
    return out.transpose(0, 3, 1, 2, 4).reshape(bsz, sp, ATT_HEADS, HEAD_DIM)[:, :seq]

def _moba_sample(q, k_new, v_new, k_pool, v_pool, page_table, slopes):
    db, ds = q.shape[0], q.shape[1]
    qg = q.reshape(db, ds, KV_HEADS, Q_PER_KV, HEAD_DIM).transpose(0, 2, 3, 1, 4)
    qpos = PAST_LEN + jnp.arange(ds)
    slope = slopes.reshape(1, KV_HEADS, Q_PER_KV, 1, 1)
    k_past = k_pool[page_table].reshape(db, PAST_LEN, KV_HEADS, HEAD_DIM)
    nbf = PAST_LEN // MOBA_BLOCK
    own_start = nbf * MOBA_BLOCK
    v_own_past = v_pool[page_table[:, own_start // PAGE_SIZE:]].reshape(db, PAST_LEN - own_start, KV_HEADS, HEAD_DIM)
    k_own = jnp.concatenate([k_past[:, own_start:], k_new.astype(k_past.dtype)], axis=1).transpose(0, 2, 1, 3)
    v_own = jnp.concatenate([v_own_past, v_new.astype(v_own_past.dtype)], axis=1).transpose(0, 2, 1, 3)
    kpos = own_start + jnp.arange(k_own.shape[2])
    dist_i = qpos[:, None] - kpos[None, :]
    own_ok = (dist_i >= 0) & ((kpos[None, :] // MOBA_BLOCK) == (qpos[:, None] // MOBA_BLOCK))
    dist = dist_i.astype(jnp.float32)
    bias_own = jnp.where(own_ok, -slope * dist, NEG_INF)
    ksel = min(MOBA_TOPK, nbf)
    if ksel == 0:
        o = _moba_attend(qg, k_own, v_own, bias_own, None, None, None)
    else:
        kb = k_past[:, :own_start].reshape(db, nbf, MOBA_BLOCK, KV_HEADS, HEAD_DIM).transpose(0, 3, 1, 2, 4)
        kmean = jnp.mean(kb.astype(jnp.float32), axis=3)
        gate = jnp.einsum('bkgqd,bknd->bkgqn', qg.astype(jnp.float32), kmean)
        valid = jnp.arange(nbf)[None, :] < (qpos // MOBA_BLOCK)[:, None]
        gate = jnp.where(valid, gate, NEG_INF)
        gval, gidx = lax.top_k(gate, ksel)
        ok = gval > 0.5 * NEG_INF
        bi = jnp.arange(db)[:, None, None, None, None]
        ki = jnp.arange(KV_HEADS)[None, :, None, None, None]
        k_sel = kb[bi, ki, gidx]
        lpage = gidx[..., None] * PAGES_PER_BLOCK + jnp.arange(PAGES_PER_BLOCK)
        phys = page_table[bi[..., None], lpage]
        v_sel = v_pool[phys, :, ki[..., None], :]
        v_sel = v_sel.reshape(gidx.shape + (MOBA_BLOCK, HEAD_DIM))
        kpos_sel = gidx[..., None] * MOBA_BLOCK + jnp.arange(MOBA_BLOCK)
        dist_sel = (qpos[:, None, None] - kpos_sel).astype(jnp.float32)
        bias_sel = jnp.where(ok[..., None], -slope[..., None] * dist_sel, NEG_INF)
        o = _moba_attend(qg, k_own, v_own, bias_own, k_sel, v_sel, bias_sel)
    return o.transpose(0, 3, 1, 2, 4).reshape(db, ds, ATT_HEADS, HEAD_DIM)

def _mem_kv(mem, norm_w, w_kv):
    bsz = mem.shape[0]
    k, v = _split(_rmsnorm(mem, norm_w) @ w_kv, [CA_W, CA_W])
    return (k.reshape(bsz, N_MEM, CA_HEADS, CA_HEAD_DIM), v.reshape(bsz, N_MEM, CA_HEADS, CA_HEAD_DIM))

def _cross_attn(h, mem_k, mem_v, w_q, w_out):
    bsz, L, _ = h.shape
    q, g = _split(h @ w_q, [CA_W, CA_W])
    q = q.reshape(bsz, L, CA_HEADS, CA_HEAD_DIM) * (CA_HEAD_DIM ** -0.5)
    s = jnp.einsum('blhd,bmhd->bhlm', q, mem_k.astype(q.dtype)).astype(jnp.float32)
    p = jax.nn.softmax(s, axis=-1).astype(mem_v.dtype)
    o = jnp.einsum('bhlm,bmhd->blhd', p, mem_v).reshape(bsz, L, CA_W)
    return (o.astype(h.dtype) * jax.nn.silu(g)) @ w_out

def setup_inputs(seed: int = 0) -> dict:
    key = jax.random.key(seed)
    ks = jax.random.split(key, 32)
    f32 = jnp.float32

    def nrm(k, shape, scale=1.0):
        return jax.random.normal(k, shape, f32) * scale

    n_pages = PAST_LEN // PAGE_SIZE
    n_used = DEC_BATCH * n_pages
    n_pool = n_used + max(1, n_used // 4)
    page_table = jax.random.permutation(ks[5], n_pool)[:n_used].reshape(DEC_BATCH, n_pages).astype(jnp.int32)
    dt0 = jnp.exp(jax.random.uniform(ks[18], (N_EVEN, SSD_HEADS), f32) * (math.log(0.1) - math.log(0.001)) + math.log(0.001))
    return {
        'x_prompt': nrm(ks[0], (BATCH, SEQ, D_MODEL)),
        'x_sample': nrm(ks[1], (DEC_BATCH, DEC_SEQ, D_MODEL)),
        'mem_prompt': nrm(ks[2], (BATCH, N_MEM, D_MODEL)),
        'cache_k': nrm(ks[3], (N_ODD, n_pool, PAGE_SIZE, KV_HEADS, HEAD_DIM)),
        'cache_v': nrm(ks[4], (N_ODD, n_pool, PAGE_SIZE, KV_HEADS, HEAD_DIM)),
        'page_table': page_table,
        'state_conv': nrm(ks[6], (N_EVEN, DEC_BATCH, SSD_CONV - 1, CONV_CH)),
        'state_ssm': nrm(ks[7], (N_EVEN, DEC_BATCH, SSD_HEADS, SSD_HEADDIM, SSD_STATE), 0.5),
        'state_sc': nrm(ks[8], (N_EVEN, DEC_BATCH, SC_WIDTH - 1, SC_DIM)),
        'cache_mem_k': nrm(ks[9], (DEPTH, DEC_BATCH, N_MEM, CA_HEADS, CA_HEAD_DIM)),
        'cache_mem_v': nrm(ks[10], (DEPTH, DEC_BATCH, N_MEM, CA_HEADS, CA_HEAD_DIM)),
        'norm_mix_w': 1.0 + nrm(ks[11], (DEPTH, D_MODEL), 0.02),
        'norm_cross_w': 1.0 + nrm(ks[12], (DEPTH, D_MODEL), 0.02),
        'norm_mem_w': 1.0 + nrm(ks[13], (DEPTH, D_MODEL), 0.02),
        'final_norm_w': 1.0 + nrm(ks[14], (D_MODEL,), 0.02),
        'ev_w_in': nrm(ks[15], (N_EVEN, D_MODEL, EV_IN), D_MODEL ** -0.5),
        'ev_conv_w': nrm(ks[16], (N_EVEN, SSD_CONV, CONV_CH), SSD_CONV ** -0.5),
        'ev_conv_b': nrm(ks[17], (N_EVEN, CONV_CH), 0.01),
        'ev_dt_bias': dt0 + jnp.log(-jnp.expm1(-dt0)),
        'ev_a_log': jnp.log(jax.random.uniform(ks[19], (N_EVEN, SSD_HEADS), f32, 1.0, 16.0)),
        'ev_d_skip': 1.0 + nrm(ks[20], (N_EVEN, SSD_HEADS), 0.1),
        'ev_norm_w': 1.0 + nrm(ks[21], (N_EVEN, SSD_INNER), 0.02),
        'ev_sc_w': nrm(ks[22], (N_EVEN, SC_WIDTH, SC_DIM), SC_WIDTH ** -0.5),
        'ev_w_out': nrm(ks[23], (N_EVEN, EV_MIX, D_MODEL), EV_MIX ** -0.5),
        'od_w_in': nrm(ks[24], (N_ODD, D_MODEL, ATT_IN), D_MODEL ** -0.5),
        'od_w_out': nrm(ks[25], (N_ODD, ATT_Q, D_MODEL), ATT_Q ** -0.5),
        'ca_w_q': nrm(ks[26], (DEPTH, D_MODEL, 2 * CA_W), D_MODEL ** -0.5),
        'ca_w_kv': nrm(ks[27], (DEPTH, D_MODEL, 2 * CA_W), D_MODEL ** -0.5),
        'ca_w_out': nrm(ks[28], (DEPTH, CA_W, D_MODEL), CA_W ** -0.5),
    }

def reference(x_prompt, x_sample, mem_prompt, cache_k, cache_v, page_table, state_conv, state_ssm, state_sc,
              cache_mem_k, cache_mem_v, norm_mix_w, norm_cross_w, norm_mem_w, final_norm_w,
              ev_w_in, ev_conv_w, ev_conv_b, ev_dt_bias, ev_a_log, ev_d_skip, ev_norm_w, ev_sc_w, ev_w_out,
              od_w_in, od_w_out, ca_w_q, ca_w_kv, ca_w_out):
    slopes = _alibi_slopes()
    bp = x_prompt.shape[0]
    xp, xs = x_prompt, x_sample
    pk, pv, sk, sv = [], [], [], []
    pconv, pssm, psc, sconv, sssm, ssc = [], [], [], [], [], []
    pmk, pmv = [], []
    for l in range(DEPTH):
        i = l // 2
        hp = _rmsnorm(xp, norm_mix_w[l])
        hs = _rmsnorm(xs, norm_mix_w[l])
        if l % 2 == 0:
            w = (ev_w_in[i], ev_conv_w[i], ev_conv_b[i], ev_dt_bias[i], ev_a_log[i], ev_d_skip[i], ev_norm_w[i], ev_sc_w[i], ev_w_out[i])
            z_conv = jnp.zeros((bp, SSD_CONV - 1, CONV_CH), x_prompt.dtype)
            z_ssm = jnp.zeros((bp, SSD_HEADS, SSD_HEADDIM, SSD_STATE), state_ssm.dtype)
            z_sc = jnp.zeros((bp, SC_WIDTH - 1, SC_DIM), x_prompt.dtype)
            op, c1, s1, q1 = _even_mixer(hp, *w, z_conv, z_ssm, z_sc)
            os_, c2, s2, q2 = _even_mixer(hs, *w, state_conv[i], state_ssm[i], state_sc[i])
            pconv.append(c1); pssm.append(s1); psc.append(q1)
            sconv.append(c2); sssm.append(s2); ssc.append(q2)
        else:
            q1, k1, v1, g1 = _attn_proj(hp, od_w_in[i])
            op = _attn_out(_moba_prompt(q1, k1, v1, slopes), g1, od_w_out[i])
            q2, k2, v2, g2 = _attn_proj(hs, od_w_in[i])
            os_ = _attn_out(_moba_sample(q2, k2, v2, cache_k[i], cache_v[i], page_table, slopes), g2, od_w_out[i])
            pk.append(k1); pv.append(v1); sk.append(k2); sv.append(v2)
        xp = xp + op
        xs = xs + os_
        mk, mv = _mem_kv(mem_prompt, norm_mem_w[l], ca_w_kv[l])
        pmk.append(mk); pmv.append(mv)
        xp = xp + _cross_attn(_rmsnorm(xp, norm_cross_w[l]), mk, mv, ca_w_q[l], ca_w_out[l])
        xs = xs + _cross_attn(_rmsnorm(xs, norm_cross_w[l]), cache_mem_k[l], cache_mem_v[l], ca_w_q[l], ca_w_out[l])
    y_prompt = _rmsnorm(xp, final_norm_w)
    y_sample = _rmsnorm(xs, final_norm_w)
    return (y_prompt, y_sample,
            jnp.stack(pk), jnp.stack(pv), jnp.stack(pconv), jnp.stack(pssm), jnp.stack(psc),
            jnp.stack(pmk), jnp.stack(pmv),
            jnp.stack(sk), jnp.stack(sv), jnp.stack(sconv), jnp.stack(sssm), jnp.stack(ssc))


_drawn_inputs = setup_inputs


def setup_inputs(seed=0):
    import zlib

    import numpy as np

    out = dict(_drawn_inputs(seed))
    spreads = {}
    factors = {'norm_cross_w': 8.0,
     'norm_mem_w': 2.872,
     'final_norm_w': 2.776,
     'ev_conv_b': 3.196,
     'ev_norm_w': 4.438}
    for name, (base, spread) in spreads.items():
        noise = np.random.default_rng([zlib.crc32(name.encode()), seed]).standard_normal(out[name].shape)
        drawn = base * np.exp(spread * noise) if base else spread * noise
        out[name] = __import__('jax').numpy.asarray(drawn.astype(out[name].dtype))
    for name, factor in factors.items():
        out[name] = (out[name] * factor).astype(out[name].dtype)
    return out
```

```python
from contextlib import ExitStack, contextmanager

import numpy as np
import concourse.bass as bass
from concourse import mybir

F32 = mybir.dt.float32
I32 = mybir.dt.int32
ACT = mybir.ActivationFunctionType
ALU = mybir.AluOpType
AX = mybir.AxisListType
ds = bass.ds

D = 2048
KC = D // 128
TP = 256
NB, TS = 8, 8
TSA = NB * TS
T = TP + TSA
EPS = 1e-5
NEG = -1e30
SSD_HEADS, HD, GROUPS, NST = 32, 64, 4, 128
CONV_CH = 3072
CCH = CONV_CH // 128
CW, SCW = 4, 3
OFF_Z, OFF_XBC, OFF_DT, OFF_SC = 0, 2048, 5120, 5152
AH, KVH, DH, G4 = 16, 4, 128, 4
PAST, PAGE, BLK = 2048, 128, 256
NPG, NBLK, TOPK = PAST // PAGE, PAST // BLK, 3
NM, CAH = 256, 4
QSCALE = float(DH) ** -0.5
NSLOT = 4

C_ID, C_ONE, C_TRIP, C_TRIS, C_BLKS, C_BM, C_SLOPE, C_TIE = 0, 128, 256, 384, 448, 512, 520, 536
C_N = 600
VA_MIX, VA_CROSS, VA_MEM, VA_FIN, VA_EV, VA_N = 0, 32, 64, 96, 112, 128
VB_CW, VB_CB, VB_N = 0, 96, 120
VC_N = 48


def host_constants():
    f = np.float32
    c = np.zeros((128, C_N), f)
    c[:, C_ID:C_ID + 128] = np.eye(128)
    c[:, C_ONE:C_ONE + 128] = 1
    s, l = np.arange(128)[:, None], np.arange(128)[None, :]
    c[:, C_TRIP:C_TRIP + 128] = s <= l
    same = (np.arange(64)[:, None] // TS) == (np.arange(64)[None, :] // TS)
    c[:64, C_TRIS:C_TRIS + 64] = same & (np.arange(64)[:, None] <= np.arange(64)[None, :])
    c[:64, C_BLKS:C_BLKS + 64] = same
    c[:64, C_BM:C_BM + 8] = (np.arange(64)[:, None] // TS) == np.arange(8)[None, :]
    slopes = np.array([2.0 ** (-8.0 * (h + 1) / AH) for h in range(AH)], dtype=f)
    c[:, C_SLOPE:C_SLOPE + AH] = slopes[None]
    c[:, C_TIE:C_TIE + 64] = (np.arange(8)[None, :] < np.arange(8)[:, None]).reshape(1, 64)
    q = np.arange(2)[None, :, None] * 128 + np.arange(128)[:, None, None]
    k = np.arange(256)[None, None, :]
    dist = np.where(q >= k, (k - q).astype(f), f(NEG)).astype(f).reshape(128, 512)
    head, tok = np.arange(128) // TS, np.arange(128) % TS
    past = (-slopes[head][:, None] * (PAST + tok[:, None] - np.arange(PAST)[None]).astype(f)).astype(f)
    col = np.arange(64)
    own = np.full((128, NB, 64), NEG, f)
    for b in range(NB):
        d = tok[:, None] - (col[None] - TS * b)
        ok = (col[None] // TS == b) & (d >= 0)
        own[:, b] = np.where(ok, -slopes[head][:, None] * d.astype(f), f(NEG))
    qmask = np.broadcast_to((col[None] // TS == np.arange(NB)[:, None]).astype(f).reshape(1, 512), (128, 512))
    selhp = np.zeros((32, 2048), f)
    selhp[np.arange(2048) // HD, np.arange(2048)] = 1
    return {"c_main": c, "c_dist": dist, "c_past": past, "c_own": own.reshape(128, 512),
            "c_qmask": np.ascontiguousarray(qmask), "c_selhp": selhp}


class Trunk:

    def __init__(self, nc, d):
        self.nc, self.d = nc, d
        self.event = 0
        self.tile = 0
        self.uses = 0
        self.freed = [0] * NSLOT


@contextmanager
def stage(nc, label, names):
    sems = {n: nc.alloc_semaphore(name=f"{label}_{n}") for n in names}
    yield sems
    nc.clear_and_free_semaphores(list(sems.values()))
    nc.all_engine_barrier()


class Proj:

    def __init__(self, e, w_src, tiles, ntok=T, kch=KC, slots_per_tile=1, tiles_per_slot=1):
        self.e, self.w_src, self.tiles, self.ntok, self.kch = e, w_src, tiles, ntok, kch
        self.spt, self.tps = slots_per_tile, tiles_per_slot
        self.slots = tiles * slots_per_tile // tiles_per_slot
        self.body_tiles = 4 if tiles_per_slot == 1 else 16
        self.body_slots = self.body_tiles * self.spt // self.tps
        self.body_events = self.body_tiles * self.spt
        self.iters = tiles // self.body_tiles
        self.event0, self.tile0, self.uses0 = e.event, e.tile, e.uses
        self.prev_freed = list(e.freed)
        e.event += tiles * self.spt
        e.tile += tiles
        e.uses += self.slots // NSLOT
        per = self.tps if self.tps > 1 else 1
        for j in range(NSLOT):
            e.freed[j] = self.event0 + (self.slots - NSLOT + j + 1) * per

    def first_loads(self, sp):
        for j in range(NSLOT):
            if self.prev_freed[j]:
                sp.wait_ge(self.e.pe_event, NSLOT + self.prev_freed[j])
            src, kch, cols = self.w_src(0, j)
            sp.dma_start(self.e.slot_view(j, kch, cols), src).then_inc(self.e.w_landed[j], 16)

    def later_loads(self, sp):
        e, per = self.e, (self.tps if self.tps > 1 else 1)
        n = self.slots - NSLOT
        if n <= 0:
            return
        with sp.Fori(0, n // NSLOT) as i:
            for j in range(NSLOT):
                sp.wait_ge(e.pe_event, i * (NSLOT * per) + (NSLOT + self.event0 + (j + 1) * per))
                src, kch, cols = self.w_src(i + 1, j)
                sp.dma_start(e.slot_view(j, kch, cols), src).then_inc(e.w_landed[j], 16)

    def loop(self, eng, body):
        if self.iters == 1:
            body(0)
        else:
            with eng.Fori(0, self.iters) as i:
                body(i)

    def matmuls(self, pe, rhs):
        e = self.e

        def body(i):
            for j in range(self.body_tiles):
                for h in range(self.spt):
                    s = (j * self.spt + h) // self.tps
                    if j % self.tps == 0:
                        pe.wait_ge(e.w_landed[s % NSLOT],
                                   i * (16 * self.body_slots // NSLOT) + 16 * (self.uses0 + s // NSLOT + 1))
                    if h == 0:
                        pe.wait_ge(e.bank_free, i * self.body_tiles + (self.tile0 + j + 1))
                    w = e.slot_view(s % NSLOT, self.kch, 128 * self.tps)
                    for k in range(self.kch):
                        m = e.nc.tensor.matmul(
                            e.bank[j % NSLOT][:, 0:self.ntok], w[:, k, 128 * (j % self.tps):128 * (j % self.tps) + 128],
                            rhs(h * self.kch + k), start=(h == 0 and k == 0),
                            stop=(h == self.spt - 1 and k == self.kch - 1))
                    m.then_inc(e.pe_event, 1)

        self.loop(pe, body)

    def take_over(self, eng):
        eng.wait_ge(self.e.bank_free, NSLOT + self.tile0)

    def wait_tile(self, eng, i, j):
        eng.wait_ge(self.e.pe_event, i * self.body_events + (NSLOT + self.event0 + (j + 1) * self.spt))


def columns(w, off=0, step=128):
    wv = w.rearrange("(c p) n -> p c n", p=128)

    def src(i, j):
        return wv[:, :, ds(i * (NSLOT * step) + (off + j * step), 128)], KC, 128
    return src


def two_slot_columns(w):
    wv = w.rearrange("(h c p) n -> p h c n", h=2, p=128)

    def src(i, j):
        return wv[:, j % 2, :, ds(i * 256 + (j // 2) * 128, 128)], KC, 128
    return src


def wide_columns(w):
    wv = w.rearrange("(c p) n -> p c n", p=128)

    def src(i, j):
        return wv[:, :, 512 * j:512 * j + 512], 4, 512
    return src


def sc_columns(w):
    wv = w.rearrange("(c p) n -> p c n", p=128)

    def src(i, j):
        return wv[:, :, ds(i * 128 + (OFF_SC + j * D), 128)], KC, 128
    return src


def transposes(e, block, s, fills):
    nc = e.nc
    evac = ("evac_v", "evac_s")

    def tensor(pe):
        for f, (parts, rows, _, _) in enumerate(fills):
            if f >= 8:
                pe.wait_ge(s[evac[f % 2]], (f - 8) // 2 + 1)
            for col, src, k, m in parts:
                t = nc.tensor.transpose(e.bank[f % 8][0:m, col:col + k], src, e.ident[0:k, 0:k])
            t.then_inc(s["turned"], 1)

    def copies(eng, par):
        for f, (_, rows, width, out) in enumerate(fills):
            if f % 2 == par:
                eng.wait_ge(s["turned"], f + 1)
                src = e.bank[f % 8][0:rows, 0:width]
                if len(out.shape) == 3:
                    src = src.rearrange("p (a b) -> p a b", a=out.shape[1])
                if par:
                    nc.scalar.activation(out, src, ACT.Copy).then_inc(s["evac_s"], 1)
                else:
                    nc.vector.tensor_copy(out, src).then_inc(s["evac_v"], 1)

    return tensor, copies


def setup(e):
    nc, d = e.nc, e.d
    with ExitStack() as ctx:
        sb = lambda n, sh: ctx.enter_context(nc.sbuf_tensor(n, sh, F32))
        s = ctx.enter_context(stage(nc, "setup", ["consts_in", "zeroed", "rows_in", "x_in", "mem_in", "turned", "evac_v", "evac_s"]))
        rows = sb("vec_rows", [128, 3, 128])
        xr = sb("x_rows", [128, 3, D])
        mr = sb("mem_rows", [128, 2, D])
        fills = [([(0, rows[:, 0, :], 128, 128)], 128, 128, e.va[:]),
                 ([(0, rows[0:VB_N, 1, :], VB_N, 128)], 128, VB_N, e.vb[:]),
                 ([(0, rows[0:VC_N, 2, :], VC_N, 128)], 128, VC_N, e.vc[:])]
        nvec = len(fills)
        for c in range(KC):
            cs = slice(128 * c, 128 * c + 128)
            fills.append(([(0, xr[:, 0, cs], 128, 128), (128, xr[:, 1, cs], 128, 128),
                           (256, xr[0:64, 2, cs], 64, 128)], 128, T, e.xt[:, c, :]))
        nx = len(fills)
        for c in range(0, KC, 2):
            fills.append(([(128 * (2 * a + m), mr[:, m, 128 * (c + a):128 * (c + a) + 128], 128, 128)
                           for a in range(2) for m in range(2)], 128, 512, e.memt[:, c:c + 2, :]))
        tensor, copies = transposes(e, None, s, fills)
        with nc.Block() as block:
            @block.sync
            def _(sp):
                sp.dma_start(e.const[:], d["c_main"]).then_inc(s["consts_in"], 16)
                vec = [("norm_mix_w", 0, VA_MIX), ("norm_cross_w", 0, VA_CROSS), ("norm_mem_w", 0, VA_MEM),
                       ("final_norm_w", 0, VA_FIN), ("ev_norm_w", 0, VA_EV),
                       ("ev_conv_w", 1, VB_CW), ("ev_conv_b", 1, VB_CB), ("ev_sc_w", 2, 0)]
                for name, t, row in vec:
                    a = d[name]
                    if len(a.shape) > 1:
                        a = a.rearrange("a b -> (a b)" if len(a.shape) == 2 else "a b c -> (a b c)")
                    n = a.shape[0] // 128
                    sp.dma_start(rows[row:row + n, t, :], a.rearrange("(r p) -> r p", p=128)).then_inc(s["rows_in"], 16)
                sp.dma_start(xr[:, 0:2, :], d["x_prompt"][0].rearrange("(t p) n -> p t n", p=128)).then_inc(s["x_in"], 16)
                sp.dma_start(xr[0:64, 2, :], d["x_sample"].rearrange("b t n -> (b t) n")).then_inc(s["x_in"], 16)
                sp.dma_start(mr[:], d["mem_prompt"][0].rearrange("(t p) n -> p t n", p=128)).then_inc(s["mem_in"], 16)
                e.next_proj.first_loads(sp)

            @block.tensor
            def _(pe):
                pe.sem_inc(e.pe_event, NSLOT)
                pe.wait_ge(s["consts_in"], 16)
                pe.wait_ge(s["rows_in"], 16 * 8)
                pe.wait_ge(s["x_in"], 32)
                pe.wait_ge(s["mem_in"], 16)
                tensor(pe)

            @block.vector
            def _(dve):
                dve.sem_inc(e.bank_free, NSLOT)
                copies(dve, 0)

            @block.scalar
            def _(act):
                copies(act, 1)


def rmsnorm(e, label, src, ntok, wcol, dst):
    nc = e.nc
    with ExitStack() as ctx:
        s = ctx.enter_context(stage(nc, label, ["squared_v", "squared_s", "summed", "var", "std", "rstd", "normed"]))
        r = ctx.enter_context(nc.sbuf_tensor(f"{label}_r", [128, T], F32))
        with nc.Block() as block:
            @block.scalar
            def _(act):
                for c in range(1, KC, 2):
                    nc.scalar.activation(dst[:, c, 0:ntok], src[:, c, 0:ntok], ACT.Square).then_inc(s["squared_s"], 1)
                act.wait_ge(s["var"], 1)
                nc.scalar.activation(r[:, 0:ntok], r[:, 0:ntok], ACT.Sqrt).then_inc(s["std"], 1)

            @block.tensor
            def _(pe):
                for c in range(KC):
                    pe.wait_ge(s["squared_s" if c % 2 else "squared_v"], c // 2 + 1)
                    m = nc.tensor.matmul(e.bank[4][:, 0:ntok], e.ones[:, :], dst[:, c, 0:ntok], start=c == 0, stop=c == KC - 1)
                m.then_inc(s["summed"], 1)

            @block.vector
            def _(dve):
                for c in range(0, KC, 2):
                    nc.vector.tensor_tensor(dst[:, c, 0:ntok], src[:, c, 0:ntok], src[:, c, 0:ntok], ALU.mult).then_inc(s["squared_v"], 1)
                dve.wait_ge(s["summed"], 1)
                nc.vector.tensor_scalar(r[:, 0:ntok], e.bank[4][:, 0:ntok], 1.0 / D, EPS, ALU.mult, ALU.add).then_inc(s["var"], 1)
                dve.wait_ge(s["std"], 1)
                nc.vector.reciprocal(r[:, 0:ntok], r[:, 0:ntok]).then_inc(s["rstd"], 1)
                dve.wait_ge(s["rstd"], 1)
                for c in range(KC):
                    nc.vector.scalar_tensor_tensor(dst[:, c, 0:ntok], src[:, c, 0:ntok], e.va[:, wcol + c:wcol + c + 1],
                                                   r[:, 0:ntok], ALU.mult, ALU.mult).then_inc(s["normed"], 1)


def memory_kv(e, layer, p, nxt):
    nc, d = e.nc, e.d
    rmsnorm(e, f"norm_mem{layer}", e.memt, NM, VA_MEM + KC * layer, e.h)
    km, vm = e.km[layer], e.vm[layer]
    with ExitStack() as ctx:
        sb = lambda n, sh: ctx.enter_context(nc.sbuf_tensor(n, sh, F32))
        s = ctx.enter_context(stage(nc, f"mem{layer}", ["turned", "evac_v", "evac_s", "stored"]))
        vt = sb(f"mem{layer}_vt", [128, CAH, NM])
        kr = sb(f"mem{layer}_krows", [128, 2, 512])
        with nc.Block() as block:
            @block.sync
            def _(sp):
                p.later_loads(sp)
                nxt.first_loads(sp)

            @block.tensor
            def _(pe):
                p.matmuls(pe, lambda k: e.h[:, k, 0:NM])

            @block.scalar
            def _(act):
                for i in range(2):
                    for j in range(4):
                        p.wait_tile(act, i, j)
                        nc.scalar.activation((vt if i else km)[:, j, :], e.bank[j][:, 0:NM], ACT.Copy).then_inc(e.bank_free, 1)
        fills = [([(128 * h, (vt if v else km)[:, h, 128 * m:128 * m + 128], 128, 128) for h in range(CAH)], 128, 512,
                  (vm if v else kr)[:, m, :]) for v in range(2) for m in range(2)]
        tensor, copies = transposes(e, None, s, fills)
        with nc.Block() as block:
            block.tensor(tensor)
            block.vector(lambda eng: copies(eng, 0))
            block.scalar(lambda eng: copies(eng, 1))

            @block.gpsimd
            def _(pool):
                pool.wait_ge(s["evac_v"], 2)
                pool.wait_ge(s["evac_s"], 2)
                for name, src in (("mem_k_o", kr), ("mem_v_o", vm)):
                    pool.dma_start(d[name][layer, 0].rearrange("(t p) h n -> p t (h n)", p=128), src[:]).then_inc(s["stored"], 16)
                pool.wait_ge(s["stored"], 32)


def even_projections(e, p_z, p_xbc, p_sc, nxt):
    nc, d = e.nc, e.d
    with ExitStack() as ctx:
        sb = lambda n, sh: ctx.enter_context(nc.sbuf_tensor(n, sh, F32))
        crows = sb("conv_tail_rows", [27, CONV_CH])
        srows = sb("sc_tail_rows", [18, D])
        tail = sb("conv_tail", [128, CCH, 27])
        sctail = sb("sc_tail", [128, KC, 18])
        with ExitStack() as c2:
            sb2 = lambda n, sh: c2.enter_context(nc.sbuf_tensor(n, sh, F32))
            conv_hist = sb2("conv_hist", [128, CCH, 24])
            sc_hist = sb2("sc_hist", [128, KC, 16])
            s = c2.enter_context(stage(nc, "hist", ["conv_in", "sc_in", "turned", "evac_v", "evac_s"]))
            fills = [([(24 * (c - c0), crows[0:24, 128 * c:128 * c + 128], 24, 128) for c in range(c0, c0 + 12)], 128, 288,
                      conv_hist[:, c0:c0 + 12, :]) for c0 in (0, 12)]
            fills.append(([(16 * c, srows[0:16, 128 * c:128 * c + 128], 16, 128) for c in range(KC)], 128, 256, sc_hist[:]))
            tensor, copies = transposes(e, None, s, fills)
            with nc.Block() as block:
                @block.sync
                def _(sp):
                    sp.dma_start(crows[0:24, :], d["state_conv"][0].rearrange("b j n -> (b j) n")).then_inc(s["conv_in"], 16)
                    sp.dma_start(srows[0:16, :], d["state_sc"][0].rearrange("b j n -> (b j) n")).then_inc(s["sc_in"], 16)

                @block.tensor
                def _(pe):
                    pe.wait_ge(s["conv_in"], 16)
                    pe.wait_ge(s["sc_in"], 16)
                    tensor(pe)
                block.vector(lambda eng: copies(eng, 0))
                block.scalar(lambda eng: copies(eng, 1))

            t = c2.enter_context(stage(nc, "even", ["dt_w_in", "dt_done", "dt_raw", "step", "silu_done", "padded"]))
            xpp = [sb2(f"conv_pad{i}", [128, CW - 1 + TP]) for i in range(2)]
            xps = [sb2(f"conv_pad_s{i}", [128, NB, CW - 1 + TS]) for i in range(2)]
            acc = [sb2(f"conv_acc{i}", [128, T]) for i in range(2)]
            part = [sb2(f"sc_part{i}", [128, T]) for i in range(4)]
            wdt = sb2("w_dt", [128, KC, SSD_HEADS])
            CONV_STEPS, SC_STEPS = 12, 13
            conv0 = 3
            sc0 = conv0 + CCH * CONV_STEPS
            with nc.Block() as block:
                @block.sync
                def _(sp):
                    sp.dma_start(wdt[:], d["ev_w_in"][0].rearrange("(c p) n -> p c n", p=128)[:, :, OFF_DT:OFF_DT + SSD_HEADS]).then_inc(t["dt_w_in"], 16)
                    p_z.later_loads(sp)
                    p_xbc.first_loads(sp)
                    p_xbc.later_loads(sp)
                    p_sc.first_loads(sp)
                    p_sc.later_loads(sp)
                    nxt.first_loads(sp)

                @block.tensor
                def _(pe):
                    pe.wait_ge(t["dt_w_in"], 16)
                    for u in range(3):
                        rows = 128 if u < 2 else TSA
                        for k in range(KC):
                            m = nc.tensor.matmul(e.bank[4][0:rows, 32 * u:32 * u + 32], e.h[:, k, 128 * u:128 * u + rows],
                                                 wdt[:, k, :], start=k == 0, stop=k == KC - 1)
                        m.then_inc(t["dt_done"], 1)
                    for p in (p_z, p_xbc, p_sc):
                        p.matmuls(pe, lambda k: e.h[:, k, :])

                @block.scalar
                def _(act):
                    act.sem_inc(t["silu_done"], 2)
                    p_z.take_over(act)
                    with act.Fori(0, p_z.iters) as i:
                        for j in range(4):
                            p_z.wait_tile(act, i, j)
                            nc.scalar.activation(e.zs[:, ds(4 * i + j, 1), :], e.bank[j][:, 0:T].unsqueeze(1), ACT.Silu).then_inc(e.bank_free, 1)
                    with act.Fori(0, p_xbc.iters) as i:
                        for j in range(4):
                            act.wait_ge(t["step"], i * (4 * CONV_STEPS) + (conv0 + j * CONV_STEPS + 10))
                            nc.scalar.activation(e.xbc[:, ds(4 * i + j, 1), :], acc[j % 2][:].unsqueeze(1), ACT.Silu,
                                                 bias=e.vb[:, ds(4 * i + (VB_CB + j), 1)]).then_inc(t["silu_done"], 1)
                    p_sc.take_over(act)
                    with act.Fori(0, p_sc.iters) as i:
                        act.wait_ge(t["step"], i * SC_STEPS + sc0)
                        for j in range(4):
                            p_sc.wait_tile(act, i, j)
                            nc.scalar.activation(part[j][:], e.bank[j][:, 0:T], ACT.Silu if j == 3 else ACT.Copy).then_inc(e.bank_free, 1)

                @block.vector
                def _(dve):
                    v = nc.vector
                    dve.wait_ge(t["dt_done"], 3)
                    v.tensor_copy(e.dt[:, 0:2, :], e.bank[4][:, 0:64].rearrange("p (u h) -> p u h", u=2)).then_inc(t["dt_raw"], 1)
                    v.tensor_copy(e.dt[0:TSA, 2, :], e.bank[4][0:TSA, 64:96]).then_inc(t["step"], 1)
                    v.memset(xpp[0][:, 0:CW - 1], 0.0).then_inc(t["step"], 1)
                    v.memset(xpp[1][:, 0:CW - 1], 0.0).then_inc(t["step"], 1)
                    p_xbc.take_over(dve)
                    with dve.Fori(0, p_xbc.iters) as i:
                        for j in range(4):
                            n = [conv0 + j * CONV_STEPS]

                            def step(ins):
                                ins.then_inc(t["step"], 1)
                                n[0] += 1

                            def settled(k=0):
                                dve.wait_ge(t["step"], i * (4 * CONV_STEPS) + (n[0] - k))

                            xp, xs, y = xpp[j % 2], xps[j % 2], acc[j % 2]
                            ys = y[:, TP:T].rearrange("p (b t) -> p b t", b=NB)
                            p_xbc.wait_tile(dve, i, j)
                            step(v.tensor_copy(xp[:, 3:3 + TP], e.bank[j][:, 0:TP]))
                            v.tensor_copy(xs[:, :, 3:11], e.bank[j][:, TP:T].rearrange("p (b t) -> p b t", b=NB)).then_inc(e.bank_free, 1)
                            step(v.tensor_scalar(xs[:, :, 0:3], conv_hist[:, ds(4 * i + j, 1), :].rearrange("p c (b t) -> p (c b) t", b=NB),
                                                 1.0, None, ALU.mult))
                            settled()
                            dve.wait_ge(t["silu_done"], i * 4 + (j + 1))
                            for k in range(CW):
                                wk = e.vb[:, ds(4 * i + (VB_CW + k * CCH + j), 1)]
                                if k == 0:
                                    step(v.tensor_scalar(y[:, 0:TP], xp[:, 0:TP], wk, None, ALU.mult))
                                    step(v.tensor_scalar(ys, xs[:, :, 0:TS], wk, None, ALU.mult))
                                else:
                                    settled(1)
                                    step(v.scalar_tensor_tensor(y[:, 0:TP], xp[:, k:k + TP], wk, y[:, 0:TP], ALU.mult, ALU.add))
                                    settled(1)
                                    step(v.scalar_tensor_tensor(ys, xs[:, :, k:k + TS], wk, ys, ALU.mult, ALU.add))
                            step(v.tensor_scalar(tail[:, ds(4 * i + j, 1), 0:3], xp[:, TP:TP + 3].unsqueeze(1), 1.0, None, ALU.mult))
                            step(v.tensor_scalar(tail[:, ds(4 * i + j, 1), 3:27].rearrange("p c (b t) -> p (c b) t", b=NB),
                                                 xs[:, :, TS:TS + 3], 1.0, None, ALU.mult))
                            assert n[0] == conv0 + (j + 1) * CONV_STEPS
                    xp, xs, y = xpp[0], xps[0], acc[0]
                    ys = y[:, TP:T].rearrange("p (b t) -> p b t", b=NB)
                    xs3 = xs[:, :, 0:SCW - 1 + TS]
                    dve.wait_ge(t["silu_done"], 2 + CCH)
                    with dve.Fori(0, p_sc.iters) as i:
                        n = [sc0]

                        def step(ins):
                            ins.then_inc(t["step"], 1)
                            n[0] += 1

                        def settled(k=0):
                            dve.wait_ge(t["step"], i * SC_STEPS + (n[0] - k))

                        fp = lambda a: a[:, 0:TP]
                        fs = lambda a: a[:, TP:T].rearrange("p (b t) -> p b t", b=NB)
                        step(v.tensor_scalar(xs3[:, :, 0:2], sc_hist[:, ds(i, 1), :].rearrange("p c (b t) -> p (c b) t", b=NB),
                                             1.0, None, ALU.mult))
                        dve.wait_ge(e.bank_free, i * 4 + (NSLOT + p_sc.tile0 + 3))
                        step(v.tensor_tensor(xp[:, 2:2 + TP], fp(part[1]), fp(part[2]), ALU.mult))
                        step(v.tensor_tensor(xs3[:, :, 2:10], fs(part[1]), fs(part[2]), ALU.mult))
                        settled()
                        for k in range(SCW):
                            wk = e.vc[:, ds(i + k * KC, 1)]
                            if k == 0:
                                step(v.tensor_scalar(y[:, 0:TP], xp[:, 0:TP], wk, None, ALU.mult))
                                step(v.tensor_scalar(ys, xs3[:, :, 0:TS], wk, None, ALU.mult))
                            else:
                                settled(1)
                                step(v.scalar_tensor_tensor(y[:, 0:TP], xp[:, k:k + TP], wk, y[:, 0:TP], ALU.mult, ALU.add))
                                settled(1)
                                step(v.scalar_tensor_tensor(ys, xs3[:, :, k:k + TS], wk, ys, ALU.mult, ALU.add))
                        step(v.tensor_scalar(sctail[:, ds(i, 1), 0:2], xp[:, TP:TP + 2].unsqueeze(1), 1.0, None, ALU.mult))
                        step(v.tensor_scalar(sctail[:, ds(i, 1), 2:18].rearrange("p c (b t) -> p (c b) t", b=NB),
                                             xs3[:, :, TS:TS + 2], 1.0, None, ALU.mult))
                        settled(2)
                        step(v.tensor_tensor(y[:], y[:], part[0][:], ALU.mult))
                        settled()
                        dve.wait_ge(e.bank_free, i * 4 + (NSLOT + p_sc.tile0 + 4))
                        step(v.tensor_tensor(e.ysc[:, ds(i, 1), :], y[:].unsqueeze(1), part[3][:].unsqueeze(1), ALU.mult))
                        assert n[0] == sc0 + SC_STEPS
        s = ctx.enter_context(stage(nc, "tails", ["turned", "evac_v", "evac_s", "stored"]))
        fills = [([(128 * a, tail[:, c + a, :], 128, 27) for a in range(4)], 27, 512, crows[:, 128 * c:128 * c + 512])
                 for c in range(0, CCH, 4)]
        fills += [([(128 * a, sctail[:, c + a, :], 128, 18) for a in range(4)], 18, 512, srows[:, 128 * c:128 * c + 512])
                  for c in range(0, KC, 4)]
        tensor, copies = transposes(e, None, s, fills)
        with nc.Block() as block:
            block.tensor(tensor)
            block.vector(lambda eng: copies(eng, 0))
            block.scalar(lambda eng: copies(eng, 1))

            @block.gpsimd
            def _(pool):
                pool.wait_ge(s["evac_v"], 5)
                pool.wait_ge(s["evac_s"], 5)
                pool.dma_start(d["conv_prompt_o"][0, 0], crows[0:3, :]).then_inc(s["stored"], 16)
                pool.dma_start(d["conv_sample_o"][0].rearrange("b j n -> (b j) n"), crows[3:27, :]).then_inc(s["stored"], 16)
                pool.dma_start(d["sc_prompt_o"][0, 0], srows[0:2, :]).then_inc(s["stored"], 16)
                pool.dma_start(d["sc_sample_o"][0].rearrange("b j n -> (b j) n"), srows[2:18, :]).then_inc(s["stored"], 16)
                pool.wait_ge(s["stored"], 64)


def ssd_steps(e, z):
    nc, d = e.nc, e.d
    with ExitStack() as ctx:
        sb = lambda n, sh: ctx.enter_context(nc.sbuf_tensor(n, sh, F32))
        s = ctx.enter_context(stage(nc, "steps", ["rows_in", "step", "minus_abs", "exped", "a_head", "a_ready",
                                                  "sums_ready", "small_ready", "sums_out", "decays"]))
        head = sb("head_rows", [128, 3, SSD_HEADS])
        dcol = sb("d_skip_col", [SSD_HEADS, 1])
        x, u, q, w, r = [sb(f"softplus_{n}", [128, 3, SSD_HEADS]) for n in "xuqwr"]
        with nc.Block() as block:
            @block.sync
            def _(sp):
                sp.dma_start(z.selhp[0:32, :], d["c_selhp"]).then_inc(s["rows_in"], 16)
                sp.dma_start(head[:, 0, :], d["ev_dt_bias"][0:1, :].partition_broadcast(128)).then_inc(s["rows_in"], 16)
                sp.dma_start(head[:, 1, :], d["ev_a_log"][0:1, :].partition_broadcast(128)).then_inc(s["rows_in"], 16)
                sp.dma_start(dcol[:], d["ev_d_skip"].rearrange("a h -> h a")).then_inc(s["rows_in"], 16)

            @block.vector
            def _(dve):
                v = nc.vector
                n = [0]

                def step(ins):
                    ins.then_inc(s["step"], 1)
                    n[0] += 1
                    dve.wait_ge(s["step"], n[0])

                bias = head[:, 0:1, :].to_broadcast([128, 3, SSD_HEADS])
                dve.wait_ge(s["rows_in"], 64)
                step(v.memset(x[:], 0.0))
                step(v.tensor_copy(x[:, 0:2, :], e.dt[:, 0:2, :]))
                step(v.tensor_copy(x[0:TSA, 2, :], e.dt[0:TSA, 2, :]))
                step(v.tensor_tensor(x[:], x[:], bias, ALU.add))
                v.scalar_tensor_tensor(u[:], x[:], -1.0, x[:], ALU.mult, ALU.min).then_inc(s["minus_abs"], 1)
                dve.wait_ge(s["exped"], 1)
                step(v.tensor_scalar(w[:], u[:], 2.0, None, ALU.add))
                step(v.reciprocal(w[:], w[:]))
                step(v.tensor_tensor(u[:], u[:], w[:], ALU.mult))
                step(v.tensor_tensor(w[:], u[:], u[:], ALU.mult))
                step(v.tensor_scalar(q[:], w[:], 1.0 / 17, None, ALU.mult))
                for k in (15, 13, 11, 9, 7, 5, 3):
                    step(v.scalar_tensor_tensor(q[:], q[:], 1.0 / k, w[:], ALU.add, ALU.mult))
                step(v.scalar_tensor_tensor(q[:], q[:], 1.0, u[:], ALU.add, ALU.mult))
                step(v.tensor_scalar(q[:], q[:], 2.0, None, ALU.mult))
                step(v.scalar_tensor_tensor(e.dt[:], x[:], 0.0, q[:], ALU.max, ALU.add))
                dve.wait_ge(s["a_head"], 1)
                step(v.memset(z.acs[:], 0.0))
                step(v.memset(r[:], 0.0))
                v.scalar_tensor_tensor(z.a[:], e.dt[:], -1.0, head[:, 1:2, :].to_broadcast([128, 3, SSD_HEADS]),
                                       ALU.mult, ALU.mult).then_inc(s["a_ready"], 1)
                dve.wait_ge(s["sums_ready"], 1)
                for k, dst in ((0, z.acs), (1, r)):
                    src = e.bank[0][:, 96 * k:96 * k + 96].rearrange("p (u h) -> p u h", u=3)
                    step(v.tensor_copy(dst[:, 0:2, :], src[:, 0:2, :]))
                    step(v.tensor_copy(dst[0:TSA, 2, :], src[0:TSA, 2, :]))
                step(v.tensor_copy(z.acst[:], e.bank[1][0:32, 0:T]))
                v.tensor_tensor(z.dec[:], r[:], z.acs[:], ALU.subtract).then_inc(s["sums_out"], 1)
                dve.wait_ge(s["small_ready"], 1)
                step(v.tensor_copy(z.dhp[:], e.bank[2][:, 0:KC]))
                step(v.tensor_copy(z.etot_hp[:], e.bank[2][:, 16:144].rearrange("p (t b) -> p t b", t=KC)))

            @block.scalar
            def _(act):
                a = nc.scalar.activation
                act.wait_ge(s["minus_abs"], 1)
                a(u[:], u[:], ACT.Exp).then_inc(s["exped"], 1)
                a(head[:, 1, :], head[:, 1, :], ACT.Exp).then_inc(s["a_head"], 1)
                act.wait_ge(s["sums_out"], 1)
                a(z.eacst[:], z.acst[:], ACT.Exp).then_inc(s["decays"], 1)
                a(z.dec[:], z.dec[:], ACT.Exp).then_inc(s["decays"], 1)
                a(z.etot[:], r[:], ACT.Exp).then_inc(s["decays"], 1)

            @block.tensor
            def _(pe):
                mm = nc.tensor.matmul
                pe.wait_ge(s["a_ready"], 1)
                for u_ in range(3):
                    n, tri, blk = unit_masks(e, u_)
                    h = slice(32 * u_, 32 * u_ + 32)
                    mm(e.bank[0][0:n, 32 * u_:32 * u_ + 32], tri, z.a[0:n, u_, :], start=True, stop=True)
                    mm(e.bank[0][0:n, 96 + 32 * u_:128 + 32 * u_], blk, z.a[0:n, u_, :], start=True, stop=True)
                    m = mm(e.bank[1][0:32, 128 * u_:128 * u_ + n], z.a[0:n, u_, :], tri, start=True, stop=True)
                m.then_inc(s["sums_ready"], 1)
                pe.wait_ge(s["decays"], 1)
                for t in range(KC):
                    sel = z.selhp[0:32, 128 * t:128 * t + 128]
                    mm(e.bank[2][:, t:t + 1], sel, dcol[:], start=True, stop=True)
                    m = mm(e.bank[2][:, 16 + 8 * t:24 + 8 * t], sel, z.eacst[:, TP + TS - 1:T:TS], start=True, stop=True)
                m.then_inc(s["small_ready"], 1)


def unit_masks(e, u):
    if u < 2:
        return 128, e.const[:, C_TRIP:C_TRIP + 128], e.ones
    return TSA, e.const[0:TSA, C_TRIS:C_TRIS + TSA], e.const[0:TSA, C_BLKS:C_BLKS + TSA]


def unit_tokens(e, z, u):
    nc = e.nc
    n = unit_masks(e, u)[0]
    tok = slice(128 * u, 128 * u + n)
    with ExitStack() as ctx:
        s = ctx.enter_context(stage(nc, f"tokens{u}", ["turned", "scaled", "decayed", "b_out"]))
        with nc.Block() as block:
            @block.tensor
            def _(pe):
                for f in range(5):
                    for a in range(4):
                        m = nc.tensor.transpose(e.bank[f][0:n, 128 * a:128 * a + 128], e.xbc[:, 4 * f + a, tok], e.ident)
                    m.then_inc(s["turned"], 1)

            @block.vector
            def _(dve):
                for f in range(4):
                    dve.wait_ge(s["turned"], f + 1)
                    v3 = lambda a: a[0:n, :].rearrange("p (h q) -> p h q", h=8)
                    nc.vector.tensor_tensor(v3(z.xr[:, 512 * f:512 * f + 512]), v3(e.bank[f][:, :]),
                                            e.dt[0:n, u, 8 * f:8 * f + 8].unsqueeze(2).to_broadcast([n, 8, HD]),
                                            ALU.mult).then_inc(s["scaled"], 1)
                for f in range(4):
                    v3 = lambda a: a[0:n, :].rearrange("p (h q) -> p h q", h=8)
                    dve.wait_ge(s["scaled"], f + 1)
                    nc.vector.tensor_tensor(v3(z.xd[:, 512 * f:512 * f + 512]), v3(z.xr[:, 512 * f:512 * f + 512]),
                                            z.dec[0:n, u, 8 * f:8 * f + 8].unsqueeze(2).to_broadcast([n, 8, HD]),
                                            ALU.mult).then_inc(s["decayed"], 1)

            @block.scalar
            def _(act):
                act.wait_ge(s["turned"], 5)
                nc.scalar.activation(z.btok[0:n, :], e.bank[4][0:n, :], ACT.Copy).then_inc(s["b_out"], 1)


def unit_groups(e, z, u):
    nc = e.nc
    n, tri, _ = unit_masks(e, u)
    tok = slice(128 * u, 128 * u + n)
    has_in = u > 0
    with ExitStack() as ctx:
        s = ctx.enter_context(stage(nc, f"unit{u}", ["cb_ready", "cb_out", "spread", "diff", "exped", "weights", "within",
                                                     "decay_ready", "decay_out", "incoming", "state_ready", "state_step",
                                                     "state_out", "joined", "y_out"]))
        cbm = ctx.enter_context(nc.sbuf_tensor(f"cbm{u}", [128, 128], F32))
        mx = [[ctx.enter_context(nc.sbuf_tensor(f"mx{u}_{g}_{q}", [128, 4, 128], F32)) for q in range(2)] for g in range(2)]
        es = ctx.enter_context(nc.sbuf_tensor(f"es{u}", [128, 4, 128], F32))
        b3 = lambda i: e.bank[i][:, 0:4 * n].rearrange("p (a l) -> p a l", a=4)
        with nc.Block() as block:
            @block.tensor
            def _(pe):
                mm = nc.tensor.matmul

                def outputs(g):
                    for q in range(2):
                        pe.wait_ge(s["weights"], 2 * g + q + 1)
                        if q == 0 and g:
                            pe.wait_ge(s["joined" if has_in else "y_out"], g if has_in else 4 * g)
                        for hh in range(4):
                            h = 8 * g + 4 * q + hh
                            p0, t = 64 * (h % 2), 2 * q + hh // 2
                            m = mm(e.bank[3][p0:p0 + 64, t * n:t * n + n], z.xr[0:n, HD * h:HD * h + HD],
                                   mx[g % 2][q][0:n, hh, 0:n], start=True, stop=True)
                    m.then_inc(s["within"], 1)

                for g in range(5):
                    if g < 4:
                        if g:
                            pe.wait_ge(s["cb_out"], g)
                        mm(e.bank[0][0:n, 0:n], e.xbc[:, 16 + g, tok], e.xbc[:, 20 + g, tok],
                           start=True, stop=True).then_inc(s["cb_ready"], 1)
                        for q in range(2):
                            if g:
                                pe.wait_ge(s["diff"], 2 * g - 1 + q)
                            for hh in range(4):
                                h = 8 * g + 4 * q + hh
                                m = mm(e.bank[1 + q][0:n, hh * n:hh * n + n], e.ident[0:32, h:h + 1].to_broadcast([32, n]),
                                       z.acst[:, tok], start=True, stop=True)
                            m.then_inc(s["spread"], 1)
                    if g:
                        outputs(g - 1)
                    if g < 4:
                        if has_in:
                            if g:
                                pe.wait_ge(s["decay_out"], g)
                            for a in range(4):
                                m = mm(b3(5)[:, a, :], z.selhp[0:32, 128 * (4 * g + a):128 * (4 * g + a) + 128],
                                       z.eacst[:, tok], start=True, stop=True)
                            m.then_inc(s["decay_ready"], 1)
                        if u == 1:
                            if g:
                                pe.wait_ge(s["joined"], g)
                            for a in range(4):
                                t = 4 * g + a
                                m = mm(b3(4)[:, a, :], z.st[:, 128 * t:128 * t + 128], e.xbc[:, 20 + g, tok], start=True, stop=True)
                            m.then_inc(s["incoming"], 1)
                        if u < 2:
                            if g:
                                pe.wait_ge(s["state_out"], g)
                            mm(e.bank[6][:, 0:512], z.btok[0:n, 128 * g:128 * g + 128], z.xd[0:n, 512 * g:512 * g + 512],
                               start=True, stop=True).then_inc(s["state_ready"], 1)

            @block.scalar
            def _(act):
                for g in range(4):
                    for q in range(2):
                        act.wait_ge(s["diff"], 2 * g + q + 1)
                        m = mx[g % 2][q][0:n, :, 0:n]
                        nc.scalar.activation(m, m, ACT.Exp).then_inc(s["exped"], 1)
                    if has_in:
                        act.wait_ge(s["decay_ready"], g + 1)
                        if g:
                            act.wait_ge(s["y_out"], 4 * g)
                        nc.scalar.activation(es[:, :, 0:n], b3(5), ACT.Copy).then_inc(s["decay_out"], 1)

            @block.vector
            def _(dve):
                v = nc.vector

                def join(g):
                    dve.wait_ge(s["within"], g + 1)
                    y, src = es[:, :, 0:n], b3(3)
                    if has_in:
                        dve.wait_ge(s["decay_out"], g + 1)
                        if u == 1:
                            dve.wait_ge(s["incoming"], g + 1)
                            off = b3(4)
                        else:
                            off = z.yoff[:, 4 * g:4 * g + 4, :]
                        v.tensor_tensor(y, y, off, ALU.mult).then_inc(s["state_step"], 1)
                        dve.wait_ge(s["state_step"], joins(g))
                        v.tensor_tensor(y, y, b3(3), ALU.add).then_inc(s["joined"], 1)
                        dve.wait_ge(s["joined"], g + 1)
                        src = y
                    for a in range(4):
                        t = 4 * g + a
                        x = e.xbc[:, t, tok]
                        v.scalar_tensor_tensor(x, x, z.dhp[:, t:t + 1], src[:, a, :], ALU.mult, ALU.add).then_inc(s["y_out"], 1)
                    if u < 2:
                        dve.wait_ge(s["state_ready"], g + 1)
                        st = z.st[:, 512 * g:512 * g + 512]
                        if u == 0:
                            v.tensor_copy(st, e.bank[6][:, 0:512]).then_inc(s["state_out"], 1)
                        else:
                            st3 = st.rearrange("p (h q) -> p h q", h=8)
                            v.tensor_tensor(st3, st3, z.etot[:, 1, 8 * g:8 * g + 8].unsqueeze(2).to_broadcast([128, 8, HD]),
                                            ALU.mult).then_inc(s["state_step"], 1)
                            dve.wait_ge(s["state_step"], joins(g) + 1)
                            v.tensor_tensor(st, st, e.bank[6][:, 0:512], ALU.add).then_inc(s["state_out"], 1)

                joins = lambda g: (2 * g if u == 1 else g) + 1
                for g in range(5):
                    if g < 4:
                        dve.wait_ge(s["cb_ready"], g + 1)
                        if g:
                            dve.wait_ge(s["weights"], 2 * g)
                        v.tensor_tensor(cbm[0:n, 0:n], e.bank[0][0:n, 0:n], tri, ALU.mult).then_inc(s["cb_out"], 1)
                        for q in range(2):
                            dve.wait_ge(s["spread"], 2 * g + q + 1)
                            if g >= 2:
                                dve.wait_ge(s["within"], g - 1)
                            for hh in range(4):
                                h = 8 * g + 4 * q + hh
                                m = v.tensor_scalar(mx[g % 2][q][0:n, hh, 0:n], e.bank[1 + q][0:n, hh * n:hh * n + n],
                                                    z.acs[0:n, u, h:h + 1], 0.0, ALU.subtract, ALU.min)
                            m.then_inc(s["diff"], 1)
                        dve.wait_ge(s["cb_out"], g + 1)
                        for q in range(2):
                            dve.wait_ge(s["exped"], 2 * g + q + 1)
                            m = mx[g % 2][q][0:n, :, 0:n]
                            v.tensor_tensor(m, m, cbm[0:n, 0:n].unsqueeze(1).to_broadcast([n, 4, n]), ALU.mult).then_inc(s["weights"], 1)
                    if g:
                        join(g - 1)


def sample_states(e, z):
    nc, d = e.nc, e.d
    with ExitStack() as ctx:
        s = ctx.enter_context(stage(nc, "sstate", ["in0", "in1", "turned", "turn_out_v", "turn_out_s", "yoff_ready", "yoff_out",
                                                   "b_masked", "new_ready", "new_out", "stored0", "stored1"]))
        sb = lambda n, sh: ctx.enter_context(nc.sbuf_tensor(n, sh, F32))
        s0 = [sb(f"s0_{i}", [128, KC, 128]) for i in range(2)]
        s0t = z.st.rearrange("p (t n) -> p t n", t=KC)
        bmk = sb("b_masked", [TSA, 512])
        src = d["state_ssm"][0].rearrange("b h p n -> b (h p) n").rearrange("b (t q) n -> q b t n", q=128)
        dst = d["ssm_sample_o"][0].rearrange("b h p n -> b (h p) n").rearrange("b (t q) n -> q b t n", q=128)
        with nc.Block() as block:
            @block.sync
            def _(sp):
                for b in range(NB):
                    if b >= 2:
                        sp.wait_ge(s[f"stored{b % 2}"], 16 * (b // 2))
                    sp.dma_start(s0[b % 2][:], src[:, b]).then_inc(s[f"in{b % 2}"], 16)

            @block.gpsimd
            def _(pool):
                for b in range(NB):
                    pool.wait_ge(s["new_out"], KC * (b + 1))
                    pool.dma_start(dst[:, b], s0[b % 2][:]).then_inc(s[f"stored{b % 2}"], 16)
                for i in range(2):
                    pool.wait_ge(s[f"stored{i}"], 16 * (NB // 2))

            @block.tensor
            def _(pe):
                mm = nc.tensor.matmul
                for b in range(NB):
                    st = s0[b % 2]
                    pe.wait_ge(s[f"in{b % 2}"], 16 * (b // 2 + 1))
                    for f in range(4):
                        if b:
                            pe.wait_ge(s["turn_out_s" if f % 2 else "turn_out_v"], 2 * (b - 1) + f // 2 + 1)
                        for a in range(4):
                            m = nc.tensor.transpose(e.bank[f][:, 128 * a:128 * a + 128], st[:, 4 * f + a, :], e.ident)
                        m.then_inc(s["turned"], 1)
                    pe.wait_ge(s["turn_out_v"], 2 * (b + 1))
                    pe.wait_ge(s["turn_out_s"], 2 * (b + 1))
                    if b:
                        pe.wait_ge(s["yoff_out"], b)
                    for t in range(KC):
                        m = mm(e.bank[4][:, 8 * t:8 * t + 8], s0t[:, t, :], e.xbc[:, 20 + t // 4, TP + TS * b:TP + TS * b + TS],
                               start=True, stop=True)
                    m.then_inc(s["yoff_ready"], 1)
                    pe.wait_ge(s["b_masked"], b + 1)
                    for g in range(GROUPS):
                        bank = 5 + g % 3
                        k = 4 * b + g
                        if b or g == 3:
                            prev = 4 * b if g == 3 else 4 * (b - 1) + (3 if g == 0 else g)
                            pe.wait_ge(s["new_out"], 4 * (prev + 1))
                        for a in range(4):
                            t = 4 * g + a
                            m = mm(e.bank[bank][:, 128 * a:128 * a + 128], z.xd[0:TSA, 128 * t:128 * t + 128],
                                   bmk[:, 128 * g:128 * g + 128], start=True, stop=True)
                        m.then_inc(s["new_ready"], 1)

            @block.scalar
            def _(act):
                for b in range(NB):
                    for f in (1, 3):
                        act.wait_ge(s["turned"], 4 * b + f + 1)
                        if b:
                            act.wait_ge(s["yoff_ready"], b)
                        nc.scalar.activation(s0t[:, 4 * f:4 * f + 4, :], e.bank[f][:].rearrange("p (a l) -> p a l", a=4), ACT.Copy).then_inc(s["turn_out_s"], 1)
                    act.wait_ge(s["yoff_ready"], b + 1)
                    nc.scalar.activation(z.yoff[:, :, TS * b:TS * b + TS], e.bank[4][:, 0:128].rearrange("p (t l) -> p t l", t=KC),
                                         ACT.Copy).then_inc(s["yoff_out"], 1)

            @block.vector
            def _(dve):
                v = nc.vector
                for b in range(NB):
                    if b:
                        dve.wait_ge(s["new_ready"], 4 * b)
                    v.tensor_scalar(bmk[:], z.btok[0:TSA, :], e.const[0:TSA, C_BM + b:C_BM + b + 1], None, ALU.mult).then_inc(s["b_masked"], 1)
                    for f in (0, 2):
                        dve.wait_ge(s["turned"], 4 * b + f + 1)
                        if b:
                            dve.wait_ge(s["yoff_ready"], b)
                        v.tensor_copy(s0t[:, 4 * f:4 * f + 4, :], e.bank[f][:].rearrange("p (a l) -> p a l", a=4)).then_inc(s["turn_out_v"], 1)
                    for g in range(GROUPS):
                        dve.wait_ge(s["new_ready"], 4 * b + g + 1)
                        for a in range(4):
                            t = 4 * g + a
                            x = s0[b % 2][:, t, :]
                            v.scalar_tensor_tensor(x, x, z.etot_hp[:, t, b:b + 1], e.bank[5 + g % 3][:, 128 * a:128 * a + 128],
                                                   ALU.mult, ALU.add).then_inc(s["new_out"], 1)


def prompt_state_out(e, z):
    nc, d = e.nc, e.d
    with ExitStack() as ctx:
        s = ctx.enter_context(stage(nc, "pstate", ["turned", "evac_v", "evac_s", "stored"]))
        out = ctx.enter_context(nc.sbuf_tensor("pstate_rows", [128, KC, 128], F32))
        fills = [([(128 * a, z.st[:, 128 * (4 * f + a):128 * (4 * f + a) + 128], 128, 128) for a in range(4)], 128, 512,
                  out[:, 4 * f:4 * f + 4, :]) for f in range(4)]
        tensor, copies = transposes(e, None, s, fills)
        with nc.Block() as block:
            block.tensor(tensor)
            block.vector(lambda eng: copies(eng, 0))
            block.scalar(lambda eng: copies(eng, 1))

            @block.gpsimd
            def _(pool):
                pool.wait_ge(s["evac_v"], 2)
                pool.wait_ge(s["evac_s"], 2)
                pool.dma_start(d["ssm_prompt_o"][0, 0].rearrange("h p n -> (h p) n").rearrange("(t q) n -> q t n", q=128),
                               out[:]).then_inc(s["stored"], 16)
                pool.wait_ge(s["stored"], 16)


def gated_group_norm(e):
    nc = e.nc
    with ExitStack() as ctx:
        s = ctx.enter_context(stage(nc, "gnorm", ["gated", "squared", "summed", "var", "std", "rstd", "normed"]))
        sq = ctx.enter_context(nc.sbuf_tensor("group_sq", [128, 4, T], F32))
        r = ctx.enter_context(nc.sbuf_tensor("group_r", [128, GROUPS, T], F32))
        with nc.Block() as block:
            @block.vector
            def _(dve):
                v = nc.vector
                for c in range(KC):
                    v.tensor_tensor(e.xbc[:, c, :], e.xbc[:, c, :], e.zs[:, c, :], ALU.mult).then_inc(s["gated"], 1)
                for g in range(GROUPS):
                    dve.wait_ge(s["summed"], g + 1)
                    v.tensor_scalar(r[:, g, :], e.bank[g][:, 0:T], 1.0 / 512, EPS, ALU.mult, ALU.add).then_inc(s["var"], 1)
                for g in range(GROUPS):
                    dve.wait_ge(s["std"], g + 1)
                    v.reciprocal(r[:, g, :], r[:, g, :]).then_inc(s["rstd"], 1)
                for c in range(KC):
                    dve.wait_ge(s["rstd"], c // 4 + 1)
                    y = e.xbc[:, c, :]
                    v.scalar_tensor_tensor(y, y, e.va[:, VA_EV + c:VA_EV + c + 1], r[:, c // 4, :], ALU.mult, ALU.mult).then_inc(s["normed"], 1)

            @block.scalar
            def _(act):
                for c in range(KC):
                    act.wait_ge(s["gated"], c + 1)
                    if c >= 4:
                        act.wait_ge(s["summed"], c // 4)
                    nc.scalar.activation(sq[:, c % 4, :], e.xbc[:, c, :], ACT.Square).then_inc(s["squared"], 1)
                for g in range(GROUPS):
                    act.wait_ge(s["var"], g + 1)
                    nc.scalar.activation(r[:, g, :], r[:, g, :], ACT.Sqrt).then_inc(s["std"], 1)

            @block.tensor
            def _(pe):
                for c in range(KC):
                    pe.wait_ge(s["squared"], c + 1)
                    m = nc.tensor.matmul(e.bank[c // 4][:, 0:T], e.ones, sq[:, c % 4, :], start=c % 4 == 0, stop=c % 4 == 3)
                    if c % 4 == 3:
                        m.then_inc(s["summed"], 1)


class Scan:
    pass


def ssd(e):
    with ExitStack() as ctx:
        sb = lambda n, sh: ctx.enter_context(e.nc.sbuf_tensor(n, sh, F32))
        z = Scan()
        z.a, z.acs, z.dec, z.etot = [sb(f"scan_{n}", [128, 3, SSD_HEADS]) for n in ("a", "acs", "dec", "etot")]
        z.acst, z.eacst = sb("scan_acst", [32, T]), sb("scan_eacst", [32, T])
        z.dhp, z.etot_hp = sb("scan_dhp", [128, KC]), sb("scan_etot_hp", [128, KC, NB])
        flat = e.h[:].rearrange("p c t -> p (c t)")
        z.xr, z.st = flat[:, 0:D], flat[:, D:2 * D]
        z.selhp = sb("selhp", [32, 2048])
        z.xd, z.btok = sb("scan_xd", [128, D]), sb("scan_btok", [128, 512])
        ssd_steps(e, z)
        for u in range(2):
            unit_tokens(e, z, u)
            unit_groups(e, z, u)
        prompt_state_out(e, z)
        unit_tokens(e, z, 2)
        z.yoff = flat[:, 2 * D:2 * D + KC * TSA].rearrange("p (t l) -> p t l", t=KC)
        sample_states(e, z)
        unit_groups(e, z, 2)
    gated_group_norm(e)


def add_projection(e, label, p, rhs, nxt):
    nc = e.nc
    with ExitStack() as ctx:
        s = ctx.enter_context(stage(nc, label, ["unused"]))
        with nc.Block() as block:
            @block.sync
            def _(sp):
                p.later_loads(sp)
                if nxt:
                    nxt.first_loads(sp)

            @block.tensor
            def _(pe):
                p.matmuls(pe, rhs)

            @block.vector
            def _(dve):
                p.take_over(dve)

                def body(i):
                    for j in range(p.body_tiles):
                        p.wait_tile(dve, i, j)
                        x = e.xt[:, ds(p.body_tiles * i + j, 1), :]
                        nc.vector.tensor_tensor(x, x, e.bank[j % NSLOT][:, 0:T].unsqueeze(1), ALU.add).then_inc(e.bank_free, 1)
                p.loop(dve, body)


def prompt_attention(e, label, heads, qt, kt, v, gated, bias=None):
    nc = e.nc
    with ExitStack() as ctx:
        s = ctx.enter_context(stage(nc, label, ["scores", "biased", "negmax", "exped", "recips", "probs", "turned",
                                                "turn_out", "out_ready", "out"]))
        sb = lambda n, sh: [ctx.enter_context(nc.sbuf_tensor(f"{label}_{n}{i}", sh, F32)) for i in range(2)]
        p, pt = sb("p", [128, 2, TP]), sb("pt", [128, 2, TP])
        nm, den, rec = sb("negmax", [128, 2]), sb("den", [128, 2]), sb("rec", [128, 2])
        sc = lambda u: e.bank[u % 2][:].rearrange("p (r k) -> p r k", r=2)
        with nc.Block() as block:
            @block.tensor
            def _(pe):
                mm = nc.tensor.matmul
                for u in range(heads + 2):
                    if u < heads:
                        if u >= 2:
                            if bias:
                                pe.wait_ge(s["biased"], u - 1)
                            else:
                                pe.wait_ge(s["exped"], 2 * (u - 1))
                        for r in range(2):
                            m = mm(sc(u)[:, r, :], qt(u)[:, 128 * r:128 * r + 128], kt(u), start=True, stop=True)
                        m.then_inc(s["scores"], 1)
                    if 1 <= u <= heads:
                        w = u - 1
                        pe.wait_ge(s["probs"], 2 * (w + 1))
                        if w >= 2:
                            pe.wait_ge(s["turn_out"], w - 1)
                        for k in range(2):
                            for r in range(2):
                                m = nc.tensor.transpose(e.bank[2 + w % 2][:, 128 * (2 * k + r):128 * (2 * k + r) + 128],
                                                        p[w % 2][:, r, 128 * k:128 * k + 128], e.ident)
                        m.then_inc(s["turned"], 1)
                    if u >= 2:
                        w = u - 2
                        pe.wait_ge(s["turn_out"], w + 1)
                        if w >= 2:
                            pe.wait_ge(s["out"], w - 1)
                        for k in range(2):
                            m = mm(e.bank[4 + w % 2][:, 0:TP], v(w, k), pt[w % 2][:, k, :], start=k == 0, stop=k == 1)
                        m.then_inc(s["out_ready"], 1)

            @block.scalar
            def _(act):
                for u in range(heads + 1):
                    if u < heads:
                        act.wait_ge(s["negmax"], u + 1)
                        if u >= 2:
                            act.wait_ge(s["recips"], u - 1)
                            act.wait_ge(s["turned"], u - 1)
                        for r in range(2):
                            src = p[u % 2][:, r, :] if bias else sc(u)[:, r, :]
                            nc.scalar.activation(p[u % 2][:, r, :], src, ACT.Exp, bias=nm[u % 2][:, r:r + 1],
                                                 accum_out=den[u % 2][:, r:r + 1]).then_inc(s["exped"], 1)
                    if u >= 1:
                        w = u - 1
                        act.wait_ge(s["turned"], w + 1)
                        if w >= 2:
                            act.wait_ge(s["out_ready"], w - 1)
                        nc.scalar.activation(pt[w % 2][:].rearrange("p k q -> p (k q)"), e.bank[2 + w % 2][:], ACT.Copy).then_inc(s["turn_out"], 1)

            @block.vector
            def _(dve):
                v_ = nc.vector
                for u in range(heads + 2):
                    if u < heads:
                        dve.wait_ge(s["scores"], u + 1)
                        src = sc(u)
                        if bias:
                            table, slope = bias(u)
                            if u >= 2:
                                dve.wait_ge(s["turned"], u - 1)
                            v_.scalar_tensor_tensor(p[u % 2][:], table, slope, sc(u), ALU.mult, ALU.add).then_inc(s["biased"], 1)
                            dve.wait_ge(s["biased"], u + 1)
                            src = p[u % 2][:]
                        if u >= 2:
                            dve.wait_ge(s["exped"], 2 * (u - 1))
                        v_.tensor_reduce(nm[u % 2][:], src, AX.X, ALU.max, negate=True).then_inc(s["negmax"], 1)
                    if 1 <= u <= heads:
                        w = u - 1
                        dve.wait_ge(s["exped"], 2 * (w + 1))
                        v_.reciprocal(rec[w % 2][:], den[w % 2][:]).then_inc(s["recips"], 1)
                        dve.wait_ge(s["recips"], w + 1)
                        for r in range(2):
                            x = p[w % 2][:, r, :]
                            v_.tensor_scalar(x, x, rec[w % 2][:, r:r + 1], None, ALU.mult).then_inc(s["probs"], 1)
                    if u >= 2:
                        w = u - 2
                        dve.wait_ge(s["out_ready"], w + 1)
                        v_.tensor_tensor(gated(w), gated(w), e.bank[4 + w % 2][:, 0:TP], ALU.mult).then_inc(s["out"], 1)


def cross_sample(e, layer, qt, gt):
    nc, d = e.nc, e.d
    L = f"xs{layer}"
    with ExitStack() as ctx:
        s = ctx.enter_context(stage(nc, L, ["mask_in", "k_in0", "k_in1", "v_in0", "v_in1", "masked", "turned", "kt_v", "kt_s",
                                            "scores", "negmax", "exped", "recips", "probs", "p_turned", "p_out", "used",
                                            "out_ready", "out"]))
        sb = lambda n, sh: ctx.enter_context(nc.sbuf_tensor(f"{L}_{n}", sh, F32))
        mask = sb("mask", [128, NB, TSA])
        kr = [sb(f"krows{i}", [128, 2, 512]) for i in range(2)]
        vr = [sb(f"vrows{i}", [128, 2, 512]) for i in range(2)]
        kt = [sb(f"kt{i}", [128, CAH, NM]) for i in range(2)]
        qm = [sb(f"qm{i}", [128, CAH, TSA]) for i in range(2)]
        p, pt = sb("p", [128, 2, NM]), sb("pt", [128, 2, 2, 128])
        nm, den, rec = sb("negmax", [128, 2]), sb("den", [128, 2]), sb("rec", [128, 2])
        rows = lambda a: a.rearrange("(t p) h n -> p t (h n)", p=128)
        with nc.Block() as block:
            @block.sync
            def _(sp):
                sp.dma_start(mask[:], d["c_qmask"].rearrange("p (b t) -> p b t", b=NB)).then_inc(s["mask_in"], 16)
                for b in range(NB):
                    if b >= 2:
                        sp.wait_ge(s["turned"], 2 * (b - 1))
                    sp.dma_start(kr[b % 2][:], rows(d["cache_mem_k"][layer, b])).then_inc(s[f"k_in{b % 2}"], 16)
                for b in range(NB):
                    if b >= 2:
                        sp.wait_ge(s["used"], b - 1)
                    sp.dma_start(vr[b % 2][:], rows(d["cache_mem_v"][layer, b])).then_inc(s[f"v_in{b % 2}"], 16)

            @block.tensor
            def _(pe):
                mm = nc.tensor.matmul
                for b in range(NB + 1):
                    if b < NB:
                        pe.wait_ge(s[f"k_in{b % 2}"], 16 * (b // 2 + 1))
                        for t in range(2):
                            if b:
                                pe.wait_ge(s["kt_s" if t else "kt_v"], b)
                            for h in range(CAH):
                                m = nc.tensor.transpose(e.bank[t][:, 128 * h:128 * h + 128], kr[b % 2][:, t, 128 * h:128 * h + 128], e.ident)
                            m.then_inc(s["turned"], 1)
                    if b:
                        c = b - 1
                        pe.wait_ge(s["kt_v"], b)
                        pe.wait_ge(s["kt_s"], b)
                        pe.wait_ge(s["masked"], b)
                        for h in range(CAH):
                            p0 = 64 * (h % 2)
                            m = mm(e.bank[2 + h // 2][p0:p0 + 64, 0:NM], qm[c % 2][:, h, :], kt[c % 2][:, h, :],
                                   start=c == 0, stop=c == NB - 1)
                        m.then_inc(s["scores"], 1)
                pe.wait_ge(s["probs"], 2)
                for t in range(2):
                    for r in range(2):
                        m = nc.tensor.transpose(e.bank[4][:, 128 * (2 * t + r):128 * (2 * t + r) + 128], p[:, r, 128 * t:128 * t + 128], e.ident)
                m.then_inc(s["p_turned"], 1)
                pe.wait_ge(s["p_out"], 1)
                for b in range(NB):
                    pe.wait_ge(s[f"v_in{b % 2}"], 16 * (b // 2 + 1))
                    for h in range(CAH):
                        c0 = 64 * (h % 2) + TS * b
                        for t in range(2):
                            m = mm(e.bank[5][:, TSA * h + TS * b:TSA * h + TS * b + TS], vr[b % 2][:, t, 128 * h:128 * h + 128],
                                   pt[:, t, h // 2, c0:c0 + TS], start=t == 0, stop=t == 1)
                    m.then_inc(s["used"], 1)

            @block.scalar
            def _(act):
                for b in range(NB):
                    act.wait_ge(s["turned"], 2 * b + 2)
                    if b >= 2:
                        act.wait_ge(s["scores"], b - 1)
                    nc.scalar.activation(kt[b % 2][:, :, 128:256], e.bank[1][:].rearrange("p (h m) -> p h m", h=CAH), ACT.Copy).then_inc(s["kt_s"], 1)
                act.wait_ge(s["negmax"], 2)
                for r in range(2):
                    nc.scalar.activation(p[:, r, :], e.bank[2 + r][:, 0:NM], ACT.Exp, bias=nm[:, r:r + 1],
                                         accum_out=den[:, r:r + 1]).then_inc(s["exped"], 1)
                act.wait_ge(s["p_turned"], 1)
                nc.scalar.activation(pt[:].rearrange("p t r q -> p (t r q)"), e.bank[4][:], ACT.Copy).then_inc(s["p_out"], 1)

            @block.vector
            def _(dve):
                v = nc.vector
                dve.wait_ge(s["mask_in"], 16)
                for b in range(NB):
                    if b >= 2:
                        dve.wait_ge(s["scores"], b - 1)
                    v.tensor_tensor(qm[b % 2][:], qt[:, :, TP:T], mask[:, b:b + 1, :].to_broadcast([128, CAH, TSA]), ALU.mult).then_inc(s["masked"], 1)
                    dve.wait_ge(s["turned"], 2 * b + 1)
                    v.tensor_copy(kt[b % 2][:, :, 0:128], e.bank[0][:].rearrange("p (h m) -> p h m", h=CAH)).then_inc(s["kt_v"], 1)
                dve.wait_ge(s["scores"], NB)
                for r in range(2):
                    v.tensor_reduce(nm[:, r:r + 1], e.bank[2 + r][:, 0:NM], AX.X, ALU.max, negate=True).then_inc(s["negmax"], 1)
                dve.wait_ge(s["exped"], 2)
                v.reciprocal(rec[:], den[:]).then_inc(s["recips"], 1)
                dve.wait_ge(s["recips"], 1)
                for r in range(2):
                    v.tensor_scalar(p[:, r, :], p[:, r, :], rec[:, r:r + 1], None, ALU.mult).then_inc(s["probs"], 1)
                dve.wait_ge(s["used"], NB)
                v.tensor_tensor(gt[:, :, TP:T], gt[:, :, TP:T], e.bank[5][:, 0:CAH * TSA].rearrange("p (h q) -> p h q", h=CAH),
                                ALU.mult).then_inc(s["out"], 1)


def cross_attention(e, layer, p_q, p_out, nxt):
    nc = e.nc
    rmsnorm(e, f"norm_cross{layer}", e.xt, T, VA_CROSS + KC * layer, e.h)
    with ExitStack() as ctx:
        sb = lambda n, sh: ctx.enter_context(nc.sbuf_tensor(n, sh, F32))
        qt, gt = sb(f"xq{layer}", [128, CAH, T]), sb(f"xg{layer}", [128, CAH, T])
        with nc.Block() as block:
            @block.sync
            def _(sp):
                p_q.later_loads(sp)
                p_out.first_loads(sp)

            @block.tensor
            def _(pe):
                p_q.matmuls(pe, lambda k: e.h[:, k, :])

            @block.scalar
            def _(act):
                p_q.take_over(act)
                for i in range(2):
                    for j in range(4):
                        p_q.wait_tile(act, i, j)
                        if i == 0:
                            nc.scalar.activation(qt[:, j, :], e.bank[j][:, 0:T], ACT.Copy, scale=QSCALE).then_inc(e.bank_free, 1)
                        else:
                            nc.scalar.activation(gt[:, j, :], e.bank[j][:, 0:T], ACT.Silu).then_inc(e.bank_free, 1)
        prompt_attention(e, f"xp{layer}", CAH, lambda h: qt[:, h, 0:TP], lambda h: e.km[layer][:, h, :],
                         lambda h, m: e.vm[layer][:, m, 128 * h:128 * h + 128], lambda h: gt[:, h, 0:TP])
        cross_sample(e, layer, qt, gt)
        add_projection(e, f"cross_out{layer}", p_out, lambda k: gt[:, k, :], nxt)


def moba_sample(e, qt, kt_new, v_new, gt):
    nc, d = e.nc, e.d
    names = ["tables_in", "pages_in", "q_ready", "k_turned", "kt_v", "kt_s", "scores", "own_scores", "step", "negmax",
             "exped", "recips", "dropped", "probs", "p_turned", "pt_v", "pt_s", "v_used", "o_ready", "o_out"]
    names += [f"k_in{i}" for i in range(4)] + [f"v_in{i}" for i in range(4)]
    with ExitStack() as ctx:
        s = ctx.enter_context(stage(nc, "ms", names))
        sb = lambda n, sh, dt=F32: ctx.enter_context(nc.sbuf_tensor(f"ms_{n}", sh, dt))
        pages = sb("pages", [1, NB * NPG], I32)
        past, own = sb("past", [128, PAST]), sb("own", [128, NB, TSA])
        krows, vrows = sb("krows", [128, 4, 512]), sb("vrows", [128, 4, 512])
        kt = sb("kt", [128, KVH, PAST])
        qb = sb("q", [128, AH, TS])
        gate, rank, drop = sb("gate", [128, NBLK]), sb("rank", [128, NBLK]), sb("drop", [128, NBLK])
        above, tied = sb("above", [128, NBLK, NBLK]), sb("tied", [128, NBLK, NBLK])
        nm, den, rec = sb("negmax", [128, 1]), sb("den", [128, 1]), sb("rec", [128, 1])
        flat = e.h[:].rearrange("p c t -> p (c t)")
        NP = PAST + TSA
        p, pt = flat[:, 0:NP], flat[:, NP:NP + (NPG + 1) * 128]
        STEPS = 17
        with nc.Block() as block:
            @block.sync
            def _(sp):
                sp.dma_start(pages[:], d["page_table"].rearrange("b n -> (b n)").unsqueeze(0)).then_inc(s["pages_in"], 16)
                sp.dma_start(past[:], d["c_past"]).then_inc(s["tables_in"], 16)
                sp.dma_start(own[:], d["c_own"].rearrange("p (b t) -> p b t", b=NB)).then_inc(s["tables_in"], 16)
                sp.wait_ge(s["pages_in"], 16)
                src = d["cache_k"][0].rearrange("n t h c -> n t (h c)")
                with sp.Fori(0, NB) as b:
                    for g in range(NPG):
                        page = sp.value_load(pages[0:1, ds(b * NPG + g, 1)], min_val=0, max_val=src.shape[0] - 1)
                        sp.wait_ge(s["k_turned"], b * NPG + (g + 1))
                        sp.dma_start(krows[:, g % 4:g % 4 + 1, :], src[ds(page, 1)].rearrange("n t c -> t n c")).then_inc(s[f"k_in{g % 4}"], 16)

            @block.gpsimd
            def _(pool):
                pool.wait_ge(s["pages_in"], 16)
                src = d["cache_v"][0].rearrange("n t h c -> n t (h c)")
                with pool.Fori(0, NB) as b:
                    for g in range(NPG):
                        page = pool.value_load(pages[0:1, ds(b * NPG + g, 1)], min_val=0, max_val=src.shape[0] - 1)
                        pool.wait_ge(s["v_used"], b * NPG + (g + 1))
                        pool.dma_start(vrows[:, g % 4:g % 4 + 1, :], src[ds(page, 1)].rearrange("n t c -> t n c")).then_inc(s[f"v_in{g % 4}"], 16)

            @block.tensor
            def _(pe):
                mm = nc.tensor.matmul
                pe.sem_inc(s["k_turned"], 4)
                pe.sem_inc(s["v_used"], 4)
                pe.sem_inc(s["kt_v"], 1)
                pe.sem_inc(s["kt_s"], 1)
                pe.sem_inc(s["pt_v"], 1)
                pe.sem_inc(s["pt_s"], 1)
                with pe.Fori(0, NB) as b:
                    pe.wait_ge(s["q_ready"], b + 1)
                    for g in range(NPG):
                        pe.wait_ge(s[f"k_in{g % 4}"], b * 64 + 16 * (g // 4 + 1))
                        pe.wait_ge(s["kt_s" if g % 2 else "kt_v"], b * 8 + (g // 2 + 1))
                        for h in range(KVH):
                            m = nc.tensor.transpose(e.bank[g % 2][:, 128 * h:128 * h + 128], krows[:, g % 4, 128 * h:128 * h + 128], e.ident)
                        m.then_inc(s["k_turned"], 1)
                        if g % 4 == 3:
                            q = g // 4
                            pe.wait_ge(s["kt_v"], b * 8 + (2 * q + 3))
                            pe.wait_ge(s["kt_s"], b * 8 + (2 * q + 3))
                            if q == 0:
                                pe.wait_ge(s["pt_v"], b * 3 + 1)
                                pe.wait_ge(s["pt_s"], b * 2 + 1)
                            for h in range(KVH):
                                m = mm(e.bank[4 + q][32 * h:32 * h + 32, :], qb[:, 4 * h:4 * h + 4, :].rearrange("p g t -> p (g t)"),
                                       kt[:, h, 512 * q:512 * q + 512], start=True, stop=True)
                            m.then_inc(s["scores"], 1)
                    for h in range(KVH):
                        m = mm(e.bank[2][32 * h:32 * h + 32, 0:TSA], qb[:, 4 * h:4 * h + 4, :].rearrange("p g t -> p (g t)"),
                               kt_new[:, h, TP:T], start=True, stop=True)
                    m.then_inc(s["own_scores"], 1)
                    pe.wait_ge(s["probs"], b + 1)
                    for f in range(4):
                        for a in range(4):
                            m = nc.tensor.transpose(e.bank[4 + f][:, 128 * a:128 * a + 128], p[:, 512 * f + 128 * a:512 * f + 128 * a + 128], e.ident)
                        m.then_inc(s["p_turned"], 1)
                    nc.tensor.transpose(e.bank[3][0:TSA, 0:128], p[:, PAST:NP], e.ident).then_inc(s["p_turned"], 1)
                    pe.wait_ge(s["pt_v"], b * 3 + 4)
                    pe.wait_ge(s["pt_s"], b * 2 + 3)
                    for g in range(NPG):
                        pe.wait_ge(s[f"v_in{g % 4}"], b * 64 + 16 * (g // 4 + 1))
                        for h in range(KVH):
                            m = mm(e.bank[2][:, 128 + 32 * h:160 + 32 * h], vrows[:, g % 4, 128 * h:128 * h + 128],
                                   pt[:, 128 * g + 32 * h:128 * g + 32 * h + 32], start=g == 0 and h == 0, stop=False, skip_group_check=True)
                        m.then_inc(s["v_used"], 1)
                    for h in range(KVH):
                        m = mm(e.bank[2][:, 128 + 32 * h:160 + 32 * h], v_new[0:TSA, 128 * h:128 * h + 128],
                               pt[0:TSA, 128 * NPG + 32 * h:128 * NPG + 32 * h + 32], start=False, stop=True, skip_group_check=True)
                    m.then_inc(s["o_ready"], 1)

            @block.scalar
            def _(act):
                with act.Fori(0, NB) as b:
                    for g in range(1, NPG, 2):
                        act.wait_ge(s["k_turned"], b * NPG + (g + 5))
                        nc.scalar.activation(kt[:, :, 128 * g:128 * g + 128], e.bank[1][:].rearrange("p (h t) -> p h t", h=KVH),
                                             ACT.Copy).then_inc(s["kt_s"], 1)
                    act.wait_ge(s["negmax"], b + 1)
                    nc.scalar.activation(p, p, ACT.Exp, bias=nm[:], accum_out=den[:]).then_inc(s["exped"], 1)
                    for f in (1, 3):
                        act.wait_ge(s["p_turned"], b * 5 + (f + 1))
                        nc.scalar.activation(pt[:, 512 * f:512 * f + 512], e.bank[4 + f][:], ACT.Copy).then_inc(s["pt_s"], 1)

            @block.vector
            def _(dve):
                v = nc.vector
                dve.wait_ge(s["tables_in"], 32)
                with dve.Fori(0, NB) as b:
                    n = [0]

                    def step(ins):
                        ins.then_inc(s["step"], 1)
                        n[0] += 1

                    def settled():
                        dve.wait_ge(s["step"], b * STEPS + n[0])

                    def past_scores(q):
                        dve.wait_ge(s["scores"], b * 4 + (q + 1))
                        step(v.tensor_reduce(gate[:, 2 * q:2 * q + 2], e.bank[4 + q][:].rearrange("p (a k) -> p a k", a=2), AX.X, ALU.add))
                        step(v.tensor_tensor(p[:, 512 * q:512 * q + 512], e.bank[4 + q][:], past[:, 512 * q:512 * q + 512], ALU.add))

                    v.tensor_copy(qb[:], qt[:, :, ds(b * TS + TP, TS)]).then_inc(s["q_ready"], 1)
                    for g in range(0, NPG, 2):
                        dve.wait_ge(s["k_turned"], b * NPG + (g + 5))
                        v.tensor_copy(kt[:, :, 128 * g:128 * g + 128], e.bank[0][:].rearrange("p (h t) -> p h t", h=KVH)).then_inc(s["kt_v"], 1)
                        if g % 4 == 2 and g >= 6:
                            past_scores(g // 4 - 1)
                    past_scores(3)
                    dve.wait_ge(s["own_scores"], b + 1)
                    step(v.tensor_tensor(p[:, PAST:NP].unsqueeze(1), e.bank[2][:, 0:TSA].unsqueeze(1), own[:, ds(b, 1), :], ALU.add))
                    settled()
                    gi = gate[:].unsqueeze(1).to_broadcast([128, NBLK, NBLK])
                    gj = gate[:].unsqueeze(2).to_broadcast([128, NBLK, NBLK])
                    step(v.tensor_tensor(above[:], gi, gj, ALU.is_gt))
                    step(v.tensor_tensor(tied[:], gi, gj, ALU.is_equal))
                    settled()
                    step(v.tensor_tensor(tied[:], tied[:], e.const[:, C_TIE:C_TIE + 64].rearrange("p (j i) -> p j i", j=NBLK), ALU.mult))
                    settled()
                    step(v.tensor_tensor(above[:], above[:], tied[:], ALU.add))
                    settled()
                    step(v.tensor_reduce(rank[:], above[:], AX.X, ALU.add))
                    settled()
                    step(v.tensor_scalar(drop[:], rank[:], TOPK - 0.5, NEG, ALU.is_gt, ALU.mult))
                    settled()
                    step(v.tensor_scalar(rank[:], gate[:], 0.5 * NEG * BLK, NEG, ALU.is_le, ALU.mult))
                    settled()
                    step(v.tensor_tensor(drop[:], drop[:], rank[:], ALU.add))
                    assert n[0] == STEPS, n
                    settled()
                    p3 = p[:, 0:PAST].rearrange("p (a k) -> p a k", a=NBLK)
                    v.tensor_tensor(p3, p3, drop[:].unsqueeze(2).to_broadcast([128, NBLK, BLK]), ALU.add).then_inc(s["dropped"], 1)
                    dve.wait_ge(s["dropped"], b + 1)
                    v.tensor_reduce(nm[:], p, AX.X, ALU.max, negate=True).then_inc(s["negmax"], 1)
                    dve.wait_ge(s["exped"], b + 1)
                    v.reciprocal(rec[:], den[:]).then_inc(s["recips"], 1)
                    dve.wait_ge(s["recips"], b + 1)
                    v.tensor_scalar(p, p, rec[:], None, ALU.mult).then_inc(s["probs"], 1)
                    for f in (0, 2):
                        dve.wait_ge(s["p_turned"], b * 5 + (f + 1))
                        v.tensor_copy(pt[:, 512 * f:512 * f + 512], e.bank[4 + f][:]).then_inc(s["pt_v"], 1)
                    dve.wait_ge(s["p_turned"], b * 5 + 5)
                    v.tensor_copy(pt[0:TSA, 128 * NPG:128 * NPG + 128], e.bank[3][0:TSA, 0:128]).then_inc(s["pt_v"], 1)
                    dve.wait_ge(s["o_ready"], b + 1)
                    go = gt[:, :, ds(b * TS + TP, TS)]
                    v.tensor_tensor(go, go, e.bank[2][:, 128:256].rearrange("p (h t) -> p h t", h=AH), ALU.mult).then_inc(s["o_out"], 1)


def moba(e, p_in, p_out, nxt):
    nc, d = e.nc, e.d
    rmsnorm(e, "norm_mix1", e.xt, T, VA_MIX + KC, e.h)
    with ExitStack() as ctx:
        sb = lambda n, sh: ctx.enter_context(nc.sbuf_tensor(n, sh, F32))
        qt, kt, gt = sb("m_q", [128, AH, T]), sb("m_k", [128, KVH, T]), sb("m_g", [128, AH, T])
        vrows = sb("m_vrows", [128, 3, 512])
        with ExitStack() as c2:
            vt = c2.enter_context(nc.sbuf_tensor("m_v", [128, KVH, T], F32))
            krows = c2.enter_context(nc.sbuf_tensor("m_krows", [128, 3, 512], F32))
            with nc.Block() as block:
                @block.sync
                def _(sp):
                    p_in.later_loads(sp)
                    p_out.first_loads(sp)

                @block.tensor
                def _(pe):
                    p_in.matmuls(pe, lambda k: e.h[:, k, :])

                @block.scalar
                def _(act):
                    def tile(i, j, dst, func, scale=1.0):
                        p_in.wait_tile(act, i, j)
                        nc.scalar.activation(dst, e.bank[j][:, 0:T].unsqueeze(1), func, scale=scale).then_inc(e.bank_free, 1)

                    p_in.take_over(act)
                    with act.Fori(0, 4) as i:
                        for j in range(4):
                            tile(i, j, qt[:, ds(4 * i + j, 1), :], ACT.Copy, QSCALE)
                    for i, dst in ((4, kt), (5, vt)):
                        for j in range(4):
                            tile(i, j, dst[:, j:j + 1, :], ACT.Copy)
                    with act.Fori(0, 4) as i:
                        for j in range(4):
                            tile(i + 6, j, gt[:, ds(4 * i + j, 1), :], ACT.Silu)
            s = c2.enter_context(stage(nc, "mrows", ["turned", "evac_v", "evac_s", "stored"]))
            fills = []
            for src, dst in ((kt, krows), (vt, vrows)):
                for u in range(3):
                    n = 128 if u < 2 else TSA
                    fills.append(([(128 * h, src[:, h, 128 * u:128 * u + n], 128, n) for h in range(KVH)], n, 512, dst[0:n, u, :]))
            tensor, copies = transposes(e, None, s, fills)
            with nc.Block() as block:
                block.tensor(tensor)
                block.vector(lambda eng: copies(eng, 0))
                block.scalar(lambda eng: copies(eng, 1))

                @block.gpsimd
                def _(pool):
                    pool.wait_ge(s["evac_v"], 3)
                    pool.wait_ge(s["evac_s"], 3)
                    for n, r in (("k", krows), ("v", vrows)):
                        pool.dma_start(d[f"{n}_prompt_o"][0, 0].rearrange("(t p) h c -> p t (h c)", p=128), r[:, 0:2, :]).then_inc(s["stored"], 16)
                        pool.dma_start(d[f"{n}_sample_o"][0].rearrange("b t h c -> (b t) (h c)"), r[0:TSA, 2, :]).then_inc(s["stored"], 16)
                    pool.wait_ge(s["stored"], 64)
        with ExitStack() as c2:
            dist = c2.enter_context(nc.sbuf_tensor("m_dist", [128, 2, TP], F32))
            s = c2.enter_context(stage(nc, "mdist", ["dist_in"]))
            with nc.Block() as block:
                @block.sync
                def _(sp):
                    sp.dma_start(dist[:], d["c_dist"].rearrange("p (r k) -> p r k", r=2)).then_inc(s["dist_in"], 16)
                    sp.wait_ge(s["dist_in"], 16)
            prompt_attention(e, "mp", AH, lambda h: qt[:, h, 0:TP], lambda h: kt[:, h // G4, 0:TP],
                             lambda h, m: vrows[:, m, 128 * (h // G4):128 * (h // G4) + 128], lambda h: gt[:, h, 0:TP],
                             bias=lambda h: (dist[:], e.const[:, C_SLOPE + h:C_SLOPE + h + 1]))
        moba_sample(e, qt, kt, vrows[:, 2, :], gt)
        add_projection(e, "odd_out", p_out, lambda k: gt[:, k, :], nxt)


def final(e):
    nc, d = e.nc, e.d
    rmsnorm(e, "norm_final", e.xt, T, VA_FIN, e.h)
    with ExitStack() as ctx:
        s = ctx.enter_context(stage(nc, "final", ["turned", "evac_v", "evac_s", "stored"]))
        rows = ctx.enter_context(nc.sbuf_tensor("y_rows", [128, 3, D], F32))
        fills = []
        for u in range(3):
            n = 128 if u < 2 else TSA
            for c in range(0, KC, 4):
                fills.append(([(128 * a, e.h[:, c + a, 128 * u:128 * u + n], 128, n) for a in range(4)], n, 512, rows[0:n, u, 128 * c:128 * c + 512]))
        tensor, copies = transposes(e, None, s, fills)
        with nc.Block() as block:
            block.tensor(tensor)
            block.vector(lambda eng: copies(eng, 0))
            block.scalar(lambda eng: copies(eng, 1))

            @block.sync
            def _(sp):
                for u in range(3):
                    sp.wait_ge(s["evac_v"], 2 * (u + 1))
                    sp.wait_ge(s["evac_s"], 2 * (u + 1))
                    if u < 2:
                        sp.dma_start(d["y_prompt_o"][0, 128 * u:128 * u + 128, :], rows[:, u, :]).then_inc(s["stored"], 16)
                    else:
                        sp.dma_start(d["y_sample_o"].rearrange("b t n -> (b t) n"), rows[0:TSA, u, :]).then_inc(s["stored"], 16)
                sp.wait_ge(s["stored"], 48)


def build(nc, d):
    e = Trunk(nc, d)
    with ExitStack() as ctx:
        sb = lambda n, sh: ctx.enter_context(nc.sbuf_tensor(n, sh, F32))
        e.const = sb("const", [128, C_N])
        e.ident = e.const[:, C_ID:C_ID + 128]
        e.ones = e.const[:, C_ONE:C_ONE + 128]
        e.va, e.vb, e.vc = sb("va", [128, VA_N]), sb("vb", [128, VB_N]), sb("vc", [128, VC_N])
        e.w = sb("w_slots", [128, NSLOT, KC * 128])
        e.slot_view = lambda j, kch, cols: e.w[:, j, :].rearrange("p (k n) -> p k n", n=cols)
        e.xt = sb("xt", [128, KC, T])
        e.h = sb("h", [128, KC, T])
        e.km = [sb(f"km{i}", [128, CAH, NM]) for i in range(2)]
        e.vm = [sb(f"vm{i}", [128, 2, 512]) for i in range(2)]
        e.bank = [ctx.enter_context(nc.psum_tensor(f"bank{i}", [128, 512], F32)) for i in range(8)]
        sem = lambda n: ctx.enter_context(nc.semaphore(n))
        e.pe_event, e.bank_free = sem("pe_event"), sem("bank_free")
        e.w_landed = [sem(f"w_landed{j}") for j in range(NSLOT)]

        w_ev = d["ev_w_in"][0]
        p_kv = [Proj(e, columns(d["ca_w_kv"][l]), 8, ntok=NM) for l in range(2)]
        p_z = Proj(e, columns(w_ev, OFF_Z), 16)
        p_xbc = Proj(e, columns(w_ev, OFF_XBC), CCH)
        p_sc = Proj(e, sc_columns(w_ev), 64)
        p_evo = Proj(e, two_slot_columns(d["ev_w_out"][0]), 16, slots_per_tile=2)
        p_xq, p_xo = [None, None], [None, None]
        p_xq[0] = Proj(e, columns(d["ca_w_q"][0]), 8)
        p_xo[0] = Proj(e, wide_columns(d["ca_w_out"][0]), 16, kch=4, tiles_per_slot=4)
        p_od = Proj(e, columns(d["od_w_in"][0]), 40)
        p_odo = Proj(e, columns(d["od_w_out"][0]), 16)
        p_xq[1] = Proj(e, columns(d["ca_w_q"][1]), 8)
        p_xo[1] = Proj(e, wide_columns(d["ca_w_out"][1]), 16, kch=4, tiles_per_slot=4)
        e.next_proj = p_kv[0]
        with ExitStack() as c2:
            e.memt = c2.enter_context(nc.sbuf_tensor("memt", [128, KC, NM], F32))
            setup(e)
            memory_kv(e, 0, p_kv[0], p_kv[1])
            memory_kv(e, 1, p_kv[1], p_z)
        with ExitStack() as c2:
            sb2 = lambda n, sh: c2.enter_context(nc.sbuf_tensor(n, sh, F32))
            e.zs, e.xbc, e.ysc = sb2("zs", [128, KC, T]), sb2("xbc", [128, CCH, T]), sb2("ysc", [128, KC, T])
            e.dt = sb2("dt", [128, 3, SSD_HEADS])
            rmsnorm(e, "norm_mix0", e.xt, T, VA_MIX, e.h)
            even_projections(e, p_z, p_xbc, p_sc, p_evo)
            ssd(e)
            add_projection(e, "even_out", p_evo, lambda k: e.xbc[:, k, :] if k < KC else e.ysc[:, k - KC, :], p_xq[0])
        cross_attention(e, 0, p_xq[0], p_xo[0], p_od)
        moba(e, p_od, p_odo, p_xq[1])
        cross_attention(e, 1, p_xq[1], p_xo[1], None)
        final(e)


_OUTS = [("y_prompt_o", (1, TP, D)), ("y_sample_o", (NB, TS, D)),
         ("k_prompt_o", (1, 1, TP, KVH, DH)), ("v_prompt_o", (1, 1, TP, KVH, DH)),
         ("conv_prompt_o", (1, 1, CW - 1, CONV_CH)), ("ssm_prompt_o", (1, 1, SSD_HEADS, HD, NST)),
         ("sc_prompt_o", (1, 1, SCW - 1, D)),
         ("mem_k_o", (2, 1, NM, CAH, DH)), ("mem_v_o", (2, 1, NM, CAH, DH)),
         ("k_sample_o", (1, NB, TS, KVH, DH)), ("v_sample_o", (1, NB, TS, KVH, DH)),
         ("conv_sample_o", (1, NB, CW - 1, CONV_CH)), ("ssm_sample_o", (1, NB, SSD_HEADS, HD, NST)),
         ("sc_sample_o", (1, NB, SCW - 1, D))]


def kernel(**inputs):
    import numpy as _np
    import concourse.bacc as _bacc
    from concourse.bass_utils import run_bass_kernel_spmd as _run

    nc = _bacc.Bacc("TRN2", target_bir_lowering=False, num_devices=1)
    arrays = {k: _np.ascontiguousarray(v) for k, v in inputs.items()}
    arrays.update(host_constants())
    d = {k: nc.dram_tensor(f"in_{k}", v.shape, mybir.dt.from_np(v.dtype), kind="ExternalInput").ap()
         for k, v in arrays.items()}
    for name, shape in _OUTS:
        d[name] = nc.dram_tensor(name, shape, F32, kind="ExternalOutput").ap()
    build(nc, d)
    r = _run(nc, [{f"in_{k}": v for k, v in arrays.items()}], core_ids=[0])
    return tuple(r.results[0][name] for name, _ in _OUTS)
```

```python
from contextlib import ExitStack, contextmanager

import numpy as np
import concourse.bass as bass
from concourse import mybir

F32 = mybir.dt.float32
F32R = mybir.dt.float32r
I32 = mybir.dt.int32
ACT = mybir.ActivationFunctionType
ALU = mybir.AluOpType
AX = mybir.AxisListType
ds = bass.ds

D = 2048
KC = D // 128
TP = 256
NB, TS = 8, 8
TSA = NB * TS
T = TP + TSA
EPS = 1e-5
NEG = -1e30
SSD_HEADS, HD, GROUPS, NST = 32, 64, 4, 128
CONV_CH = 3072
CCH = CONV_CH // 128
CW, SCW = 4, 3
OFF_Z, OFF_XBC, OFF_DT, OFF_SC = 0, 2048, 5120, 5152
AH, KVH, DH, G4 = 16, 4, 128, 4
PAST, PAGE, BLK = 2048, 128, 256
NPG, NBLK, TOPK = PAST // PAGE, PAST // BLK, 3
NM, CAH = 256, 4
QSCALE = float(DH) ** -0.5
NSLOT = 4
CROSS_V_AHEAD = 4
NSPLIT = 2

C_ID, C_ONE, C_TRIP, C_TRIS, C_BLKS, C_BM, C_SLOPE, C_TIE = 0, 128, 256, 384, 448, 512, 520, 536
C_N = 600
VA_MIX, VA_CROSS, VA_MEM, VA_FIN, VA_EV, VA_N = 0, 32, 64, 96, 112, 128
VB_CW, VB_CB, VB_N = 0, 96, 120
VC_N = 48


def host_constants():
    f = np.float32
    c = np.zeros((128, C_N), f)
    c[:, C_ID:C_ID + 128] = np.eye(128)
    c[:, C_ONE:C_ONE + 128] = 1
    s, l = np.arange(128)[:, None], np.arange(128)[None, :]
    c[:, C_TRIP:C_TRIP + 128] = s <= l
    same = (np.arange(64)[:, None] // TS) == (np.arange(64)[None, :] // TS)
    c[:64, C_TRIS:C_TRIS + 64] = same & (np.arange(64)[:, None] <= np.arange(64)[None, :])
    c[:64, C_BLKS:C_BLKS + 64] = same
    c[:64, C_BM:C_BM + 8] = (np.arange(64)[:, None] // TS) == np.arange(8)[None, :]
    slopes = np.array([2.0 ** (-8.0 * (h + 1) / AH) for h in range(AH)], dtype=f)
    c[:, C_SLOPE:C_SLOPE + AH] = slopes[None]
    c[:, C_TIE:C_TIE + 64] = (np.arange(8)[None, :] < np.arange(8)[:, None]).reshape(1, 64)
    q = np.arange(2)[None, :, None] * 128 + np.arange(128)[:, None, None]
    k = np.arange(256)[None, None, :]
    dist = np.where(q >= k, (k - q).astype(f), f(NEG)).astype(f).reshape(128, 512)
    head, tok = np.arange(128) // TS, np.arange(128) % TS
    past = (-slopes[head][:, None] * (PAST + tok[:, None] - np.arange(PAST)[None]).astype(f)).astype(f)
    col = np.arange(64)
    own = np.full((128, NB, 64), NEG, f)
    for b in range(NB):
        d = tok[:, None] - (col[None] - TS * b)
        ok = (col[None] // TS == b) & (d >= 0)
        own[:, b] = np.where(ok, -slopes[head][:, None] * d.astype(f), f(NEG))
    qmask = np.broadcast_to((col[None] // TS == np.arange(NB)[:, None]).astype(f).reshape(1, 512), (128, 512))
    selhp = np.zeros((32, 2048), f)
    selhp[np.arange(2048) // HD, np.arange(2048)] = 1
    return {"c_main": c, "c_dist": dist, "c_past": past, "c_own": own.reshape(128, 512),
            "c_qmask": np.ascontiguousarray(qmask), "c_selhp": selhp}


class Trunk:

    def __init__(self, nc, d):
        self.nc, self.d = nc, d
        self.tile = 0
        self.slot = 0


@contextmanager
def stage(nc, label, names):
    sems = {n: nc.alloc_semaphore(name=f"{label}_{n}") for n in names}
    yield sems
    nc.clear_and_free_semaphores(list(sems.values()))
    nc.all_engine_barrier()


class Proj:

    def __init__(self, e, w_src, tiles, ntok=T, kch=KC, tiles_per_slot=1):
        self.e, self.w_src, self.tiles, self.ntok, self.kch = e, w_src, tiles, ntok, kch
        self.tps = tiles_per_slot
        self.slots = tiles // tiles_per_slot
        self.iters = self.slots // NSLOT
        self.tile0, self.slot0 = e.tile, e.slot
        e.tile += tiles
        e.slot += self.slots

    def load(self, sp, i, j):
        sp.wait_ge(self.e.w_lo, i * NSLOT + (self.slot0 + j + 1))
        src, kch, cols = self.w_src(i, j)
        sp.dma_start(self.e.w[:, j, :].rearrange("p (k n) -> p k n", n=cols), src).then_inc(self.e.w_landed[j], 16)

    def first_loads(self, sp):
        for j in range(NSLOT):
            self.load(sp, 0, j)

    def later_loads(self, sp):
        if self.iters > 1:
            with sp.Fori(0, self.iters - 1) as i:
                for j in range(NSLOT):
                    self.load(sp, i + 1, j)

    def high(self, act, i, j):
        e = self.e
        act.wait_ge(e.w_landed[j % NSLOT], i * 16 + 16 * ((self.slot0 + j) // NSLOT + 1))
        done = (j - 1) * self.tps if j else -1
        act.wait_ge(e.pe_event, i * (NSLOT * self.tps) + (NSLOT + self.tile0 + done))
        e.nc.scalar.activation(e.w_split[0][:, j % NSPLIT, :], e.w[:, j % NSLOT, :], ACT.Copy).then_inc(e.w_hi, 1)

    def low(self, pool):
        e = self.e

        def body(i):
            for j in range(NSLOT):
                pool.wait_ge(e.w_hi, i * NSLOT + (self.slot0 + j + 1))
                e.nc.gpsimd.tensor_tensor(e.w_split[1][:, j % NSPLIT, :], e.w[:, j, :],
                                          e.w_split[0][:, j % NSPLIT, :].bitcast(F32), ALU.subtract).then_inc(e.w_lo, 1)
        self.loop(pool, body)

    def loop(self, eng, body):
        if self.iters == 1:
            body(0)
        else:
            with eng.Fori(0, self.iters) as i:
                body(i)

    def act_loop(self, act, tile, more=False):
        def body(i, last):
            for j in range(NSLOT):
                tile(i, j)
                if not last or j + NSPLIT < NSLOT or more:
                    self.high(act, i, j + NSPLIT)

        if self.iters > 1:
            with act.Fori(0, self.iters - 1) as i:
                body(i, False)
        body(self.iters - 1, True)

    def first_highs(self, act):
        for j in range(NSPLIT):
            self.high(act, 0, j)

    def matmuls(self, pe, rhs):
        e = self.e

        def body(i):
            for j in range(NSLOT * self.tps):
                slot = j // self.tps
                w = [e.w_split[p][:, slot % NSPLIT, :].rearrange("p (k n) -> p k n", n=128 * self.tps) for p in range(2)]
                cols = slice(128 * (j % self.tps), 128 * (j % self.tps) + 128)
                if j % self.tps == 0:
                    pe.wait_ge(e.w_hi, i * NSLOT + (self.slot0 + slot + 1))
                pe.wait_ge(e.bank_free, i * (NSLOT * self.tps) + (self.tile0 + j + 1))
                out = e.bank[j % NSLOT][:, 0:self.ntok]
                for k in range(self.kch):
                    for part in range(2):
                        e.nc.tensor.matmul(out, w[0][:, k, cols], rhs(k)[part], start=(k == 0 and part == 0), stop=False)
                if j % self.tps == 0:
                    pe.wait_ge(e.w_lo, i * NSLOT + (NSLOT + self.slot0 + slot + 1))
                for k in range(self.kch):
                    m = e.nc.tensor.matmul(out, w[1][:, k, cols], rhs(k)[0], start=False, stop=k == self.kch - 1)
                m.then_inc(e.pe_event, 1)

        self.loop(pe, body)

    def take_over(self, eng):
        eng.wait_ge(self.e.bank_free, NSLOT + self.tile0)

    def wait_tile(self, eng, i, j):
        eng.wait_ge(self.e.pe_event, i * (NSLOT * self.tps) + (NSLOT + self.tile0 + j + 1))


@contextmanager
def split_buffers(e, label, kch, ntok=T):
    with ExitStack() as ctx:
        sb = lambda n, sh: ctx.enter_context(e.nc.sbuf_tensor(f"{label}_{n}", sh, F32R))
        e.w_split = [sb(f"w_{p}", [128, NSPLIT, KC * 128]) for p in ("hi", "lo")]
        yield [sb(f"x_{p}", [128, kch, ntok]) for p in ("hi", "lo")]


def split_input(e, label, src, dst, kch):
    nc = e.nc
    with ExitStack() as ctx:
        s = ctx.enter_context(stage(nc, label, ["hi", "lo_v", "lo_p"]))
        with nc.Block() as block:
            @block.scalar
            def _(act):
                for k in range(0, kch, 2):
                    nc.scalar.activation(dst[0][:, k:k + 2, :], src(k), ACT.Copy).then_inc(s["hi"], 1)

            def low(eng, q, par, sem):
                for k in range(0, kch, 2):
                    if k // 2 % 3 in par:
                        eng.wait_ge(s["hi"], k // 2 + 1)
                        q.tensor_tensor(dst[1][:, k:k + 2, :], src(k), dst[0][:, k:k + 2, :].bitcast(F32), ALU.subtract).then_inc(sem, 1)

            block.vector(lambda dve: low(dve, nc.vector, (0, 1), s["lo_v"]))
            block.gpsimd(lambda pool: low(pool, nc.gpsimd, (2,), s["lo_p"]))


def columns(w, off=0, step=128):
    wv = w.rearrange("(c p) n -> p c n", p=128)

    def src(i, j):
        return wv[:, :, ds(i * (NSLOT * step) + (off + j * step), 128)], KC, 128
    return src


def wide_columns(w):
    wv = w.rearrange("(c p) n -> p c n", p=128)

    def src(i, j):
        return wv[:, :, 512 * j:512 * j + 512], 4, 512
    return src


def sc_columns(w):
    wv = w.rearrange("(c p) n -> p c n", p=128)

    def src(i, j):
        return wv[:, :, ds(i * 128 + (OFF_SC + j * D), 128)], KC, 128
    return src


def transposes(e, s, fills):
    nc = e.nc
    evac = ("evac_v", "evac_s")

    def tensor(pe):
        for f, (parts, rows, _, _) in enumerate(fills):
            if f >= 8:
                pe.wait_ge(s[evac[f % 2]], (f - 8) // 2 + 1)
            for col, src, k, m in parts:
                t = nc.tensor.transpose(e.bank[f % 8][0:m, col:col + k], src, e.ident[0:k, 0:k])
            t.then_inc(s["turned"], 1)

    def copies(eng, par):
        for f, (_, rows, width, out) in enumerate(fills):
            if f % 2 == par:
                eng.wait_ge(s["turned"], f + 1)
                src = e.bank[f % 8][0:rows, 0:width]
                if len(out.shape) == 3:
                    src = src.rearrange("p (a b) -> p a b", a=out.shape[1])
                if par:
                    nc.scalar.activation(out, src, ACT.Copy).then_inc(s["evac_s"], 1)
                else:
                    nc.vector.tensor_copy(out, src).then_inc(s["evac_v"], 1)

    return tensor, copies


def setup(e):
    nc, d = e.nc, e.d
    with ExitStack() as ctx:
        sb = lambda n, sh: ctx.enter_context(nc.sbuf_tensor(n, sh, F32))
        s = ctx.enter_context(stage(nc, "setup", ["consts_in", "zeroed", "rows_in", "x_in", "mem_in", "turned", "evac_v", "evac_s"]))
        rows = sb("vec_rows", [128, 3, 128])
        xr = sb("x_rows", [128, 3, D])
        mr = sb("mem_rows", [128, 2, D])
        fills = [([(0, rows[:, 0, :], 128, 128)], 128, 128, e.va[:]),
                 ([(0, rows[0:VB_N, 1, :], VB_N, 128)], 128, VB_N, e.vb[:]),
                 ([(0, rows[0:VC_N, 2, :], VC_N, 128)], 128, VC_N, e.vc[:])]
        nvec = len(fills)
        for c in range(KC):
            cs = slice(128 * c, 128 * c + 128)
            fills.append(([(0, xr[:, 0, cs], 128, 128), (128, xr[:, 1, cs], 128, 128),
                           (256, xr[0:64, 2, cs], 64, 128)], 128, T, e.xt[:, c, :]))
        nx = len(fills)
        for c in range(0, KC, 2):
            fills.append(([(128 * (2 * a + m), mr[:, m, 128 * (c + a):128 * (c + a) + 128], 128, 128)
                           for a in range(2) for m in range(2)], 128, 512, e.memt[:, c:c + 2, :]))
        tensor, copies = transposes(e, s, fills)
        with nc.Block() as block:
            @block.sync
            def _(sp):
                sp.dma_start(e.const[:], d["c_main"]).then_inc(s["consts_in"], 16)
                vec = [("norm_mix_w", 0, VA_MIX), ("norm_cross_w", 0, VA_CROSS), ("norm_mem_w", 0, VA_MEM),
                       ("final_norm_w", 0, VA_FIN), ("ev_norm_w", 0, VA_EV),
                       ("ev_conv_w", 1, VB_CW), ("ev_conv_b", 1, VB_CB), ("ev_sc_w", 2, 0)]
                for name, t, row in vec:
                    a = d[name]
                    if len(a.shape) > 1:
                        a = a.rearrange("a b -> (a b)" if len(a.shape) == 2 else "a b c -> (a b c)")
                    n = a.shape[0] // 128
                    sp.dma_start(rows[row:row + n, t, :], a.rearrange("(r p) -> r p", p=128)).then_inc(s["rows_in"], 16)
                sp.dma_start(xr[:, 0:2, :], d["x_prompt"][0].rearrange("(t p) n -> p t n", p=128)).then_inc(s["x_in"], 16)
                sp.dma_start(xr[0:64, 2, :], d["x_sample"].rearrange("b t n -> (b t) n")).then_inc(s["x_in"], 16)
                sp.dma_start(mr[:], d["mem_prompt"][0].rearrange("(t p) n -> p t n", p=128)).then_inc(s["mem_in"], 16)
                e.next_proj.first_loads(sp)

            @block.gpsimd
            def _(pool):
                pool.sem_inc(e.w_lo, NSLOT)

            @block.tensor
            def _(pe):
                pe.sem_inc(e.pe_event, NSLOT)
                pe.wait_ge(s["consts_in"], 16)
                pe.wait_ge(s["rows_in"], 16 * 8)
                pe.wait_ge(s["x_in"], 32)
                pe.wait_ge(s["mem_in"], 16)
                tensor(pe)

            @block.vector
            def _(dve):
                dve.sem_inc(e.bank_free, NSLOT)
                copies(dve, 0)

            @block.scalar
            def _(act):
                copies(act, 1)


def norm_sums(e, label, src, ntok, r):
    nc = e.nc
    RING = 4
    with ExitStack() as ctx:
        s = ctx.enter_context(stage(nc, label, ["squared_v", "squared_s", "added", "var", "std", "rstd"]))
        sq = ctx.enter_context(nc.sbuf_tensor(f"{label}_sq", [128, RING, T], F32))

        def squares(eng, par, square, sem):
            for n in range(KC // 4):
                c = 4 * n + 2 * par
                if c >= RING:
                    eng.wait_ge(s["added"], c + 2 - RING)
                square(sq[:, c % RING:c % RING + 2, 0:ntok], src[:, c:c + 2, 0:ntok]).then_inc(sem, 1)

        with nc.Block() as block:
            @block.scalar
            def _(act):
                squares(act, 1, lambda o, x: nc.scalar.activation(o, x, ACT.Square), s["squared_s"])
                act.wait_ge(s["var"], 1)
                nc.scalar.activation(r[:, 0:ntok], r[:, 0:ntok], ACT.Sqrt).then_inc(s["std"], 1)

            @block.tensor
            def _(pe):
                for c in range(KC):
                    if c % 2 == 0:
                        pe.wait_ge(s["squared_s" if c % 4 else "squared_v"], c // 4 + 1)
                    nc.tensor.matmul(e.bank[4][:, 0:ntok], e.ones, sq[:, c % RING, 0:ntok], start=c == 0,
                                     stop=c == KC - 1).then_inc(s["added"], 1)

            @block.vector
            def _(dve):
                squares(dve, 0, lambda o, x: nc.vector.tensor_tensor(o, x, x, ALU.mult), s["squared_v"])
                dve.wait_ge(s["added"], KC)
                nc.vector.tensor_scalar(r[:, 0:ntok], e.bank[4][:, 0:ntok], 1.0 / D, EPS, ALU.mult, ALU.add).then_inc(s["var"], 1)
                dve.wait_ge(s["std"], 1)
                nc.vector.reciprocal(r[:, 0:ntok], r[:, 0:ntok]).then_inc(s["rstd"], 1)


def norm_apply(e, label, src, ntok, wcol, r, dst):
    nc = e.nc
    RING = 4
    with ExitStack() as ctx:
        s = ctx.enter_context(stage(nc, label, ["normed", "hi", "lo_v", "lo_p"]))
        y = ctx.enter_context(nc.sbuf_tensor(f"{label}_y", [128, RING, T], F32))
        on_pool = lambda c: c % 2 == 1
        with nc.Block() as block:
            def low(eng, q, c, sem):
                eng.wait_ge(s["hi"], c + 1)
                q.tensor_tensor(dst[1][:, c, 0:ntok], y[:, c % RING, 0:ntok], dst[0][:, c, 0:ntok].bitcast(F32),
                                ALU.subtract).then_inc(sem, 1)

            @block.vector
            def _(dve):
                for c in range(KC + 2):
                    if c < KC:
                        if c >= RING:
                            p = c - RING
                            dve.wait_ge(s["lo_p" if on_pool(p) else "lo_v"], p // 2 + 1)
                        nc.vector.scalar_tensor_tensor(y[:, c % RING, 0:ntok], src[:, c, 0:ntok], e.va[:, wcol + c:wcol + c + 1],
                                                       r[:, 0:ntok], ALU.mult, ALU.mult).then_inc(s["normed"], 1)
                    if c >= 2 and not on_pool(c - 2):
                        low(dve, nc.vector, c - 2, s["lo_v"])

            @block.scalar
            def _(act):
                for c in range(KC):
                    act.wait_ge(s["normed"], c + 1)
                    nc.scalar.activation(dst[0][:, c, 0:ntok], y[:, c % RING, 0:ntok], ACT.Copy).then_inc(s["hi"], 1)

            @block.gpsimd
            def _(pool):
                for c in range(KC):
                    if on_pool(c):
                        low(pool, nc.gpsimd, c, s["lo_p"])


def rmsnorm(e, label, wcol, dst):
    with e.nc.sbuf_tensor(f"{label}_r", [128, T], F32) as r:
        norm_sums(e, f"{label}_sums", e.xt, T, r)
        norm_apply(e, label, e.xt, T, wcol, r, dst)


def memory_kv(e, layer, p, nxt, r):
    nc, d = e.nc, e.d
    with ExitStack() as ctx:
        x = ctx.enter_context(split_buffers(e, f"mem{layer}", KC, NM))
        norm_apply(e, f"norm_mem{layer}", e.memt, NM, VA_MEM + KC * layer, r, x)
        sb = lambda n, sh: ctx.enter_context(nc.sbuf_tensor(n, sh, F32))
        s = ctx.enter_context(stage(nc, f"mem{layer}", ["turned", "evac_v", "evac_s", "stored"]))
        kvt = sb(f"mem{layer}_kvt", [128, 2 * CAH, NM])
        kvr = sb(f"mem{layer}_kvrows", [128, 2, 2, 512])
        with nc.Block() as block:
            @block.sync
            def _(sp):
                p.later_loads(sp)
                nxt.first_loads(sp)

            @block.tensor
            def _(pe):
                p.matmuls(pe, lambda k: (x[0][:, k, :], x[1][:, k, :]))

            @block.gpsimd
            def _(pool):
                p.low(pool)

            @block.scalar
            def _(act):
                def tile(i, j):
                    p.wait_tile(act, i, j)
                    nc.scalar.activation(kvt[:, ds(4 * i + j, 1), :], e.bank[j][:, 0:NM].unsqueeze(1), ACT.Copy).then_inc(e.bank_free, 1)
                p.first_highs(act)
                p.act_loop(act, tile)
        fills = [([(128 * h, kvt[:, CAH * kv + h, 128 * m:128 * m + 128], 128, 128) for h in range(CAH)], 128, 512,
                  kvr[:, kv, m, :]) for kv in range(2) for m in range(2)]
        tensor, copies = transposes(e, s, fills)
        with nc.Block() as block:
            block.tensor(tensor)
            block.vector(lambda eng: copies(eng, 0))
            block.scalar(lambda eng: copies(eng, 1))

            @block.sync
            def _(sp):
                sp.wait_ge(s["evac_v"], 2)
                sp.wait_ge(s["evac_s"], 2)
                for kv, name in enumerate(("mem_k_o", "mem_v_o")):
                    sp.dma_start(d[name][layer, 0].rearrange("(t p) h n -> p t (h n)", p=128), kvr[:, kv]).then_inc(s["stored"], 16)
                sp.wait_ge(s["stored"], 32)


def even_projections(e, p_z, p_xbc, p_sc, nxt):
    nc, d = e.nc, e.d
    with ExitStack() as ctx:
        sb = lambda n, sh: ctx.enter_context(nc.sbuf_tensor(n, sh, F32))
        tail = sb("conv_tail", [128, CCH, 27])
        sctail = sb("sc_tail", [128, KC, 18])
        with ExitStack() as c2:
            x = c2.enter_context(split_buffers(e, "even", KC))
            rmsnorm(e, "norm_mix0", VA_MIX, x)
            rhs = lambda k: (x[0][:, k, :], x[1][:, k, :])
            dt_and_history(e, x, tail, sctail)
            conv_projections(e, p_z, p_xbc, p_sc, rhs, tail)
            short_conv_projection(e, p_sc, nxt, rhs, sctail)
        store_tails(e, tail, sctail)


def dt_and_history(e, x, tail, sctail):
    nc, d = e.nc, e.d
    with ExitStack() as ctx:
        sb = lambda n, sh, dt=F32: ctx.enter_context(nc.sbuf_tensor(n, sh, dt))
        s = ctx.enter_context(stage(nc, "hist", ["conv_in", "sc_in", "dt_w_in", "turned", "evac_v", "evac_s", "dt_hi", "dt_lo",
                                                 "dt_done", "dt_raw", "dt_turned", "dt_out"]))
        crows = e.xbc[:].rearrange("p c t -> p (c t)")[:, 0:CONV_CH]
        srows = e.ysc[:].rearrange("p c t -> p (c t)")[:, 0:D]
        wdt = sb("w_dt", [128, KC, SSD_HEADS])
        wdts = [sb(f"w_dt_{p}", [128, KC, SSD_HEADS], F32R) for p in ("hi", "lo")]
        dtt = e.zs[0:SSD_HEADS, 0, :]
        fills = [([(24 * (c - c0), crows[0:24, 128 * c:128 * c + 128], 24, 128) for c in range(c0, c0 + 12)], 128, 288,
                  tail[:, c0:c0 + 12, 3:27]) for c0 in (0, 12)]
        fills.append(([(16 * c, srows[0:16, 128 * c:128 * c + 128], 16, 128) for c in range(KC)], 128, 256, sctail[:, :, 2:18]))
        tensor, copies = transposes(e, s, fills)
        units = [(0, 128), (1, 128), (2, TSA)]
        with nc.Block() as block:
            @block.sync
            def _(sp):
                sp.dma_start(wdt[:], d["ev_w_in"][0].rearrange("(c p) n -> p c n", p=128)[:, :, OFF_DT:OFF_DT + SSD_HEADS]).then_inc(s["dt_w_in"], 16)
                sp.dma_start(crows[0:24, :], d["state_conv"][0].rearrange("b j n -> (b j) n")).then_inc(s["conv_in"], 16)
                sp.dma_start(srows[0:16, :], d["state_sc"][0].rearrange("b j n -> (b j) n")).then_inc(s["sc_in"], 16)

            @block.tensor
            def _(pe):
                pe.wait_ge(s["dt_lo"], 1)
                for n, (p, q) in enumerate(((0, 0), (0, 1), (1, 0))):
                    for k in range(KC):
                        m = nc.tensor.matmul(e.bank[4][0:SSD_HEADS, 0:T], wdts[p][:, k, :], x[q][:, k, :],
                                             start=n == 0 and k == 0, stop=n == 2 and k == KC - 1)
                m.then_inc(s["dt_done"], 1)
                pe.wait_ge(s["conv_in"], 16)
                pe.wait_ge(s["sc_in"], 16)
                tensor(pe)
                pe.wait_ge(s["dt_raw"], 1)
                for u, rows in units:
                    m = nc.tensor.transpose(e.bank[5][0:rows, 32 * u:32 * u + 32], dtt[:, 128 * u:128 * u + rows], e.ident[0:32, 0:32])
                m.then_inc(s["dt_turned"], 1)

            @block.scalar
            def _(act):
                act.wait_ge(s["dt_w_in"], 16)
                nc.scalar.activation(wdts[0][:], wdt[:], ACT.Copy).then_inc(s["dt_hi"], 1)
                copies(act, 1)

            @block.vector
            def _(dve):
                v = nc.vector
                dve.wait_ge(s["dt_hi"], 1)
                v.tensor_tensor(wdts[1][:], wdt[:], wdts[0][:].bitcast(F32), ALU.subtract).then_inc(s["dt_lo"], 1)
                dve.wait_ge(s["dt_done"], 1)
                v.tensor_copy(dtt, e.bank[4][0:SSD_HEADS, 0:T]).then_inc(s["dt_raw"], 1)
                copies(dve, 0)
                dve.wait_ge(s["dt_turned"], 1)
                v.tensor_copy(e.dt[:, 0:2, :], e.bank[5][:, 0:64].rearrange("p (u h) -> p u h", u=2)).then_inc(s["dt_out"], 1)
                v.tensor_copy(e.dt[0:TSA, 2, :], e.bank[5][0:TSA, 64:96]).then_inc(s["dt_out"], 1)


def conv_projections(e, p_z, p_xbc, p_sc, rhs, tail):
    nc = e.nc
    with ExitStack() as ctx:
            sb = lambda n, sh: ctx.enter_context(nc.sbuf_tensor(n, sh, F32))
            t = ctx.enter_context(stage(nc, "conv", ["step", "silu_done"]))
            xpp = [sb(f"conv_pad{i}", [128, CW - 1 + TP]) for i in range(2)]
            xps = [sb(f"conv_pad_s{i}", [128, NB, CW - 1 + TS]) for i in range(2)]
            acc = [sb(f"conv_acc{i}", [128, T]) for i in range(2)]
            CONV_STEPS = 12
            conv0 = 2
            with nc.Block() as block:
                @block.sync
                def _(sp):
                    p_z.later_loads(sp)
                    p_xbc.first_loads(sp)
                    p_xbc.later_loads(sp)
                    p_sc.first_loads(sp)

                @block.tensor
                def _(pe):
                    for p in (p_z, p_xbc):
                        p.matmuls(pe, rhs)

                @block.gpsimd
                def _(pool):
                    for p in (p_z, p_xbc):
                        p.low(pool)

                @block.scalar
                def _(act):
                    act.sem_inc(t["silu_done"], 2)

                    def z_tile(i, j):
                        p_z.wait_tile(act, i, j)
                        nc.scalar.activation(e.zs[:, ds(4 * i + j, 1), :], e.bank[j][:, 0:T].unsqueeze(1), ACT.Silu).then_inc(e.bank_free, 1)

                    def conv_tile(i, j):
                        act.wait_ge(t["step"], i * (4 * CONV_STEPS) + (conv0 + j * CONV_STEPS + 10))
                        nc.scalar.activation(e.xbc[:, ds(4 * i + j, 1), :], acc[j % 2][:].unsqueeze(1), ACT.Silu,
                                             bias=e.vb[:, ds(4 * i + (VB_CB + j), 1)]).then_inc(t["silu_done"], 1)

                    p_z.first_highs(act)
                    p_z.act_loop(act, z_tile, more=True)

                    def body(i, last):
                        for j in range(NSLOT):
                            if not last or j + NSPLIT < NSLOT:
                                p_xbc.high(act, i, j + NSPLIT)
                            conv_tile(i, j)
                    with act.Fori(0, p_xbc.iters - 1) as i:
                        body(i, False)
                    body(p_xbc.iters - 1, True)

                @block.vector
                def _(dve):
                    v = nc.vector
                    v.memset(xpp[0][:, 0:CW - 1], 0.0).then_inc(t["step"], 1)
                    v.memset(xpp[1][:, 0:CW - 1], 0.0).then_inc(t["step"], 1)
                    p_xbc.take_over(dve)
                    with dve.Fori(0, p_xbc.iters) as i:
                        for j in range(4):
                            n = [conv0 + j * CONV_STEPS]

                            def step(ins):
                                ins.then_inc(t["step"], 1)
                                n[0] += 1

                            def settled(k=0):
                                dve.wait_ge(t["step"], i * (4 * CONV_STEPS) + (n[0] - k))

                            xp, xs, y = xpp[j % 2], xps[j % 2], acc[j % 2]
                            ys = y[:, TP:T].rearrange("p (b t) -> p b t", b=NB)
                            p_xbc.wait_tile(dve, i, j)
                            step(v.tensor_copy(xp[:, 3:3 + TP], e.bank[j][:, 0:TP]))
                            v.tensor_copy(xs[:, :, 3:11], e.bank[j][:, TP:T].rearrange("p (b t) -> p b t", b=NB)).then_inc(e.bank_free, 1)
                            step(v.tensor_scalar(xs[:, :, 0:3], tail[:, ds(4 * i + j, 1), 3:27].rearrange("p c (b t) -> p (c b) t", b=NB),
                                                 1.0, None, ALU.mult))
                            settled()
                            dve.wait_ge(t["silu_done"], i * 4 + (j + 1))
                            for k in range(CW):
                                wk = e.vb[:, ds(4 * i + (VB_CW + k * CCH + j), 1)]
                                if k == 0:
                                    step(v.tensor_scalar(y[:, 0:TP], xp[:, 0:TP], wk, None, ALU.mult))
                                    step(v.tensor_scalar(ys, xs[:, :, 0:TS], wk, None, ALU.mult))
                                else:
                                    settled(1)
                                    step(v.scalar_tensor_tensor(y[:, 0:TP], xp[:, k:k + TP], wk, y[:, 0:TP], ALU.mult, ALU.add))
                                    settled(1)
                                    step(v.scalar_tensor_tensor(ys, xs[:, :, k:k + TS], wk, ys, ALU.mult, ALU.add))
                            step(v.tensor_scalar(tail[:, ds(4 * i + j, 1), 0:3], xp[:, TP:TP + 3].unsqueeze(1), 1.0, None, ALU.mult))
                            step(v.tensor_scalar(tail[:, ds(4 * i + j, 1), 3:27].rearrange("p c (b t) -> p (c b) t", b=NB),
                                                 xs[:, :, TS:TS + 3], 1.0, None, ALU.mult))
                            assert n[0] == conv0 + (j + 1) * CONV_STEPS


def short_conv_projection(e, p_sc, nxt, rhs, sctail):
    nc = e.nc
    with ExitStack() as ctx:
            sb = lambda n, sh: ctx.enter_context(nc.sbuf_tensor(n, sh, F32))
            t = ctx.enter_context(stage(nc, "sc", ["step"]))
            xp = sb("sc_pad", [128, SCW - 1 + TP])
            xs = sb("sc_pad_s", [128, NB, SCW - 1 + TS])
            part = [sb(f"sc_part{i}", [128, T]) for i in range(3)]
            SC_STEPS = 13
            sc0 = 1
            with nc.Block() as block:
                @block.sync
                def _(sp):
                    p_sc.later_loads(sp)
                    nxt.first_loads(sp)

                @block.tensor
                def _(pe):
                    p_sc.matmuls(pe, rhs)

                @block.gpsimd
                def _(pool):
                    p_sc.low(pool)

                @block.scalar
                def _(act):
                    def tile(i, j):
                        p_sc.wait_tile(act, i, j)
                        if j == 0:
                            act.wait_ge(t["step"], i * SC_STEPS + sc0)
                        if j == 3:
                            act.wait_ge(t["step"], i * SC_STEPS + (sc0 + 3))
                        nc.scalar.activation(part[1 if j == 3 else j][:], e.bank[j][:, 0:T],
                                             ACT.Silu if j == 3 else ACT.Copy).then_inc(e.bank_free, 1)

                    p_sc.take_over(act)
                    p_sc.first_highs(act)
                    p_sc.act_loop(act, tile)

                @block.vector
                def _(dve):
                    v = nc.vector
                    v.memset(xp[:, 0:SCW - 1], 0.0).then_inc(t["step"], 1)
                    y = part[2]
                    ys = y[:, TP:T].rearrange("p (b t) -> p b t", b=NB)
                    with dve.Fori(0, p_sc.iters) as i:
                        n = [sc0]

                        def step(ins):
                            ins.then_inc(t["step"], 1)
                            n[0] += 1

                        def settled(k=0):
                            dve.wait_ge(t["step"], i * SC_STEPS + (n[0] - k))

                        fp = lambda a: a[:, 0:TP]
                        fs = lambda a: a[:, TP:T].rearrange("p (b t) -> p b t", b=NB)
                        step(v.tensor_scalar(xs[:, :, 0:2], sctail[:, ds(i, 1), 2:18].rearrange("p c (b t) -> p (c b) t", b=NB),
                                             1.0, None, ALU.mult))
                        dve.wait_ge(e.bank_free, i * 4 + (NSLOT + p_sc.tile0 + 3))
                        step(v.tensor_tensor(xp[:, 2:2 + TP], fp(part[1]), fp(part[2]), ALU.mult))
                        step(v.tensor_tensor(xs[:, :, 2:10], fs(part[1]), fs(part[2]), ALU.mult))
                        settled()
                        for k in range(SCW):
                            wk = e.vc[:, ds(i + k * KC, 1)]
                            if k == 0:
                                step(v.tensor_scalar(y[:, 0:TP], xp[:, 0:TP], wk, None, ALU.mult))
                                step(v.tensor_scalar(ys, xs[:, :, 0:TS], wk, None, ALU.mult))
                            else:
                                settled(1)
                                step(v.scalar_tensor_tensor(y[:, 0:TP], xp[:, k:k + TP], wk, y[:, 0:TP], ALU.mult, ALU.add))
                                settled(1)
                                step(v.scalar_tensor_tensor(ys, xs[:, :, k:k + TS], wk, ys, ALU.mult, ALU.add))
                        step(v.tensor_scalar(sctail[:, ds(i, 1), 0:2], xp[:, TP:TP + 2].unsqueeze(1), 1.0, None, ALU.mult))
                        step(v.tensor_scalar(sctail[:, ds(i, 1), 2:18].rearrange("p c (b t) -> p (c b) t", b=NB),
                                             xs[:, :, TS:TS + 2], 1.0, None, ALU.mult))
                        settled(2)
                        step(v.tensor_tensor(y[:], y[:], part[0][:], ALU.mult))
                        settled()
                        dve.wait_ge(e.bank_free, i * 4 + (NSLOT + p_sc.tile0 + 4))
                        step(v.tensor_tensor(e.ysc[:, ds(i, 1), :], y[:].unsqueeze(1), part[1][:].unsqueeze(1), ALU.mult))
                        assert n[0] == sc0 + SC_STEPS


def store_tails(e, tail, sctail):
    nc, d = e.nc, e.d
    with ExitStack() as ctx:
        sb = lambda n, sh: ctx.enter_context(nc.sbuf_tensor(n, sh, F32))
        crows = sb("conv_tail_rows", [27, CONV_CH])
        srows = sb("sc_tail_rows", [18, D])
        s = ctx.enter_context(stage(nc, "tails", ["turned", "evac_v", "evac_s", "stored"]))
        fills = [([(128 * a, tail[:, c + a, :], 128, 27) for a in range(4)], 27, 512, crows[:, 128 * c:128 * c + 512])
                 for c in range(0, CCH, 4)]
        fills += [([(128 * a, sctail[:, c + a, :], 128, 18) for a in range(4)], 18, 512, srows[:, 128 * c:128 * c + 512])
                  for c in range(0, KC, 4)]
        tensor, copies = transposes(e, s, fills)
        with nc.Block() as block:
            block.tensor(tensor)
            block.vector(lambda eng: copies(eng, 0))
            block.scalar(lambda eng: copies(eng, 1))

            @block.gpsimd
            def _(pool):
                pool.wait_ge(s["evac_v"], 5)
                pool.wait_ge(s["evac_s"], 5)
                pool.dma_start(d["conv_prompt_o"][0, 0], crows[0:3, :]).then_inc(s["stored"], 16)
                pool.dma_start(d["conv_sample_o"][0].rearrange("b j n -> (b j) n"), crows[3:27, :]).then_inc(s["stored"], 16)
                pool.dma_start(d["sc_prompt_o"][0, 0], srows[0:2, :]).then_inc(s["stored"], 16)
                pool.dma_start(d["sc_sample_o"][0].rearrange("b j n -> (b j) n"), srows[2:18, :]).then_inc(s["stored"], 16)
                pool.wait_ge(s["stored"], 64)


def ssd_steps(e, z):
    nc, d = e.nc, e.d
    with ExitStack() as ctx:
        sb = lambda n, sh: ctx.enter_context(nc.sbuf_tensor(n, sh, F32))
        s = ctx.enter_context(stage(nc, "steps", ["rows_in", "step", "minus_abs", "exped", "a_head", "a_ready",
                                                  "sums_ready", "small_ready", "sums_out", "decays"]))
        head = sb("head_rows", [128, 3, SSD_HEADS])
        dcol = sb("d_skip_col", [SSD_HEADS, 1])
        x, u, q, w, r = [sb(f"softplus_{n}", [128, 3, SSD_HEADS]) for n in "xuqwr"]
        with nc.Block() as block:
            @block.sync
            def _(sp):
                sp.dma_start(z.selhp[0:32, :], d["c_selhp"]).then_inc(s["rows_in"], 16)
                sp.dma_start(head[:, 0, :], d["ev_dt_bias"][0:1, :].partition_broadcast(128)).then_inc(s["rows_in"], 16)
                sp.dma_start(head[:, 1, :], d["ev_a_log"][0:1, :].partition_broadcast(128)).then_inc(s["rows_in"], 16)
                sp.dma_start(dcol[:], d["ev_d_skip"].rearrange("a h -> h a")).then_inc(s["rows_in"], 16)

            @block.vector
            def _(dve):
                v = nc.vector
                n = [0]

                def step(ins):
                    ins.then_inc(s["step"], 1)
                    n[0] += 1
                    dve.wait_ge(s["step"], n[0])

                bias = head[:, 0:1, :].to_broadcast([128, 3, SSD_HEADS])
                dve.wait_ge(s["rows_in"], 64)
                step(v.memset(x[:], 0.0))
                step(v.tensor_copy(x[:, 0:2, :], e.dt[:, 0:2, :]))
                step(v.tensor_copy(x[0:TSA, 2, :], e.dt[0:TSA, 2, :]))
                step(v.tensor_tensor(x[:], x[:], bias, ALU.add))
                v.scalar_tensor_tensor(u[:], x[:], -1.0, x[:], ALU.mult, ALU.min).then_inc(s["minus_abs"], 1)
                dve.wait_ge(s["exped"], 1)
                step(v.tensor_scalar(w[:], u[:], 2.0, None, ALU.add))
                step(v.reciprocal(w[:], w[:]))
                step(v.tensor_tensor(u[:], u[:], w[:], ALU.mult))
                step(v.tensor_tensor(w[:], u[:], u[:], ALU.mult))
                step(v.tensor_scalar(q[:], w[:], 1.0 / 17, None, ALU.mult))
                for k in (15, 13, 11, 9, 7, 5, 3):
                    step(v.scalar_tensor_tensor(q[:], q[:], 1.0 / k, w[:], ALU.add, ALU.mult))
                step(v.scalar_tensor_tensor(q[:], q[:], 1.0, u[:], ALU.add, ALU.mult))
                step(v.tensor_scalar(q[:], q[:], 2.0, None, ALU.mult))
                step(v.scalar_tensor_tensor(e.dt[:], x[:], 0.0, q[:], ALU.max, ALU.add))
                dve.wait_ge(s["a_head"], 1)
                step(v.memset(z.acs[:], 0.0))
                step(v.memset(r[:], 0.0))
                v.scalar_tensor_tensor(z.a[:], e.dt[:], -1.0, head[:, 1:2, :].to_broadcast([128, 3, SSD_HEADS]),
                                       ALU.mult, ALU.mult).then_inc(s["a_ready"], 1)
                dve.wait_ge(s["sums_ready"], 1)
                for k, dst in ((0, z.acs), (1, r)):
                    src = e.bank[0][:, 96 * k:96 * k + 96].rearrange("p (u h) -> p u h", u=3)
                    step(v.tensor_copy(dst[:, 0:2, :], src[:, 0:2, :]))
                    step(v.tensor_copy(dst[0:TSA, 2, :], src[0:TSA, 2, :]))
                step(v.tensor_copy(z.acst[:], e.bank[1][0:32, 0:T]))
                v.tensor_tensor(z.dec[:], r[:], z.acs[:], ALU.subtract).then_inc(s["sums_out"], 1)
                dve.wait_ge(s["small_ready"], 1)
                step(v.tensor_copy(z.dhp[:], e.bank[2][:, 0:KC]))
                step(v.tensor_copy(z.etot_hp[:], e.bank[2][:, 16:144].rearrange("p (t b) -> p t b", t=KC)))

            @block.scalar
            def _(act):
                a = nc.scalar.activation
                act.wait_ge(s["minus_abs"], 1)
                a(u[:], u[:], ACT.Exp).then_inc(s["exped"], 1)
                a(head[:, 1, :], head[:, 1, :], ACT.Exp).then_inc(s["a_head"], 1)
                act.wait_ge(s["sums_out"], 1)
                a(z.eacst[:], z.acst[:], ACT.Exp).then_inc(s["decays"], 1)
                a(z.dec[:], z.dec[:], ACT.Exp).then_inc(s["decays"], 1)
                a(z.etot[:], r[:], ACT.Exp).then_inc(s["decays"], 1)

            @block.tensor
            def _(pe):
                mm = nc.tensor.matmul
                pe.wait_ge(s["a_ready"], 1)
                for u_ in range(3):
                    n, tri, blk = unit_masks(e, u_)
                    h = slice(32 * u_, 32 * u_ + 32)
                    mm(e.bank[0][0:n, 32 * u_:32 * u_ + 32], tri, z.a[0:n, u_, :], start=True, stop=True)
                    mm(e.bank[0][0:n, 96 + 32 * u_:128 + 32 * u_], blk, z.a[0:n, u_, :], start=True, stop=True)
                    m = mm(e.bank[1][0:32, 128 * u_:128 * u_ + n], z.a[0:n, u_, :], tri, start=True, stop=True)
                m.then_inc(s["sums_ready"], 1)
                pe.wait_ge(s["decays"], 1)
                for t in range(KC):
                    sel = z.selhp[0:32, 128 * t:128 * t + 128]
                    mm(e.bank[2][:, t:t + 1], sel, dcol[:], start=True, stop=True)
                    m = mm(e.bank[2][:, 16 + 8 * t:24 + 8 * t], sel, z.eacst[:, TP + TS - 1:T:TS], start=True, stop=True)
                m.then_inc(s["small_ready"], 1)


def unit_masks(e, u):
    if u < 2:
        return 128, e.const[:, C_TRIP:C_TRIP + 128], e.ones
    return TSA, e.const[0:TSA, C_TRIS:C_TRIS + TSA], e.const[0:TSA, C_BLKS:C_BLKS + TSA]


def unit_tokens(e, z, u):
    nc = e.nc
    n = unit_masks(e, u)[0]
    tok = slice(128 * u, 128 * u + n)
    with ExitStack() as ctx:
        s = ctx.enter_context(stage(nc, f"tokens{u}", ["turned", "scaled", "decayed", "b_out"]))
        with nc.Block() as block:
            @block.tensor
            def _(pe):
                for f in range(5):
                    for a in range(4):
                        m = nc.tensor.transpose(e.bank[f][0:n, 128 * a:128 * a + 128], e.xbc[:, 4 * f + a, tok], e.ident)
                    m.then_inc(s["turned"], 1)

            @block.vector
            def _(dve):
                for f in range(4):
                    dve.wait_ge(s["turned"], f + 1)
                    v3 = lambda a: a[0:n, :].rearrange("p (h q) -> p h q", h=8)
                    nc.vector.tensor_tensor(v3(z.xr[:, 512 * f:512 * f + 512]), v3(e.bank[f][:, :]),
                                            e.dt[0:n, u, 8 * f:8 * f + 8].unsqueeze(2).to_broadcast([n, 8, HD]),
                                            ALU.mult).then_inc(s["scaled"], 1)
                for f in range(4):
                    v3 = lambda a: a[0:n, :].rearrange("p (h q) -> p h q", h=8)
                    dve.wait_ge(s["scaled"], f + 1)
                    nc.vector.tensor_tensor(v3(z.xd[:, 512 * f:512 * f + 512]), v3(z.xr[:, 512 * f:512 * f + 512]),
                                            z.dec[0:n, u, 8 * f:8 * f + 8].unsqueeze(2).to_broadcast([n, 8, HD]),
                                            ALU.mult).then_inc(s["decayed"], 1)

            @block.scalar
            def _(act):
                act.wait_ge(s["turned"], 5)
                nc.scalar.activation(z.btok[0:n, :], e.bank[4][0:n, :], ACT.Copy).then_inc(s["b_out"], 1)


def unit_groups(e, z, u):
    nc = e.nc
    n, tri, _ = unit_masks(e, u)
    tok = slice(128 * u, 128 * u + n)
    has_in = u > 0
    with ExitStack() as ctx:
        s = ctx.enter_context(stage(nc, f"unit{u}", ["cb_ready", "cb_out", "spread", "diff", "exped", "weights", "within",
                                                     "decay_ready", "decay_out", "incoming", "state_ready", "state_step",
                                                     "state_out", "joined", "y_out"]))
        cbm = ctx.enter_context(nc.sbuf_tensor(f"cbm{u}", [128, 128], F32))
        mx = [[ctx.enter_context(nc.sbuf_tensor(f"mx{u}_{g}_{q}", [128, 4, 128], F32)) for q in range(2)] for g in range(2)]
        es = ctx.enter_context(nc.sbuf_tensor(f"es{u}", [128, 4, 128], F32))
        b3 = lambda i: e.bank[i][:, 0:4 * n].rearrange("p (a l) -> p a l", a=4)
        with nc.Block() as block:
            @block.tensor
            def _(pe):
                mm = nc.tensor.matmul

                def outputs(g):
                    for q in range(2):
                        pe.wait_ge(s["weights"], 2 * g + q + 1)
                        if q == 0 and g:
                            pe.wait_ge(s["joined" if has_in else "y_out"], g if has_in else 4 * g)
                        for hh in range(4):
                            h = 8 * g + 4 * q + hh
                            p0, t = 64 * (h % 2), 2 * q + hh // 2
                            m = mm(e.bank[3][p0:p0 + 64, t * n:t * n + n], z.xr[0:n, HD * h:HD * h + HD],
                                   mx[g % 2][q][0:n, hh, 0:n], start=True, stop=True)
                    m.then_inc(s["within"], 1)

                for g in range(5):
                    if g < 4:
                        if g:
                            pe.wait_ge(s["cb_out"], g)
                        mm(e.bank[0][0:n, 0:n], e.xbc[:, 16 + g, tok], e.xbc[:, 20 + g, tok],
                           start=True, stop=True).then_inc(s["cb_ready"], 1)
                        for q in range(2):
                            if g:
                                pe.wait_ge(s["diff"], 2 * g - 1 + q)
                            for hh in range(4):
                                h = 8 * g + 4 * q + hh
                                m = mm(e.bank[1 + q][0:n, hh * n:hh * n + n], e.ident[0:32, h:h + 1].to_broadcast([32, n]),
                                       z.acst[:, tok], start=True, stop=True)
                            m.then_inc(s["spread"], 1)
                    if g:
                        outputs(g - 1)
                    if g < 4:
                        if has_in:
                            if g:
                                pe.wait_ge(s["decay_out"], g)
                            for a in range(4):
                                m = mm(b3(5)[:, a, :], z.selhp[0:32, 128 * (4 * g + a):128 * (4 * g + a) + 128],
                                       z.eacst[:, tok], start=True, stop=True)
                            m.then_inc(s["decay_ready"], 1)
                        if u == 1:
                            if g:
                                pe.wait_ge(s["joined"], g)
                            for a in range(4):
                                t = 4 * g + a
                                m = mm(b3(4)[:, a, :], z.st[:, 128 * t:128 * t + 128], e.xbc[:, 20 + g, tok], start=True, stop=True)
                            m.then_inc(s["incoming"], 1)
                        if u < 2:
                            if g:
                                pe.wait_ge(s["state_out"], g)
                            mm(e.bank[6][:, 0:512], z.btok[0:n, 128 * g:128 * g + 128], z.xd[0:n, 512 * g:512 * g + 512],
                               start=True, stop=True).then_inc(s["state_ready"], 1)

            @block.scalar
            def _(act):
                for g in range(4):
                    for q in range(2):
                        act.wait_ge(s["diff"], 2 * g + q + 1)
                        m = mx[g % 2][q][0:n, :, 0:n]
                        nc.scalar.activation(m, m, ACT.Exp).then_inc(s["exped"], 1)
                    if has_in:
                        act.wait_ge(s["decay_ready"], g + 1)
                        if g:
                            act.wait_ge(s["y_out"], 4 * g)
                        nc.scalar.activation(es[:, :, 0:n], b3(5), ACT.Copy).then_inc(s["decay_out"], 1)

            @block.vector
            def _(dve):
                v = nc.vector

                def join(g):
                    dve.wait_ge(s["within"], g + 1)
                    y, src = es[:, :, 0:n], b3(3)
                    if has_in:
                        dve.wait_ge(s["decay_out"], g + 1)
                        if u == 1:
                            dve.wait_ge(s["incoming"], g + 1)
                            off = b3(4)
                        else:
                            off = z.yoff[:, 4 * g:4 * g + 4, :]
                        v.tensor_tensor(y, y, off, ALU.mult).then_inc(s["state_step"], 1)
                        dve.wait_ge(s["state_step"], joins(g))
                        v.tensor_tensor(y, y, b3(3), ALU.add).then_inc(s["joined"], 1)
                        dve.wait_ge(s["joined"], g + 1)
                        src = y
                    for a in range(4):
                        t = 4 * g + a
                        x = e.xbc[:, t, tok]
                        v.scalar_tensor_tensor(x, x, z.dhp[:, t:t + 1], src[:, a, :], ALU.mult, ALU.add).then_inc(s["y_out"], 1)
                    if u < 2:
                        dve.wait_ge(s["state_ready"], g + 1)
                        st = z.st[:, 512 * g:512 * g + 512]
                        if u == 0:
                            v.tensor_copy(st, e.bank[6][:, 0:512]).then_inc(s["state_out"], 1)
                        else:
                            st3 = st.rearrange("p (h q) -> p h q", h=8)
                            v.tensor_tensor(st3, st3, z.etot[:, 1, 8 * g:8 * g + 8].unsqueeze(2).to_broadcast([128, 8, HD]),
                                            ALU.mult).then_inc(s["state_step"], 1)
                            dve.wait_ge(s["state_step"], joins(g) + 1)
                            v.tensor_tensor(st, st, e.bank[6][:, 0:512], ALU.add).then_inc(s["state_out"], 1)

                joins = lambda g: (2 * g if u == 1 else g) + 1
                for g in range(5):
                    if g < 4:
                        dve.wait_ge(s["cb_ready"], g + 1)
                        if g:
                            dve.wait_ge(s["weights"], 2 * g)
                        v.tensor_tensor(cbm[0:n, 0:n], e.bank[0][0:n, 0:n], tri, ALU.mult).then_inc(s["cb_out"], 1)
                        for q in range(2):
                            dve.wait_ge(s["spread"], 2 * g + q + 1)
                            if g >= 2:
                                dve.wait_ge(s["within"], g - 1)
                            for hh in range(4):
                                h = 8 * g + 4 * q + hh
                                m = v.tensor_scalar(mx[g % 2][q][0:n, hh, 0:n], e.bank[1 + q][0:n, hh * n:hh * n + n],
                                                    z.acs[0:n, u, h:h + 1], 0.0, ALU.subtract, ALU.min)
                            m.then_inc(s["diff"], 1)
                        dve.wait_ge(s["cb_out"], g + 1)
                        for q in range(2):
                            dve.wait_ge(s["exped"], 2 * g + q + 1)
                            m = mx[g % 2][q][0:n, :, 0:n]
                            v.tensor_tensor(m, m, cbm[0:n, 0:n].unsqueeze(1).to_broadcast([n, 4, n]), ALU.mult).then_inc(s["weights"], 1)
                    if g:
                        join(g - 1)


def sample_states(e, z):
    nc, d = e.nc, e.d
    with ExitStack() as ctx:
        s = ctx.enter_context(stage(nc, "sstate", ["in0", "in1", "turned", "turn_out_v", "turn_out_s", "yoff_ready", "yoff_out",
                                                   "b_masked", "new_ready", "new_out", "stored0", "stored1"]))
        sb = lambda n, sh: ctx.enter_context(nc.sbuf_tensor(n, sh, F32))
        s0 = [sb(f"s0_{i}", [128, KC, 128]) for i in range(2)]
        s0t = z.st[:].rearrange("p (t n) -> p t n", t=KC)
        bmk = sb("b_masked", [TSA, 512])
        src = d["state_ssm"][0].rearrange("b h p n -> b (h p) n").rearrange("b (t q) n -> q b t n", q=128)
        dst = d["ssm_sample_o"][0].rearrange("b h p n -> b (h p) n").rearrange("b (t q) n -> q b t n", q=128)
        with nc.Block() as block:
            @block.sync
            def _(sp):
                for b in range(NB):
                    if b >= 2:
                        sp.wait_ge(s[f"stored{b % 2}"], 16 * (b // 2))
                    sp.dma_start(s0[b % 2][:], src[:, b]).then_inc(s[f"in{b % 2}"], 16)

            @block.gpsimd
            def _(pool):
                for b in range(NB):
                    pool.wait_ge(s["new_out"], KC * (b + 1))
                    pool.dma_start(dst[:, b], s0[b % 2][:]).then_inc(s[f"stored{b % 2}"], 16)
                for i in range(2):
                    pool.wait_ge(s[f"stored{i}"], 16 * (NB // 2))

            @block.tensor
            def _(pe):
                mm = nc.tensor.matmul
                for b in range(NB):
                    st = s0[b % 2]
                    pe.wait_ge(s[f"in{b % 2}"], 16 * (b // 2 + 1))
                    for f in range(4):
                        if b:
                            pe.wait_ge(s["turn_out_s" if f % 2 else "turn_out_v"], 2 * (b - 1) + f // 2 + 1)
                        for a in range(4):
                            m = nc.tensor.transpose(e.bank[f][:, 128 * a:128 * a + 128], st[:, 4 * f + a, :], e.ident)
                        m.then_inc(s["turned"], 1)
                    pe.wait_ge(s["turn_out_v"], 2 * (b + 1))
                    pe.wait_ge(s["turn_out_s"], 2 * (b + 1))
                    if b:
                        pe.wait_ge(s["yoff_out"], b)
                    for t in range(KC):
                        m = mm(e.bank[4][:, 8 * t:8 * t + 8], s0t[:, t, :], e.xbc[:, 20 + t // 4, TP + TS * b:TP + TS * b + TS],
                               start=True, stop=True)
                    m.then_inc(s["yoff_ready"], 1)
                    pe.wait_ge(s["b_masked"], b + 1)
                    for g in range(GROUPS):
                        bank = 5 + g % 3
                        k = 4 * b + g
                        if b or g == 3:
                            prev = 4 * b if g == 3 else 4 * (b - 1) + (3 if g == 0 else g)
                            pe.wait_ge(s["new_out"], 4 * (prev + 1))
                        for a in range(4):
                            t = 4 * g + a
                            m = mm(e.bank[bank][:, 128 * a:128 * a + 128], z.xd[0:TSA, 128 * t:128 * t + 128],
                                   bmk[:, 128 * g:128 * g + 128], start=True, stop=True)
                        m.then_inc(s["new_ready"], 1)

            @block.scalar
            def _(act):
                for b in range(NB):
                    for f in (1, 3):
                        act.wait_ge(s["turned"], 4 * b + f + 1)
                        if b:
                            act.wait_ge(s["yoff_ready"], b)
                        nc.scalar.activation(s0t[:, 4 * f:4 * f + 4, :], e.bank[f][:].rearrange("p (a l) -> p a l", a=4), ACT.Copy).then_inc(s["turn_out_s"], 1)
                    act.wait_ge(s["yoff_ready"], b + 1)
                    nc.scalar.activation(z.yoff[:, :, TS * b:TS * b + TS], e.bank[4][:, 0:128].rearrange("p (t l) -> p t l", t=KC),
                                         ACT.Copy).then_inc(s["yoff_out"], 1)

            @block.vector
            def _(dve):
                v = nc.vector
                for b in range(NB):
                    if b:
                        dve.wait_ge(s["new_ready"], 4 * b)
                    v.tensor_scalar(bmk[:], z.btok[0:TSA, :], e.const[0:TSA, C_BM + b:C_BM + b + 1], None, ALU.mult).then_inc(s["b_masked"], 1)
                    for f in (0, 2):
                        dve.wait_ge(s["turned"], 4 * b + f + 1)
                        if b:
                            dve.wait_ge(s["yoff_ready"], b)
                        v.tensor_copy(s0t[:, 4 * f:4 * f + 4, :], e.bank[f][:].rearrange("p (a l) -> p a l", a=4)).then_inc(s["turn_out_v"], 1)
                    for g in range(GROUPS):
                        dve.wait_ge(s["new_ready"], 4 * b + g + 1)
                        for a in range(4):
                            t = 4 * g + a
                            x = s0[b % 2][:, t, :]
                            v.scalar_tensor_tensor(x, x, z.etot_hp[:, t, b:b + 1], e.bank[5 + g % 3][:, 128 * a:128 * a + 128],
                                                   ALU.mult, ALU.add).then_inc(s["new_out"], 1)


def prompt_state_out(e, z):
    nc, d = e.nc, e.d
    with ExitStack() as ctx:
        s = ctx.enter_context(stage(nc, "pstate", ["turned", "evac_v", "evac_s", "stored"]))
        out = ctx.enter_context(nc.sbuf_tensor("pstate_rows", [128, KC, 128], F32))
        fills = [([(128 * a, z.st[:, 128 * (4 * f + a):128 * (4 * f + a) + 128], 128, 128) for a in range(4)], 128, 512,
                  out[:, 4 * f:4 * f + 4, :]) for f in range(4)]
        tensor, copies = transposes(e, s, fills)
        with nc.Block() as block:
            block.tensor(tensor)
            block.vector(lambda eng: copies(eng, 0))
            block.scalar(lambda eng: copies(eng, 1))

            @block.gpsimd
            def _(pool):
                pool.wait_ge(s["evac_v"], 2)
                pool.wait_ge(s["evac_s"], 2)
                pool.dma_start(d["ssm_prompt_o"][0, 0].rearrange("h p n -> (h p) n").rearrange("(t q) n -> q t n", q=128),
                               out[:]).then_inc(s["stored"], 16)
                pool.wait_ge(s["stored"], 16)


def gated_group_norm(e, dst):
    nc = e.nc
    with ExitStack() as ctx:
        s = ctx.enter_context(stage(nc, "gnorm", ["gated", "squared", "summed", "var", "std", "rstd", "normed", "hi", "lo_v", "lo_p"]))
        sq = ctx.enter_context(nc.sbuf_tensor("group_sq", [128, 4, T], F32))
        r = ctx.enter_context(nc.sbuf_tensor("group_r", [128, GROUPS, T], F32))
        with nc.Block() as block:
            def low(eng, q, c, sem):
                eng.wait_ge(s["hi"], c + 1)
                q.tensor_tensor(dst[1][:, c, :], e.xbc[:, c, :], dst[0][:, c, :].bitcast(F32), ALU.subtract).then_inc(s[sem], 1)

            @block.vector
            def _(dve):
                v = nc.vector
                for c in range(KC):
                    v.tensor_tensor(e.xbc[:, c, :], e.xbc[:, c, :], e.zs[:, c, :], ALU.mult).then_inc(s["gated"], 1)
                for g in range(GROUPS):
                    dve.wait_ge(s["summed"], g + 1)
                    v.tensor_scalar(r[:, g, :], e.bank[g][:, 0:T], 1.0 / 512, EPS, ALU.mult, ALU.add).then_inc(s["var"], 1)
                for g in range(GROUPS):
                    dve.wait_ge(s["std"], g + 1)
                    v.reciprocal(r[:, g, :], r[:, g, :]).then_inc(s["rstd"], 1)
                for c in range(KC):
                    dve.wait_ge(s["rstd"], c // 4 + 1)
                    y = e.xbc[:, c, :]
                    v.scalar_tensor_tensor(y, y, e.va[:, VA_EV + c:VA_EV + c + 1], r[:, c // 4, :], ALU.mult, ALU.mult).then_inc(s["normed"], 1)
                    if c >= 2 and c % 2 == 0:
                        low(dve, v, c - 2, "lo_v")
                low(dve, v, KC - 2, "lo_v")

            @block.gpsimd
            def _(pool):
                for c in range(1, KC, 2):
                    low(pool, nc.gpsimd, c, "lo_p")

            @block.scalar
            def _(act):
                for c in range(KC):
                    act.wait_ge(s["gated"], c + 1)
                    if c >= 4:
                        act.wait_ge(s["summed"], c // 4)
                    nc.scalar.activation(sq[:, c % 4, :], e.xbc[:, c, :], ACT.Square).then_inc(s["squared"], 1)
                for g in range(GROUPS):
                    act.wait_ge(s["var"], g + 1)
                    nc.scalar.activation(r[:, g, :], r[:, g, :], ACT.Sqrt).then_inc(s["std"], 1)
                for c in range(KC):
                    act.wait_ge(s["normed"], c + 1)
                    nc.scalar.activation(dst[0][:, c, :], e.xbc[:, c, :], ACT.Copy).then_inc(s["hi"], 1)

            @block.tensor
            def _(pe):
                for c in range(KC):
                    pe.wait_ge(s["squared"], c + 1)
                    m = nc.tensor.matmul(e.bank[c // 4][:, 0:T], e.ones, sq[:, c % 4, :], start=c % 4 == 0, stop=c % 4 == 3)
                    if c % 4 == 3:
                        m.then_inc(s["summed"], 1)


class Scan:
    pass


def ssd(e):
    with ExitStack() as ctx:
        sb = lambda n, sh: ctx.enter_context(e.nc.sbuf_tensor(n, sh, F32))
        z = Scan()
        z.a, z.acs, z.dec, z.etot = [sb(f"scan_{n}", [128, 3, SSD_HEADS]) for n in ("a", "acs", "dec", "etot")]
        z.acst, z.eacst = sb("scan_acst", [32, T]), sb("scan_eacst", [32, T])
        z.dhp, z.etot_hp = sb("scan_dhp", [128, KC]), sb("scan_etot_hp", [128, KC, NB])
        z.xr, z.st = sb("scan_xr", [128, D]), sb("scan_state", [128, D])
        z.selhp = sb("selhp", [32, 2048])
        z.xd, z.btok = sb("scan_xd", [128, D]), sb("scan_btok", [128, 512])
        ssd_steps(e, z)
        for u in range(2):
            unit_tokens(e, z, u)
            unit_groups(e, z, u)
        prompt_state_out(e, z)
        unit_tokens(e, z, 2)
        z.yoff = sb("scan_yoff", [128, KC, TSA])
        sample_states(e, z)
        unit_groups(e, z, 2)


def add_projection(e, p, x, nxt=None):
    nc = e.nc
    with nc.Block() as block:
        @block.sync
        def _(sp):
            p.later_loads(sp)
            if nxt:
                nxt.first_loads(sp)

        @block.tensor
        def _(pe):
            p.matmuls(pe, lambda k: (x[0][:, k, :], x[1][:, k, :]))

        @block.gpsimd
        def _(pool):
            p.low(pool)

        @block.scalar
        def _(act):
            p.first_highs(act)
            p.act_loop(act, lambda i, j: None)

        @block.vector
        def _(dve):
            p.take_over(dve)

            def body(i):
                for j in range(NSLOT * p.tps):
                    p.wait_tile(dve, i, j)
                    y = e.xt[:, ds(NSLOT * p.tps * i + j, 1), :]
                    nc.vector.tensor_tensor(y, y, e.bank[j % NSLOT][:, 0:T].unsqueeze(1), ALU.add).then_inc(e.bank_free, 1)
            p.loop(dve, body)
    nc.all_engine_barrier()


def prompt_attention(e, label, heads, qt, kt, v, gated, bias=None):
    nc = e.nc
    with ExitStack() as ctx:
        s = ctx.enter_context(stage(nc, label, ["scores", "biased", "negmax", "exped", "recips", "probs", "turned",
                                                "turn_out", "out_ready", "out"]))
        sb = lambda n, sh: [ctx.enter_context(nc.sbuf_tensor(f"{label}_{n}{i}", sh, F32)) for i in range(2)]
        p, pt = sb("p", [128, 2, TP]), sb("pt", [128, 2, TP])
        nm, den, rec = sb("negmax", [128, 2]), sb("den", [128, 2]), sb("rec", [128, 2])
        sc = lambda u: e.bank[u % 2][:].rearrange("p (r k) -> p r k", r=2)
        with nc.Block() as block:
            @block.tensor
            def _(pe):
                mm = nc.tensor.matmul
                for u in range(heads + 2):
                    if u < heads:
                        if u >= 2:
                            if bias:
                                pe.wait_ge(s["biased"], u - 1)
                            else:
                                pe.wait_ge(s["exped"], 2 * (u - 1))
                        for r in range(2):
                            m = mm(sc(u)[:, r, :], qt(u)[:, 128 * r:128 * r + 128], kt(u), start=True, stop=True)
                        m.then_inc(s["scores"], 1)
                    if 1 <= u <= heads:
                        w = u - 1
                        pe.wait_ge(s["probs"], 2 * (w + 1))
                        if w >= 2:
                            pe.wait_ge(s["turn_out"], w - 1)
                        for k in range(2):
                            for r in range(2):
                                m = nc.tensor.transpose(e.bank[2 + w % 2][:, 128 * (2 * k + r):128 * (2 * k + r) + 128],
                                                        p[w % 2][:, r, 128 * k:128 * k + 128], e.ident)
                        m.then_inc(s["turned"], 1)
                    if u >= 2:
                        w = u - 2
                        pe.wait_ge(s["turn_out"], w + 1)
                        if w >= 2:
                            pe.wait_ge(s["out"], w - 1)
                        for k in range(2):
                            m = mm(e.bank[4 + w % 2][:, 0:TP], v(w, k), pt[w % 2][:, k, :], start=k == 0, stop=k == 1)
                        m.then_inc(s["out_ready"], 1)

            @block.scalar
            def _(act):
                for u in range(heads + 1):
                    if u < heads:
                        act.wait_ge(s["negmax"], u + 1)
                        if u >= 2:
                            act.wait_ge(s["recips"], u - 1)
                            act.wait_ge(s["turned"], u - 1)
                        for r in range(2):
                            src = p[u % 2][:, r, :] if bias else sc(u)[:, r, :]
                            nc.scalar.activation(p[u % 2][:, r, :], src, ACT.Exp, bias=nm[u % 2][:, r:r + 1],
                                                 accum_out=den[u % 2][:, r:r + 1]).then_inc(s["exped"], 1)
                    if u >= 1:
                        w = u - 1
                        act.wait_ge(s["turned"], w + 1)
                        if w >= 2:
                            act.wait_ge(s["out_ready"], w - 1)
                        nc.scalar.activation(pt[w % 2][:].rearrange("p k q -> p (k q)"), e.bank[2 + w % 2][:], ACT.Copy).then_inc(s["turn_out"], 1)

            @block.vector
            def _(dve):
                v_ = nc.vector
                for u in range(heads + 2):
                    if u < heads:
                        dve.wait_ge(s["scores"], u + 1)
                        src = sc(u)
                        if bias:
                            table, slope = bias(u)
                            if u >= 2:
                                dve.wait_ge(s["turned"], u - 1)
                            v_.scalar_tensor_tensor(p[u % 2][:], table, slope, sc(u), ALU.mult, ALU.add).then_inc(s["biased"], 1)
                            dve.wait_ge(s["biased"], u + 1)
                            src = p[u % 2][:]
                        if u >= 2:
                            dve.wait_ge(s["exped"], 2 * (u - 1))
                        v_.tensor_reduce(nm[u % 2][:], src, AX.X, ALU.max, negate=True).then_inc(s["negmax"], 1)
                    if 1 <= u <= heads:
                        w = u - 1
                        dve.wait_ge(s["exped"], 2 * (w + 1))
                        v_.reciprocal(rec[w % 2][:], den[w % 2][:]).then_inc(s["recips"], 1)
                        dve.wait_ge(s["recips"], w + 1)
                        for r in range(2):
                            x = p[w % 2][:, r, :]
                            v_.tensor_scalar(x, x, rec[w % 2][:, r:r + 1], None, ALU.mult).then_inc(s["probs"], 1)
                    if u >= 2:
                        w = u - 2
                        dve.wait_ge(s["out_ready"], w + 1)
                        v_.tensor_tensor(gated(w), gated(w), e.bank[4 + w % 2][:, 0:TP], ALU.mult).then_inc(s["out"], 1)


def cross_sample(e, layer, qt, gt, kr, vr):
    nc, d = e.nc, e.d
    L = f"xs{layer}"
    with ExitStack() as ctx:
        s = ctx.enter_context(stage(nc, L, ["mask_in", "v_in", "masked", "turned", "kt_v", "kt_s",
                                            "scores", "negmax", "exped", "recips", "probs", "p_turned", "p_out", "used",
                                            "out_ready", "out"]))
        sb = lambda n, sh: ctx.enter_context(nc.sbuf_tensor(f"{L}_{n}", sh, F32))
        mask = sb("mask", [128, NB, TSA])
        vr = [*vr, *[sb(f"vrows{i}", [128, 2, 512]) for i in range(len(vr), NB)]]
        kt = [sb(f"kt{i}", [128, CAH, NM]) for i in range(2)]
        qm = [sb(f"qm{i}", [128, CAH, TSA]) for i in range(2)]
        p, pt = sb("p", [128, 2, NM]), sb("pt", [128, 2, 2, 128])
        nm, den, rec = sb("negmax", [128, 2]), sb("den", [128, 2]), sb("rec", [128, 2])
        rows = lambda a: a.rearrange("(t p) h n -> p t (h n)", p=128)
        with nc.Block() as block:
            @block.sync
            def _(sp):
                sp.dma_start(mask[:], d["c_qmask"].rearrange("p (b t) -> p b t", b=NB)).then_inc(s["mask_in"], 16)
                for b in range(CROSS_V_AHEAD, NB):
                    sp.dma_start(vr[b][:], rows(d["cache_mem_v"][layer, b])).then_inc(s["v_in"], 16)

            @block.tensor
            def _(pe):
                mm = nc.tensor.matmul
                pe.wait_ge(e.cross_in, e.cross_loads(layer))
                for b in range(NB + 1):
                    if b < NB:
                        for t in range(2):
                            if b:
                                pe.wait_ge(s["kt_s" if t else "kt_v"], b)
                            for h in range(CAH):
                                m = nc.tensor.transpose(e.bank[t][:, 128 * h:128 * h + 128], kr[b][:, t, 128 * h:128 * h + 128], e.ident)
                            m.then_inc(s["turned"], 1)
                    if b:
                        c = b - 1
                        pe.wait_ge(s["kt_v"], b)
                        pe.wait_ge(s["kt_s"], b)
                        pe.wait_ge(s["masked"], b)
                        for h in range(CAH):
                            p0 = 64 * (h % 2)
                            m = mm(e.bank[2 + h // 2][p0:p0 + 64, 0:NM], qm[c % 2][:, h, :], kt[c % 2][:, h, :],
                                   start=c == 0, stop=c == NB - 1)
                        m.then_inc(s["scores"], 1)
                pe.wait_ge(s["probs"], 2)
                for t in range(2):
                    for r in range(2):
                        m = nc.tensor.transpose(e.bank[4][:, 128 * (2 * t + r):128 * (2 * t + r) + 128], p[:, r, 128 * t:128 * t + 128], e.ident)
                m.then_inc(s["p_turned"], 1)
                pe.wait_ge(s["p_out"], 1)
                for b in range(NB):
                    if b == CROSS_V_AHEAD:
                        pe.wait_ge(s["v_in"], 16 * (NB - CROSS_V_AHEAD))
                    for h in range(CAH):
                        c0 = 64 * (h % 2) + TS * b
                        for t in range(2):
                            m = mm(e.bank[5][:, TSA * h + TS * b:TSA * h + TS * b + TS], vr[b][:, t, 128 * h:128 * h + 128],
                                   pt[:, t, h // 2, c0:c0 + TS], start=t == 0, stop=t == 1)
                    m.then_inc(s["used"], 1)

            @block.scalar
            def _(act):
                for b in range(NB):
                    act.wait_ge(s["turned"], 2 * b + 2)
                    if b >= 2:
                        act.wait_ge(s["scores"], b - 1)
                    nc.scalar.activation(kt[b % 2][:, :, 128:256], e.bank[1][:].rearrange("p (h m) -> p h m", h=CAH), ACT.Copy).then_inc(s["kt_s"], 1)
                act.wait_ge(s["negmax"], 2)
                for r in range(2):
                    nc.scalar.activation(p[:, r, :], e.bank[2 + r][:, 0:NM], ACT.Exp, bias=nm[:, r:r + 1],
                                         accum_out=den[:, r:r + 1]).then_inc(s["exped"], 1)
                act.wait_ge(s["p_turned"], 1)
                nc.scalar.activation(pt[:].rearrange("p t r q -> p (t r q)"), e.bank[4][:], ACT.Copy).then_inc(s["p_out"], 1)

            @block.vector
            def _(dve):
                v = nc.vector
                dve.wait_ge(s["mask_in"], 16)
                for b in range(NB):
                    if b >= 2:
                        dve.wait_ge(s["scores"], b - 1)
                    v.tensor_tensor(qm[b % 2][:], qt[:, :, TP:T], mask[:, b:b + 1, :].to_broadcast([128, CAH, TSA]), ALU.mult).then_inc(s["masked"], 1)
                    dve.wait_ge(s["turned"], 2 * b + 1)
                    v.tensor_copy(kt[b % 2][:, :, 0:128], e.bank[0][:].rearrange("p (h m) -> p h m", h=CAH)).then_inc(s["kt_v"], 1)
                dve.wait_ge(s["scores"], NB)
                for r in range(2):
                    v.tensor_reduce(nm[:, r:r + 1], e.bank[2 + r][:, 0:NM], AX.X, ALU.max, negate=True).then_inc(s["negmax"], 1)
                dve.wait_ge(s["exped"], 2)
                v.reciprocal(rec[:], den[:]).then_inc(s["recips"], 1)
                dve.wait_ge(s["recips"], 1)
                for r in range(2):
                    v.tensor_scalar(p[:, r, :], p[:, r, :], rec[:, r:r + 1], None, ALU.mult).then_inc(s["probs"], 1)
                dve.wait_ge(s["used"], NB)
                v.tensor_tensor(gt[:, :, TP:T], gt[:, :, TP:T], e.bank[5][:, 0:CAH * TSA].rearrange("p (h q) -> p h q", h=CAH),
                                ALU.mult).then_inc(s["out"], 1)


def cross_attention(e, layer, p_q, p_out, nxt):
    nc, d = e.nc, e.d
    rows = lambda a: a.rearrange("(t p) h n -> p t (h n)", p=128)
    with ExitStack() as ctx:
        sb = lambda n, sh: ctx.enter_context(nc.sbuf_tensor(f"x{layer}_{n}", sh, F32))
        qt, gt = sb("q", [128, CAH, T]), sb("g", [128, CAH, T])
        with ExitStack() as c2:
            sb2 = lambda n, sh: c2.enter_context(nc.sbuf_tensor(f"x{layer}_{n}", sh, F32))
            km, vm = sb2("km", [128, CAH, NM]), sb2("vm", [128, 2, 512])
            kr = [sb2(f"krows{i}", [128, 2, 512]) for i in range(NB)]
            vr = [sb2(f"vrows{i}", [128, 2, 512]) for i in range(CROSS_V_AHEAD)]
            kmr = vr[-1]
            with ExitStack() as c3:
                x = c3.enter_context(split_buffers(e, f"xq{layer}", KC))
                rmsnorm(e, f"norm_cross{layer}", VA_CROSS + KC * layer, x)
                s = c3.enter_context(stage(nc, f"xproj{layer}", ["turned", "km_v"]))
                with nc.Block() as block:
                    @block.sync
                    def _(sp):
                        sp.dma_start(kmr[:], rows(d["mem_k_o"][layer, 0])).then_inc(e.cross_in, 16)
                        sp.dma_start(vm[:], rows(d["mem_v_o"][layer, 0])).then_inc(e.cross_in, 16)
                        p_q.later_loads(sp)
                        for b in range(NB):
                            sp.dma_start(kr[b][:], rows(d["cache_mem_k"][layer, b])).then_inc(e.cross_in, 16)
                            if b < CROSS_V_AHEAD - 1:
                                sp.dma_start(vr[b][:], rows(d["cache_mem_v"][layer, b])).then_inc(e.cross_in, 16)
                        sp.wait_ge(s["turned"], 2)
                        sp.dma_start(kmr[:], rows(d["cache_mem_v"][layer, CROSS_V_AHEAD - 1])).then_inc(e.cross_in, 16)
                        p_out.first_loads(sp)

                    @block.tensor
                    def _(pe):
                        pe.wait_ge(e.cross_in, e.cross_loads(layer - 1) + 32)
                        for t in range(2):
                            for h in range(CAH):
                                m = nc.tensor.transpose(e.bank[4 + t][:, 128 * h:128 * h + 128], kmr[:, t, 128 * h:128 * h + 128], e.ident)
                            m.then_inc(s["turned"], 1)
                        p_q.matmuls(pe, lambda k: (x[0][:, k, :], x[1][:, k, :]))

                    @block.gpsimd
                    def _(pool):
                        p_q.low(pool)

                    @block.vector
                    def _(dve):
                        for t in range(2):
                            dve.wait_ge(s["turned"], t + 1)
                            nc.vector.tensor_copy(km[:, :, 128 * t:128 * t + 128], e.bank[4 + t][:].rearrange("p (h m) -> p h m", h=CAH)).then_inc(s["km_v"], 1)

                    @block.scalar
                    def _(act):
                        def query(i, j):
                            p_q.wait_tile(act, i, j)
                            nc.scalar.activation(qt[:, j, :], e.bank[j][:, 0:T], ACT.Copy, scale=QSCALE).then_inc(e.bank_free, 1)

                        def gate(i, j):
                            p_q.wait_tile(act, i, j)
                            nc.scalar.activation(gt[:, j, :], e.bank[j][:, 0:T], ACT.Silu).then_inc(e.bank_free, 1)

                        p_q.take_over(act)
                        p_q.first_highs(act)
                        for i in range(2):
                            for j in range(NSLOT):
                                (gate if i else query)(i, j)
                                if i == 0 or j < NSPLIT:
                                    p_q.high(act, i, j + NSPLIT)
            prompt_attention(e, f"xp{layer}", CAH, lambda h: qt[:, h, 0:TP], lambda h: km[:, h, :],
                             lambda h, m: vm[:, m, 128 * h:128 * h + 128], lambda h: gt[:, h, 0:TP])
            cross_sample(e, layer, qt, gt, kr, vr)
        x = ctx.enter_context(split_buffers(e, f"xo{layer}", CAH))
        split_input(e, f"xsplit{layer}", lambda k: gt[:, k:k + 2, :], x, CAH)
        add_projection(e, p_out, x, nxt)


def moba_sample(e, qt, kt_new, v_new, gt, nxt):
    nc, d = e.nc, e.d
    names = ["zeroed", "tables_in", "pages_in", "q_ready", "k_turned", "kt_v", "kt_s", "scores", "own_scores", "step", "biases",
             "exped", "recips", "p_turned", "pt_v", "pt_s", "v_used", "o_ready", "o_rows", "o_turned", "o_out"]
    KRING, QUAD = 8, 4
    HALF = NPG // 2
    names += [f"k_in{i}" for i in range(KRING // QUAD)] + [f"v_in{i}" for i in range(NPG // QUAD)]
    with ExitStack() as ctx:
        s = ctx.enter_context(stage(nc, "ms", names))
        sb = lambda n, sh, dt=F32: ctx.enter_context(nc.sbuf_tensor(f"ms_{n}", sh, dt))
        pages = sb("pages", [1, NB * NPG], I32)
        past, own = sb("past", [128, PAST]), sb("own", [128, NB, TSA])
        krows, vrows = sb("krows", [128, KRING, 512]), e.w[:].rearrange("p j (g c) -> p (j g) c", c=512)
        kt = sb("kt", [128, KVH, PAST])
        qb = sb("q", [128, AH, TS])
        gate, rank, drop = sb("gate", [128, NBLK]), sb("rank", [128, NBLK]), sb("drop", [128, NBLK + 1])
        top, dropped, bias, den = [sb(n, [128, NBLK + 1]) for n in ("top", "dropped", "bias", "den")]
        orows = sb("orows", [128, DH])
        above, tied = sb("above", [128, NBLK, NBLK]), sb("tied", [128, NBLK, NBLK])
        nm, den1, rec = sb("negmax", [128, 1]), sb("den_sum", [128, 1]), sb("rec", [128, 1])
        NP = PAST + TSA
        p, pt = sb("p", [128, NP]), sb("pt", [128, (NPG + 1) * 128])
        STEPS = 25
        with nc.Block() as block:
            @block.sync
            def _(sp):
                sp.dma_start(pages[:], d["page_table"].rearrange("b n -> (b n)").unsqueeze(0)).then_inc(s["pages_in"], 16)
                sp.dma_start(past[:], d["c_past"]).then_inc(s["tables_in"], 16)
                sp.dma_start(own[:], d["c_own"].rearrange("p (b t) -> p b t", b=NB)).then_inc(s["tables_in"], 16)
                sp.wait_ge(s["pages_in"], 16)
                ksrc = d["cache_k"][0].rearrange("n t h c -> n t (h c)")

                def keys(b, g):
                    page = sp.value_load(pages[0:1, ds(b * NPG + g, 1)], min_val=0, max_val=ksrc.shape[0] - 1)
                    sp.wait_ge(s["k_turned"], b * NPG + (g + 1))
                    sp.dma_start(krows[:, g % KRING:g % KRING + 1, :], ksrc[ds(page, 1)].rearrange("n t c -> t n c")
                                 ).then_inc(s[f"k_in{g // QUAD % 2}"], 16)

                def batch(b, last):
                    for g in range(HALF, NPG):
                        keys(b, g)
                    if not last:
                        for g in range(HALF):
                            keys(b + 1, g)

                for g in range(HALF):
                    keys(0, g)
                with sp.Fori(0, NB - 1) as b:
                    batch(b, False)
                batch(NB - 1, True)
                sp.wait_ge(s["v_used"], NPG + NB * NPG)
                nxt.first_loads(sp)

            @block.gpsimd
            def _(pool):
                pool.wait_ge(s["pages_in"], 16)
                vsrc = d["cache_v"][0].rearrange("n t h c -> n t (h c)")
                with pool.Fori(0, NB) as b:
                    for g in range(NPG):
                        page = pool.value_load(pages[0:1, ds(b * NPG + g, 1)], min_val=0, max_val=vsrc.shape[0] - 1)
                        pool.wait_ge(s["v_used"], b * NPG + (g + 1))
                        pool.dma_start(vrows[:, g:g + 1, :], vsrc[ds(page, 1)].rearrange("n t c -> t n c")
                                       ).then_inc(s[f"v_in{g // QUAD}"], 16)

            @block.tensor
            def _(pe):
                mm = nc.tensor.matmul
                pe.sem_inc(s["k_turned"], KRING)
                pe.sem_inc(s["v_used"], NPG)

                def turn(b, g):
                    if g % QUAD == 0:
                        pe.wait_ge(s[f"k_in{g // QUAD % 2}"], b * 128 + 64 * (g // KRING + 1))
                    if g >= 2 or not isinstance(b, int):
                        if g == 0:
                            pe.wait_ge(s["kt_v"], b * 4)
                        elif g >= 10 and g % 2 == 0:
                            pe.wait_ge(s["kt_v"], b * 4 + (g - 8) // 2)
                        else:
                            pe.wait_ge(s["kt_s"], b * 12 + (g - 1 if g < 10 else 8 + (g - 9) // 2))
                    for h in range(KVH):
                        m = nc.tensor.transpose(e.bank[g % 2][:, 128 * h:128 * h + 128], krows[:, g % KRING, 128 * h:128 * h + 128], e.ident)
                    m.then_inc(s["k_turned"], 1)

                def scores(b, q):
                    if q < 2:
                        pe.wait_ge(s["kt_s"], b * 12 + 4 * (q + 1))
                    else:
                        pe.wait_ge(s["kt_v"], b * 4 + 2 * (q - 1))
                        pe.wait_ge(s["kt_s"], b * 12 + (8 + 2 * (q - 1)))
                    for h in range(KVH):
                        m = mm(e.bank[4 + q][32 * h:32 * h + 32, :], qb[:, 4 * h:4 * h + 4, :].rearrange("p g t -> p (g t)"),
                               kt[:, h, 512 * q:512 * q + 512], start=True, stop=True)
                    m.then_inc(s["scores"], 1)

                def batch(b, last):
                    pe.wait_ge(s["q_ready"], b + 1)
                    scores(b, 0)
                    scores(b, 1)
                    for g in range(HALF, NPG):
                        turn(b, g)
                        if g % QUAD == QUAD - 1:
                            scores(b, g // QUAD)
                    for h in range(KVH):
                        m = mm(e.bank[2][32 * h:32 * h + 32, 0:TSA], qb[:, 4 * h:4 * h + 4, :].rearrange("p g t -> p (g t)"),
                               kt_new[:, h, TP:T], start=True, stop=True)
                    m.then_inc(s["own_scores"], 1)
                    if not last:
                        for g in range(HALF):
                            turn(b + 1, g)
                    for f in range(4):
                        pe.wait_ge(s["exped"], b * 9 + (2 * f + 3))
                        for a in range(4):
                            m = nc.tensor.transpose(e.bank[4 + f][:, 128 * a:128 * a + 128], p[:, 512 * f + 128 * a:512 * f + 128 * a + 128], e.ident)
                        m.then_inc(s["p_turned"], 1)
                        if f == 0:
                            nc.tensor.transpose(e.bank[3][0:TSA, 0:128], p[:, PAST:NP], e.ident).then_inc(s["p_turned"], 1)
                    for g in range(NPG):
                        if g % QUAD == 0:
                            f = g // QUAD
                            if f < 3:
                                pe.wait_ge(s["pt_v"], b * 4 + (f + 2 if f else 1))
                            else:
                                pe.wait_ge(s["pt_s"], b + 1)
                            pe.wait_ge(s[f"v_in{f}"], b * 64 + 64)
                        for h in range(KVH):
                            m = mm(e.bank[2][32 * h:32 * h + 32, 128:256], pt[:, 128 * g + 32 * h:128 * g + 32 * h + 32],
                                   vrows[:, g, 128 * h:128 * h + 128], start=g == 0, stop=False, skip_group_check=True)
                        m.then_inc(s["v_used"], 1)
                    for h in range(KVH):
                        m = mm(e.bank[2][32 * h:32 * h + 32, 128:256], pt[0:TSA, 128 * NPG + 32 * h:128 * NPG + 32 * h + 32],
                               v_new[0:TSA, 128 * h:128 * h + 128], start=False, stop=True, skip_group_check=True)
                    m.then_inc(s["o_ready"], 1)
                    pe.wait_ge(s["o_rows"], b + 1)
                    nc.tensor.transpose(e.bank[3][:, 128:256], orows[:], e.ident).then_inc(s["o_turned"], 1)

                for g in range(HALF):
                    turn(0, g)
                with pe.Fori(0, NB - 1) as b:
                    batch(b, False)
                batch(NB - 1, True)

            @block.scalar
            def _(act):
                def evacuate(b, g):
                    act.wait_ge(s["k_turned"], b * NPG + (g + 1 + KRING))
                    nc.scalar.activation(kt[:, :, 128 * g:128 * g + 128], e.bank[g % 2][:].rearrange("p (h t) -> p h t", h=KVH),
                                         ACT.Copy).then_inc(s["kt_s"], 1)

                def batch(b, last):
                    for g in range(HALF + 1, NPG, 2):
                        evacuate(b, g)
                    if not last:
                        for g in range(HALF):
                            evacuate(b + 1, g)
                    act.wait_ge(s["biases"], b + 1)
                    for k in (NBLK, *range(NBLK)):
                        x = p[:, BLK * k:BLK * k + (BLK if k < NBLK else TSA)]
                        nc.scalar.activation(x, x, ACT.Exp, bias=bias[:, k:k + 1], accum_out=den[:, k:k + 1]).then_inc(s["exped"], 1)
                    act.wait_ge(s["p_turned"], b * 5 + 5)
                    nc.scalar.activation(pt[:, 1536:2048], e.bank[7][:], ACT.Copy).then_inc(s["pt_s"], 1)

                for g in range(HALF):
                    evacuate(0, g)
                with act.Fori(0, NB - 1) as b:
                    batch(b, False)
                batch(NB - 1, True)

            @block.vector
            def _(dve):
                v = nc.vector

                def batch(b, last):
                    n = [0]

                    def step(ins):
                        ins.then_inc(s["step"], 1)
                        n[0] += 1

                    def settled():
                        dve.wait_ge(s["step"], b * STEPS + n[0])

                    def past_scores(q):
                        dve.wait_ge(s["scores"], b * 4 + (q + 1))
                        step(v.tensor_reduce(gate[:, 2 * q:2 * q + 2], e.bank[4 + q][:].rearrange("p (a k) -> p a k", a=2), AX.X, ALU.add))
                        step(v.tensor_tensor(p[:, 512 * q:512 * q + 512], e.bank[4 + q][:], past[:, 512 * q:512 * q + 512], ALU.add))
                        settled()
                        step(v.tensor_reduce(top[:, 2 * q:2 * q + 2], p[:, 512 * q:512 * q + 512].rearrange("p (a k) -> p a k", a=2), AX.X, ALU.max))

                    def evacuate(g):
                        dve.wait_ge(s["k_turned"], b * NPG + (g + 1 + KRING))
                        v.tensor_copy(kt[:, :, 128 * g:128 * g + 128], e.bank[g % 2][:].rearrange("p (h t) -> p h t", h=KVH)).then_inc(s["kt_v"], 1)

                    past_scores(0)
                    evacuate(8)
                    past_scores(1)
                    evacuate(10)
                    evacuate(12)
                    past_scores(2)
                    evacuate(14)
                    past_scores(3)
                    dve.wait_ge(s["own_scores"], b + 1)
                    step(v.tensor_tensor(p[:, PAST:NP].unsqueeze(1), e.bank[2][:, 0:TSA].unsqueeze(1), own[:, ds(b, 1), :], ALU.add))
                    settled()
                    step(v.tensor_reduce(top[:, NBLK:NBLK + 1], p[:, PAST:NP], AX.X, ALU.max))
                    gi = gate[:].unsqueeze(1).to_broadcast([128, NBLK, NBLK])
                    gj = gate[:].unsqueeze(2).to_broadcast([128, NBLK, NBLK])
                    step(v.tensor_tensor(above[:], gi, gj, ALU.is_gt))
                    step(v.tensor_tensor(tied[:], gi, gj, ALU.is_equal))
                    settled()
                    step(v.tensor_tensor(tied[:], tied[:], e.const[:, C_TIE:C_TIE + 64].rearrange("p (j i) -> p j i", j=NBLK), ALU.mult))
                    settled()
                    step(v.tensor_tensor(above[:], above[:], tied[:], ALU.add))
                    settled()
                    step(v.tensor_reduce(rank[:], above[:], AX.X, ALU.add))
                    settled()
                    step(v.tensor_scalar(drop[:, 0:NBLK], rank[:], TOPK - 0.5, NEG, ALU.is_gt, ALU.mult))
                    settled()
                    step(v.tensor_scalar(rank[:], gate[:], 0.5 * NEG * BLK, NEG, ALU.is_le, ALU.mult))
                    settled()
                    step(v.tensor_tensor(drop[:, 0:NBLK], drop[:, 0:NBLK], rank[:], ALU.add))
                    settled()
                    step(v.tensor_tensor(dropped[:], top[:], drop[:], ALU.add))
                    settled()
                    step(v.tensor_reduce(nm[:], dropped[:], AX.X, ALU.max, negate=True))
                    settled()
                    v.tensor_scalar(bias[:], drop[:], nm[:], None, ALU.add).then_inc(s["biases"], 1)
                    for f in range(3):
                        dve.wait_ge(s["p_turned"], b * 5 + (f + 2 if f else 1))
                        v.tensor_copy(pt[:, 512 * f:512 * f + 512], e.bank[4 + f][:]).then_inc(s["pt_v"], 1)
                        if f == 0:
                            dve.wait_ge(s["p_turned"], b * 5 + 2)
                            v.tensor_copy(pt[0:TSA, 128 * NPG:128 * NPG + 128], e.bank[3][0:TSA, 0:128]).then_inc(s["pt_v"], 1)
                    dve.wait_ge(s["exped"], b * 9 + 9)
                    step(v.tensor_reduce(den1[:], den[:], AX.X, ALU.add))
                    settled()
                    v.reciprocal(rec[:], den1[:]).then_inc(s["recips"], 1)
                    if not last:
                        v.tensor_copy(qb[:], qt[:, :, ds(b * TS + (TP + TS), TS)]).then_inc(s["q_ready"], 1)
                    dve.wait_ge(s["recips"], b + 1)
                    dve.wait_ge(s["o_ready"], b + 1)
                    v.tensor_scalar(orows[:], e.bank[2][:, 128:256], rec[:], None, ALU.mult).then_inc(s["o_rows"], 1)
                    dve.wait_ge(s["o_turned"], b + 1)
                    go = gt[:, :, ds(b * TS + TP, TS)]
                    v.tensor_tensor(go, go, e.bank[3][:, 128:256].rearrange("p (h t) -> p h t", h=AH), ALU.mult).then_inc(s["o_out"], 1)
                    assert n[0] == STEPS, n

                v.tensor_copy(qb[:], qt[:, :, TP:TP + TS]).then_inc(s["q_ready"], 1)
                v.memset(drop[:, NBLK:NBLK + 1], 0.0).then_inc(s["zeroed"], 1)
                dve.wait_ge(s["zeroed"], 1)
                dve.wait_ge(s["tables_in"], 32)
                with dve.Fori(0, NB - 1) as b:
                    batch(b, False)
                batch(NB - 1, True)


def moba(e, p_in, p_out, nxt):
    nc, d = e.nc, e.d
    with ExitStack() as ctx:
        sb = lambda n, sh: ctx.enter_context(nc.sbuf_tensor(n, sh, F32))
        qt, kt, gt = sb("m_q", [128, AH, T]), sb("m_k", [128, KVH, T]), sb("m_g", [128, AH, T])
        vrows = sb("m_vrows", [128, 3, 512])
        with ExitStack() as c2:
            vt = c2.enter_context(nc.sbuf_tensor("m_v", [128, KVH, T], F32))
            krows = c2.enter_context(nc.sbuf_tensor("m_krows", [128, 3, 512], F32))
            with split_buffers(e, "odd", KC) as x:
                rmsnorm(e, "norm_mix1", VA_MIX + KC, x)
                with nc.Block() as block:
                    @block.sync
                    def _(sp):
                        p_in.later_loads(sp)

                    @block.tensor
                    def _(pe):
                        p_in.matmuls(pe, lambda k: (x[0][:, k, :], x[1][:, k, :]))

                    @block.gpsimd
                    def _(pool):
                        p_in.low(pool)

                    @block.scalar
                    def _(act):
                        def tile(i, j, dst, func, scale=1.0):
                            p_in.wait_tile(act, i, j)
                            nc.scalar.activation(dst, e.bank[j][:, 0:T].unsqueeze(1), func, scale=scale).then_inc(e.bank_free, 1)
                            if not (isinstance(i, int) and i == p_in.iters - 1 and j >= NSLOT - NSPLIT):
                                p_in.high(act, i, j + NSPLIT)

                        p_in.take_over(act)
                        p_in.first_highs(act)
                        with act.Fori(0, 4) as i:
                            for j in range(4):
                                tile(i, j, qt[:, ds(4 * i + j, 1), :], ACT.Copy, QSCALE)
                        for i, dst in ((4, kt), (5, vt)):
                            for j in range(4):
                                tile(i, j, dst[:, j:j + 1, :], ACT.Copy)
                        with act.Fori(0, 3) as i:
                            for j in range(4):
                                tile(i + 6, j, gt[:, ds(4 * i + j, 1), :], ACT.Silu)
                        for j in range(4):
                            tile(9, j, gt[:, 12 + j:13 + j, :], ACT.Silu)
                nc.all_engine_barrier()
            s = c2.enter_context(stage(nc, "mrows", ["turned", "evac_v", "evac_s", "stored"]))
            fills = []
            for src, dst in ((kt, krows), (vt, vrows)):
                for u in range(3):
                    n = 128 if u < 2 else TSA
                    fills.append(([(128 * h, src[:, h, 128 * u:128 * u + n], 128, n) for h in range(KVH)], n, 512, dst[0:n, u, :]))
            tensor, copies = transposes(e, s, fills)
            with nc.Block() as block:
                block.tensor(tensor)
                block.vector(lambda eng: copies(eng, 0))
                block.scalar(lambda eng: copies(eng, 1))

                @block.gpsimd
                def _(pool):
                    pool.wait_ge(s["evac_v"], 3)
                    pool.wait_ge(s["evac_s"], 3)
                    for n, r in (("k", krows), ("v", vrows)):
                        pool.dma_start(d[f"{n}_prompt_o"][0, 0].rearrange("(t p) h c -> p t (h c)", p=128), r[:, 0:2, :]).then_inc(s["stored"], 16)
                        pool.dma_start(d[f"{n}_sample_o"][0].rearrange("b t h c -> (b t) (h c)"), r[0:TSA, 2, :]).then_inc(s["stored"], 16)
                    pool.wait_ge(s["stored"], 64)
        with ExitStack() as c2:
            dist = c2.enter_context(nc.sbuf_tensor("m_dist", [128, 2, TP], F32))
            s = c2.enter_context(stage(nc, "mdist", ["dist_in"]))
            with nc.Block() as block:
                @block.sync
                def _(sp):
                    sp.dma_start(dist[:], d["c_dist"].rearrange("p (r k) -> p r k", r=2)).then_inc(s["dist_in"], 16)
                    sp.wait_ge(s["dist_in"], 16)
            prompt_attention(e, "mp", AH, lambda h: qt[:, h, 0:TP], lambda h: kt[:, h // G4, 0:TP],
                             lambda h, m: vrows[:, m, 128 * (h // G4):128 * (h // G4) + 128], lambda h: gt[:, h, 0:TP],
                             bias=lambda h: (dist[:], e.const[:, C_SLOPE + h:C_SLOPE + h + 1]))
        moba_sample(e, qt, kt, vrows[:, 2, :], gt, p_out)
        x = ctx.enter_context(split_buffers(e, "odd_out", KC))
        split_input(e, "odd_split", lambda k: gt[:, k:k + 2, :], x, KC)
        add_projection(e, p_out, x, nxt)


def final(e):
    nc, d = e.nc, e.d
    with ExitStack() as ctx:
        s = ctx.enter_context(stage(nc, "final", ["normed", "turned", "evac_v", "evac_s", "stored"]))
        r = ctx.enter_context(nc.sbuf_tensor("final_r", [128, T], F32))
        norm_sums(e, "norm_final", e.xt, T, r)
        rows = ctx.enter_context(nc.sbuf_tensor("y_rows", [128, 3, D], F32))
        fills = []
        for u in range(3):
            n = 128 if u < 2 else TSA
            for c in range(0, KC, 4):
                fills.append(([(128 * a, e.xt[:, c + a, 128 * u:128 * u + n], 128, n) for a in range(4)], n, 512, rows[0:n, u, 128 * c:128 * c + 512]))
        tensor, copies = transposes(e, s, fills)
        with nc.Block() as block:
            @block.tensor
            def _(pe):
                pe.wait_ge(s["normed"], KC)
                tensor(pe)

            @block.vector
            def _(dve):
                for c in range(KC):
                    x = e.xt[:, c, :]
                    nc.vector.scalar_tensor_tensor(x, x, e.va[:, VA_FIN + c:VA_FIN + c + 1], r[:], ALU.mult, ALU.mult).then_inc(s["normed"], 1)
                copies(dve, 0)
            block.scalar(lambda eng: copies(eng, 1))

            @block.sync
            def _(sp):
                for u in range(3):
                    sp.wait_ge(s["evac_v"], 2 * (u + 1))
                    sp.wait_ge(s["evac_s"], 2 * (u + 1))
                    if u < 2:
                        sp.dma_start(d["y_prompt_o"][0, 128 * u:128 * u + 128, :], rows[:, u, :]).then_inc(s["stored"], 16)
                    else:
                        sp.dma_start(d["y_sample_o"].rearrange("b t n -> (b t) n"), rows[0:TSA, u, :]).then_inc(s["stored"], 16)
                sp.wait_ge(s["stored"], 48)


def build(nc, d):
    e = Trunk(nc, d)
    with ExitStack() as ctx:
        sb = lambda n, sh: ctx.enter_context(nc.sbuf_tensor(n, sh, F32))
        e.const = sb("const", [128, C_N])
        e.ident = e.const[:, C_ID:C_ID + 128]
        e.ones = e.const[:, C_ONE:C_ONE + 128]
        e.va, e.vb, e.vc = sb("va", [128, VA_N]), sb("vb", [128, VB_N]), sb("vc", [128, VC_N])
        e.w = sb("w_slots", [128, NSLOT, KC * 128])
        e.xt = sb("xt", [128, KC, T])
        e.bank = [ctx.enter_context(nc.psum_tensor(f"bank{i}", [128, 512], F32)) for i in range(8)]
        sem = lambda n: ctx.enter_context(nc.semaphore(n))
        e.pe_event, e.bank_free, e.w_hi, e.w_lo = [sem(n) for n in ("pe_event", "bank_free", "w_hi", "w_lo")]
        e.cross_in = sem("cross_in")
        e.cross_loads = lambda layer: (layer + 1) * 16 * (2 + NB + CROSS_V_AHEAD)
        e.w_landed = [sem(f"w_landed{j}") for j in range(NSLOT)]

        w_ev = d["ev_w_in"][0]
        p_kv = [Proj(e, columns(d["ca_w_kv"][l]), 8, ntok=NM) for l in range(2)]
        p_z = Proj(e, columns(w_ev, OFF_Z), 16)
        p_xbc = Proj(e, columns(w_ev, OFF_XBC), CCH)
        p_sc = Proj(e, sc_columns(w_ev), 64)
        p_evy, p_evs = [Proj(e, columns(d["ev_w_out"][0][D * i:D * i + D, :]), 16) for i in (1, 0)][::-1]
        p_xq, p_xo = [None, None], [None, None]
        p_xq[0] = Proj(e, columns(d["ca_w_q"][0]), 8)
        p_xo[0] = Proj(e, wide_columns(d["ca_w_out"][0]), 16, kch=CAH, tiles_per_slot=4)
        p_od = Proj(e, columns(d["od_w_in"][0]), 40)
        p_odo = Proj(e, columns(d["od_w_out"][0]), 16)
        p_xq[1] = Proj(e, columns(d["ca_w_q"][1]), 8)
        p_xo[1] = Proj(e, wide_columns(d["ca_w_out"][1]), 16, kch=CAH, tiles_per_slot=4)
        e.next_proj = p_kv[0]
        with ExitStack() as c2:
            e.memt = c2.enter_context(nc.sbuf_tensor("memt", [128, KC, NM], F32))
            setup(e)
            r = c2.enter_context(nc.sbuf_tensor("mem_r", [128, T], F32))
            norm_sums(e, "norm_mem", e.memt, NM, r)
            memory_kv(e, 0, p_kv[0], p_kv[1], r)
            memory_kv(e, 1, p_kv[1], p_z, r)
        with ExitStack() as c2:
            sb2 = lambda n, sh: c2.enter_context(nc.sbuf_tensor(n, sh, F32))
            e.zs, e.xbc = sb2("zs", [128, KC, T]), sb2("xbc", [128, CCH, T])
            e.dt = sb2("dt", [128, 3, SSD_HEADS])
            with nc.sbuf_tensor("ysc", [128, KC, T], F32) as e.ysc:
                even_projections(e, p_z, p_xbc, p_sc, p_evs)
                with split_buffers(e, "sc_out", KC) as x:
                    split_input(e, "sc_split", lambda k: e.ysc[:, k:k + 2, :], x, KC)
                    add_projection(e, p_evs, x, p_evy)
            ssd(e)
            with split_buffers(e, "scan_out", KC) as x:
                gated_group_norm(e, x)
                add_projection(e, p_evy, x, p_xq[0])
        cross_attention(e, 0, p_xq[0], p_xo[0], p_od)
        moba(e, p_od, p_odo, p_xq[1])
        cross_attention(e, 1, p_xq[1], p_xo[1], None)
        final(e)


_OUTS = [("y_prompt_o", (1, TP, D)), ("y_sample_o", (NB, TS, D)),
         ("k_prompt_o", (1, 1, TP, KVH, DH)), ("v_prompt_o", (1, 1, TP, KVH, DH)),
         ("conv_prompt_o", (1, 1, CW - 1, CONV_CH)), ("ssm_prompt_o", (1, 1, SSD_HEADS, HD, NST)),
         ("sc_prompt_o", (1, 1, SCW - 1, D)),
         ("mem_k_o", (2, 1, NM, CAH, DH)), ("mem_v_o", (2, 1, NM, CAH, DH)),
         ("k_sample_o", (1, NB, TS, KVH, DH)), ("v_sample_o", (1, NB, TS, KVH, DH)),
         ("conv_sample_o", (1, NB, CW - 1, CONV_CH)), ("ssm_sample_o", (1, NB, SSD_HEADS, HD, NST)),
         ("sc_sample_o", (1, NB, SCW - 1, D))]


def kernel(**inputs):
    import numpy as _np
    import concourse.bacc as _bacc
    from concourse.bass_utils import run_bass_kernel_spmd as _run

    nc = _bacc.Bacc("TRN2", target_bir_lowering=False, num_devices=1)
    arrays = {k: _np.ascontiguousarray(v) for k, v in inputs.items()}
    arrays.update(host_constants())
    d = {k: nc.dram_tensor(f"in_{k}", v.shape, mybir.dt.from_np(v.dtype), kind="ExternalInput").ap()
         for k, v in arrays.items()}
    for name, shape in _OUTS:
        d[name] = nc.dram_tensor(name, shape, F32, kind="ExternalOutput").ap()
    build(nc, d)
    r = _run(nc, [{f"in_{k}": v for k, v in arrays.items()}], core_ids=[0])
    return tuple(r.results[0][name] for name, _ in _OUTS)
```

```python
from contextlib import ExitStack, contextmanager

import numpy as np
import concourse.bass as bass
from concourse import mybir

F32 = mybir.dt.float32
F32R = mybir.dt.float32r
I32 = mybir.dt.int32
ACT = mybir.ActivationFunctionType
ALU = mybir.AluOpType
AX = mybir.AxisListType
ds = bass.ds

D = 2048
KC = D // 128
TP = 256
NB, TS = 8, 8
TSA = NB * TS
T = TP + TSA
EPS = 1e-5
NEG = -1e30
SSD_HEADS, HD, GROUPS, NST = 32, 64, 4, 128
CONV_CH = 3072
CCH = CONV_CH // 128
CW, SCW = 4, 3
OFF_Z, OFF_XBC, OFF_DT, OFF_SC = 0, 2048, 5120, 5152
AH, KVH, DH, G4 = 16, 4, 128, 4
PAST, PAGE, BLK = 2048, 128, 256
NPG, NBLK, TOPK = PAST // PAGE, PAST // BLK, 3
NM, CAH = 256, 4
QSCALE = float(DH) ** -0.5
NSLOT = 4
CROSS_V_AHEAD = 4
S0_RING = 3
NSPLIT = 2

C_ID, C_ONE, C_TRIP, C_TRIS, C_BLKS, C_BM, C_SLOPE, C_TIE = 0, 128, 256, 384, 448, 512, 520, 536
C_N = 600
VA_MIX, VA_CROSS, VA_MEM, VA_FIN, VA_EV, VA_N = 0, 32, 64, 96, 112, 128
VB_CW, VB_CB, VB_N = 0, 96, 120
VC_N = 48


def host_constants():
    f = np.float32
    c = np.zeros((128, C_N), f)
    c[:, C_ID:C_ID + 128] = np.eye(128)
    c[:, C_ONE:C_ONE + 128] = 1
    s, l = np.arange(128)[:, None], np.arange(128)[None, :]
    c[:, C_TRIP:C_TRIP + 128] = s <= l
    same = (np.arange(64)[:, None] // TS) == (np.arange(64)[None, :] // TS)
    c[:64, C_TRIS:C_TRIS + 64] = same & (np.arange(64)[:, None] <= np.arange(64)[None, :])
    c[:64, C_BLKS:C_BLKS + 64] = same
    c[:64, C_BM:C_BM + 8] = (np.arange(64)[:, None] // TS) == np.arange(8)[None, :]
    slopes = np.array([2.0 ** (-8.0 * (h + 1) / AH) for h in range(AH)], dtype=f)
    c[:, C_SLOPE:C_SLOPE + AH] = slopes[None]
    c[:, C_TIE:C_TIE + 64] = (np.arange(8)[None, :] < np.arange(8)[:, None]).reshape(1, 64)
    q = np.arange(2)[None, :, None] * 128 + np.arange(128)[:, None, None]
    k = np.arange(256)[None, None, :]
    dist = np.where(q >= k, (k - q).astype(f), f(NEG)).astype(f).reshape(128, 512)
    head, tok = np.arange(128) // TS, np.arange(128) % TS
    past = (-slopes[head][:, None] * (PAST + tok[:, None] - np.arange(PAST)[None]).astype(f)).astype(f)
    col = np.arange(64)
    own = np.full((128, NB, 64), NEG, f)
    for b in range(NB):
        d = tok[:, None] - (col[None] - TS * b)
        ok = (col[None] // TS == b) & (d >= 0)
        own[:, b] = np.where(ok, -slopes[head][:, None] * d.astype(f), f(NEG))
    qmask = np.broadcast_to((col[None] // TS == np.arange(NB)[:, None]).astype(f).reshape(1, 512), (128, 512))
    selhp = np.zeros((32, 2048), f)
    selhp[np.arange(2048) // HD, np.arange(2048)] = 1
    return {"c_main": c, "c_dist": dist, "c_past": past, "c_own": own.reshape(128, 512),
            "c_qmask": np.ascontiguousarray(qmask), "c_selhp": selhp}


class Trunk:

    def __init__(self, nc, d):
        self.nc, self.d = nc, d
        self.tile = 0
        self.slot = 0


@contextmanager
def stage(nc, label, names):
    sems = {n: nc.alloc_semaphore(name=f"{label}_{n}") for n in names}
    yield sems
    nc.clear_and_free_semaphores(list(sems.values()))
    nc.all_engine_barrier()


class Proj:

    def __init__(self, e, w_src, tiles, ntok=T, kch=KC, tiles_per_slot=1):
        self.e, self.w_src, self.tiles, self.ntok, self.kch = e, w_src, tiles, ntok, kch
        self.tps = tiles_per_slot
        self.slots = tiles // tiles_per_slot
        self.iters = self.slots // NSLOT
        self.tile0, self.slot0 = e.tile, e.slot
        e.tile += tiles
        e.slot += self.slots

    def load(self, sp, i, j):
        sp.wait_ge(self.e.w_lo, i * NSLOT + (self.slot0 + j + 1))
        src, kch, cols = self.w_src(i, j)
        sp.dma_start(self.e.w[:, j, :].rearrange("p (k n) -> p k n", n=cols), src).then_inc(self.e.w_landed[j], 16)

    def first_loads(self, sp):
        for j in range(NSLOT):
            self.load(sp, 0, j)

    def later_loads(self, sp):
        if self.iters > 1:
            with sp.Fori(0, self.iters - 1) as i:
                for j in range(NSLOT):
                    self.load(sp, i + 1, j)

    def high(self, act, i, j):
        e = self.e
        act.wait_ge(e.w_landed[j % NSLOT], i * 16 + 16 * ((self.slot0 + j) // NSLOT + 1))
        done = (j - 1) * self.tps if j else -1
        act.wait_ge(e.pe_event, i * (NSLOT * self.tps) + (NSLOT + self.tile0 + done))
        e.nc.scalar.activation(e.w_split[0][:, j % NSPLIT, :], e.w[:, j % NSLOT, :], ACT.Copy).then_inc(e.w_hi, 1)

    def low(self, pool, first=0, end=None):
        e = self.e

        def one(i, j):
            pool.wait_ge(e.w_hi, i * NSLOT + (self.slot0 + j + 1))
            e.nc.gpsimd.tensor_tensor(e.w_split[1][:, j % NSPLIT, :], e.w[:, j % NSLOT, :],
                                      e.w_split[0][:, j % NSPLIT, :].bitcast(F32), ALU.subtract).then_inc(e.w_lo, 1)

        bodies, rest = divmod((self.slots if end is None else end) - first, NSLOT)
        if bodies > 1:
            with pool.Fori(0, bodies) as i:
                for j in range(NSLOT):
                    one(i, first + j)
        else:
            rest += NSLOT * bodies
            bodies = 0
        for j in range(rest):
            one(bodies, first + j)

    def loop(self, eng, body):
        if self.iters == 1:
            body(0)
        else:
            with eng.Fori(0, self.iters) as i:
                body(i)

    def act_loop(self, act, tile, more=False):
        def body(i, last):
            for j in range(NSLOT):
                tile(i, j)
                if not last or j + NSPLIT < NSLOT or more:
                    self.high(act, i, j + NSPLIT)

        if self.iters > 1:
            with act.Fori(0, self.iters - 1) as i:
                body(i, False)
        body(self.iters - 1, True)

    def matmuls(self, pe, rhs, ready=None):
        e = self.e

        def body(i):
            for j in range(NSLOT * self.tps):
                slot = j // self.tps
                w = [e.w_split[p][:, slot % NSPLIT, :].rearrange("p (k n) -> p k n", n=128 * self.tps) for p in range(2)]
                cols = slice(128 * (j % self.tps), 128 * (j % self.tps) + 128)
                if j % self.tps == 0:
                    pe.wait_ge(e.w_hi, i * NSLOT + (self.slot0 + slot + 1))
                pe.wait_ge(e.bank_free, i * (NSLOT * self.tps) + (self.tile0 + j + 1))
                out = e.bank[j % NSLOT][:, 0:self.ntok]
                for k in range(self.kch):
                    if ready and isinstance(i, int) and j == 0:
                        ready(pe, k)
                    for part in range(2):
                        e.nc.tensor.matmul(out, w[0][:, k, cols], rhs(k)[part], start=(k == 0 and part == 0), stop=False)
                if j % self.tps == 0:
                    pe.wait_ge(e.w_lo, i * NSLOT + (NSLOT + self.slot0 + slot + 1))
                for k in range(self.kch):
                    m = e.nc.tensor.matmul(out, w[1][:, k, cols], rhs(k)[0], start=False, stop=k == self.kch - 1)
                m.then_inc(e.pe_event, 1)

        if ready:
            body(0)
            if self.iters > 1:
                with pe.Fori(0, self.iters - 1) as i:
                    body(i + 1)
        else:
            self.loop(pe, body)

    def take_over(self, eng):
        eng.wait_ge(self.e.bank_free, NSLOT + self.tile0)

    def wait_tile(self, eng, i, j):
        eng.wait_ge(self.e.pe_event, i * (NSLOT * self.tps) + (NSLOT + self.tile0 + j + 1))


@contextmanager
def split_buffers(e, label, kch, ntok=T):
    with ExitStack() as ctx:
        sb = lambda n, sh: ctx.enter_context(e.nc.sbuf_tensor(f"{label}_{n}", sh, F32R))
        e.w_split = [sb(f"w_{p}", [128, NSPLIT, KC * 128]) for p in ("hi", "lo")]
        yield [sb(f"x_{p}", [128, kch, ntok]) for p in ("hi", "lo")]


class Feed:
    sems = ["made", "hi", "lo"]

    def __init__(self, e, s, dst, kch, y, make=None, ring=None):
        self.e, self.s, self.dst, self.kch, self.y, self.make, self.ring = e, s, dst, kch, y, make, ring

    def vector(self, dve):
        LAG = 2
        for c in range(self.kch + LAG):
            if self.make and c < self.kch:
                if self.ring and c >= self.ring:
                    dve.wait_ge(self.s["lo"], c - self.ring + 1)
                self.make(c).then_inc(self.s["made"], 1)
            if c >= LAG:
                b = c - LAG
                dve.wait_ge(self.s["hi"], b + 1)
                self.e.nc.vector.tensor_tensor(self.dst[1][:, b, :], self.y(b), self.dst[0][:, b, :].bitcast(F32),
                                               ALU.subtract).then_inc(self.s["lo"], 1)

    def scalar(self, act, p=None):
        if p:
            p.high(act, 0, 0)
        for c in range(self.kch):
            if self.make:
                act.wait_ge(self.s["made"], c + 1)
            self.e.nc.scalar.activation(self.dst[0][:, c, :], self.y(c), ACT.Copy).then_inc(self.s["hi"], 1)
        if p:
            p.high(act, 0, 1)

    def ready(self, pe, c):
        pe.wait_ge(self.s["lo"], c + 1)

    def rhs(self, k):
        return self.dst[0][:, k, :], self.dst[1][:, k, :]


def columns(w, off=0, step=128):
    wv = w.rearrange("(c p) n -> p c n", p=128)

    def src(i, j):
        return wv[:, :, ds(i * (NSLOT * step) + (off + j * step), 128)], KC, 128
    return src


def wide_columns(w):
    wv = w.rearrange("(c p) n -> p c n", p=128)

    def src(i, j):
        return wv[:, :, 512 * j:512 * j + 512], 4, 512
    return src


def sc_columns(w):
    wv = w.rearrange("(c p) n -> p c n", p=128)

    def src(i, j):
        return wv[:, :, ds(i * 128 + (OFF_SC + j * D), 128)], KC, 128
    return src


def transposes(e, s, fills, arrivals={}):
    nc = e.nc
    evac = ("evac_v", "evac_s")

    def tensor(pe):
        for f, (parts, rows, _, _) in enumerate(fills):
            for name, value in arrivals.get(f, ()):
                pe.wait_ge(s[name], value)
            if f >= 8:
                pe.wait_ge(s[evac[f % 2]], (f - 8) // 2 + 1)
            for col, src, k, m in parts:
                t = nc.tensor.transpose(e.bank[f % 8][0:m, col:col + k], src, e.ident[0:k, 0:k])
            t.then_inc(s["turned"], 1)

    def copies(eng, par):
        for f, (_, rows, width, out) in enumerate(fills):
            if f % 2 == par:
                eng.wait_ge(s["turned"], f + 1)
                src = e.bank[f % 8][0:rows, 0:width]
                if len(out.shape) == 3:
                    src = src.rearrange("p (a b) -> p a b", a=out.shape[1])
                if par:
                    nc.scalar.activation(out, src, ACT.Copy).then_inc(s["evac_s"], 1)
                else:
                    nc.vector.tensor_copy(out, src).then_inc(s["evac_v"], 1)

    return tensor, copies


def setup(e):
    nc, d = e.nc, e.d
    with ExitStack() as ctx:
        sb = lambda n, sh: ctx.enter_context(nc.sbuf_tensor(n, sh, F32))
        s = ctx.enter_context(stage(nc, "setup", ["consts_in", "zeroed", "rows_in", "x_in", "mem_in", "turned", "evac_v", "evac_s"]))
        rows = sb("vec_rows", [128, 3, 128])
        xr = sb("x_rows", [128, 3, D])
        mr = sb("mem_rows", [128, 2, D])
        fills = [([(0, rows[:, 0, :], 128, 128)], 128, 128, e.va[:]),
                 ([(0, rows[0:VB_N, 1, :], VB_N, 128)], 128, VB_N, e.vb[:]),
                 ([(0, rows[0:VC_N, 2, :], VC_N, 128)], 128, VC_N, e.vc[:])]
        nvec = len(fills)
        for c in range(0, KC, 2):
            fills.append(([(128 * (2 * a + m), mr[:, m, 128 * (c + a):128 * (c + a) + 128], 128, 128)
                           for a in range(2) for m in range(2)], 128, 512, e.memt[:, c:c + 2, :]))
        nmem = len(fills)
        for c in range(KC):
            cs = slice(128 * c, 128 * c + 128)
            fills.append(([(0, xr[:, 0, cs], 128, 128), (128, xr[:, 1, cs], 128, 128),
                           (256, xr[0:64, 2, cs], 64, 128)], 128, T, e.xt[:, c, :]))
        arrivals = {0: [("consts_in", 16), ("rows_in", 16 * 8)], nvec: [("mem_in", 16)], nmem: [("x_in", 32)]}
        tensor, copies = transposes(e, s, fills, arrivals)
        with nc.Block() as block:
            @block.sync
            def _(sp):
                sp.dma_start(e.const[:], d["c_main"]).then_inc(s["consts_in"], 16)
                vec = [("norm_mix_w", 0, VA_MIX), ("norm_cross_w", 0, VA_CROSS), ("norm_mem_w", 0, VA_MEM),
                       ("final_norm_w", 0, VA_FIN), ("ev_norm_w", 0, VA_EV),
                       ("ev_conv_w", 1, VB_CW), ("ev_conv_b", 1, VB_CB), ("ev_sc_w", 2, 0)]
                for name, t, row in vec:
                    a = d[name]
                    if len(a.shape) > 1:
                        a = a.rearrange("a b -> (a b)" if len(a.shape) == 2 else "a b c -> (a b c)")
                    n = a.shape[0] // 128
                    sp.dma_start(rows[row:row + n, t, :], a.rearrange("(r p) -> r p", p=128)).then_inc(s["rows_in"], 16)
                sp.dma_start(mr[:], d["mem_prompt"][0].rearrange("(t p) n -> p t n", p=128)).then_inc(s["mem_in"], 16)
                sp.dma_start(xr[:, 0:2, :], d["x_prompt"][0].rearrange("(t p) n -> p t n", p=128)).then_inc(s["x_in"], 16)
                sp.dma_start(xr[0:64, 2, :], d["x_sample"].rearrange("b t n -> (b t) n")).then_inc(s["x_in"], 16)
                e.next_proj.first_loads(sp)

            @block.gpsimd
            def _(pool):
                pool.sem_inc(e.w_lo, NSLOT)

            @block.tensor
            def _(pe):
                pe.sem_inc(e.pe_event, NSLOT)
                tensor(pe)

            @block.vector
            def _(dve):
                dve.sem_inc(e.bank_free, NSLOT)
                copies(dve, 0)

            @block.scalar
            def _(act):
                copies(act, 1)


def norm_sums(e, label, src, ntok, r, squares=None):
    nc = e.nc
    RING = 4
    with ExitStack() as ctx:
        s = ctx.enter_context(stage(nc, label, ["squared_v", "squared_s", "added", "var", "std", "rstd"]))
        chunks = KC if squares is None else 1
        sq = ctx.enter_context(nc.sbuf_tensor(f"{label}_sq", [128, RING, T], F32)) if squares is None else squares.unsqueeze(1)

        def square(eng, par, op, sem):
            for n in range(KC // 4):
                c = 4 * n + 2 * par
                if c >= RING:
                    eng.wait_ge(s["added"], c + 2 - RING)
                op(sq[:, c % RING:c % RING + 2, 0:ntok], src[:, c:c + 2, 0:ntok]).then_inc(sem, 1)

        with nc.Block() as block:
            @block.scalar
            def _(act):
                if squares is None:
                    square(act, 1, lambda o, x: nc.scalar.activation(o, x, ACT.Square), s["squared_s"])
                act.wait_ge(s["var"], 1)
                nc.scalar.activation(r[:, 0:ntok], r[:, 0:ntok], ACT.Sqrt).then_inc(s["std"], 1)

            @block.tensor
            def _(pe):
                for c in range(chunks):
                    if squares is None and c % 2 == 0:
                        pe.wait_ge(s["squared_s" if c % 4 else "squared_v"], c // 4 + 1)
                    nc.tensor.matmul(e.bank[4][:, 0:ntok], e.ones, sq[:, c % RING, 0:ntok], start=c == 0,
                                     stop=c == chunks - 1).then_inc(s["added"], 1)

            @block.vector
            def _(dve):
                if squares is None:
                    square(dve, 0, lambda o, x: nc.vector.tensor_tensor(o, x, x, ALU.mult), s["squared_v"])
                dve.wait_ge(s["added"], chunks)
                nc.vector.tensor_scalar(r[:, 0:ntok], e.bank[4][:, 0:ntok], 1.0 / D, EPS, ALU.mult, ALU.add).then_inc(s["var"], 1)
                dve.wait_ge(s["std"], 1)
                nc.vector.reciprocal(r[:, 0:ntok], r[:, 0:ntok]).then_inc(s["rstd"], 1)


@contextmanager
def normed(e, label, src, ntok, wcol, dst, r=None, scratch=None, squares=None):
    with ExitStack() as ctx:
        RING = 3
        if r is None:
            r = ctx.enter_context(e.nc.sbuf_tensor(f"{label}_r", [128, T], F32)) if scratch is None else scratch[:, RING, :]
            norm_sums(e, f"{label}_sums", src, ntok, r, squares)
        y = ctx.enter_context(e.nc.sbuf_tensor(f"{label}_y", [128, RING, ntok], F32)) if scratch is None else scratch[:, 0:RING, :]
        s = ctx.enter_context(stage(e.nc, label, Feed.sems))
        chunk = lambda c: y[:, c % RING, :]
        make = lambda c: e.nc.vector.scalar_tensor_tensor(chunk(c), src[:, c, 0:ntok], e.va[:, wcol + c:wcol + c + 1],
                                                          r[:, 0:ntok], ALU.mult, ALU.mult)
        yield Feed(e, s, dst, KC, chunk, make, RING)


def memory_kv(e, layer, p, nxt, r, kvr, stored):
    nc, d = e.nc, e.d
    with ExitStack() as ctx:
        x = ctx.enter_context(split_buffers(e, f"mem{layer}", KC, NM))
        feed = ctx.enter_context(normed(e, f"norm_mem{layer}", e.memt, NM, VA_MEM + KC * layer, x, r))
        sb = lambda n, sh: ctx.enter_context(nc.sbuf_tensor(n, sh, F32))
        s = ctx.enter_context(stage(nc, f"mem{layer}", ["turned", "evac_v", "evac_s"]))
        kvt = sb(f"mem{layer}_kvt", [128, 2 * CAH, NM])
        with nc.Block() as block:
            @block.sync
            def _(sp):
                p.later_loads(sp)
                nxt.first_loads(sp)

            @block.tensor
            def _(pe):
                p.matmuls(pe, feed.rhs, feed.ready)

            block.vector(feed.vector)

            @block.gpsimd
            def _(pool):
                p.low(pool)

            @block.scalar
            def _(act):
                def tile(i, j):
                    p.wait_tile(act, i, j)
                    nc.scalar.activation(kvt[:, ds(4 * i + j, 1), :], e.bank[j][:, 0:NM].unsqueeze(1), ACT.Copy).then_inc(e.bank_free, 1)
                feed.scalar(act, p)
                p.act_loop(act, tile)
        fills = [([(128 * h, kvt[:, CAH * kv + h, 128 * m:128 * m + 128], 128, 128) for h in range(CAH)], 128, 512,
                  kvr[:, kv, m, :]) for kv in range(2) for m in range(2)]
        tensor, copies = transposes(e, s, fills)
        with nc.Block() as block:
            block.tensor(tensor)
            block.vector(lambda eng: copies(eng, 0))
            block.scalar(lambda eng: copies(eng, 1))

            @block.sync
            def _(sp):
                sp.wait_ge(s["evac_v"], 2)
                sp.wait_ge(s["evac_s"], 2)
                for kv, name in enumerate(("mem_k_o", "mem_v_o")):
                    sp.dma_start(d[name][layer, 0].rearrange("(t p) h n -> p t (h n)", p=128), kvr[:, kv]).then_inc(stored, 16)
                if layer == 1:
                    sp.wait_ge(stored, 64)


def even_projections(e, p_z, p_xbc, p_sc, nxt, tail, sctail):
    nc, d = e.nc, e.d
    with ExitStack() as ctx:
        sb = lambda n, sh: ctx.enter_context(nc.sbuf_tensor(n, sh, F32))
        with ExitStack() as c2:
            x = c2.enter_context(split_buffers(e, "even", KC))
            with normed(e, "norm_mix0", e.xt, T, VA_MIX, x, scratch=e.zs) as feed:
                rhs = feed.rhs
                dt_and_history(e, feed, p_z, tail, sctail)
            conv_projections(e, p_z, p_xbc, p_sc, rhs, tail)
            short_conv_projection(e, p_sc, nxt, rhs, sctail)


def dt_and_history(e, feed, p_z, tail, sctail):
    nc, d = e.nc, e.d
    with ExitStack() as ctx:
        sb = lambda n, sh, dt=F32: ctx.enter_context(nc.sbuf_tensor(n, sh, dt))
        s = ctx.enter_context(stage(nc, "hist", ["conv_in", "sc_in", "dt_w_in", "turned", "evac_v", "evac_s", "dt_hi", "dt_lo",
                                                 "dt_done", "dt_raw", "dt_turned", "dt_out"]))
        crows = e.xbc[:].rearrange("p c t -> p (c t)")[:, 0:CONV_CH]
        srows = e.ysc[:].rearrange("p c t -> p (c t)")[:, 0:D]
        wdt = e.zs[:, 6:8, :].rearrange("p c t -> p (c t)")[:, 0:KC * SSD_HEADS].rearrange("p (k h) -> p k h", k=KC)
        wdts = [sb(f"w_dt_{p}", [128, KC, SSD_HEADS], F32R) for p in ("hi", "lo")]
        dtt = e.zs[0:SSD_HEADS, 5, :]
        fills = [([(24 * (c - c0), crows[0:24, 128 * c:128 * c + 128], 24, 128) for c in range(c0, c0 + 12)], 128, 288,
                  tail[:, c0:c0 + 12, 3:27]) for c0 in (0, 12)]
        fills.append(([(16 * c, srows[0:16, 128 * c:128 * c + 128], 16, 128) for c in range(KC)], 128, 256, sctail[:, :, 2:18]))
        tensor, copies = transposes(e, s, fills)
        units = [(0, 128), (1, 128), (2, TSA)]
        with nc.Block() as block:
            @block.sync
            def _(sp):
                sp.dma_start(wdt, d["ev_w_in"][0].rearrange("(c p) n -> p c n", p=128)[:, :, OFF_DT:OFF_DT + SSD_HEADS]).then_inc(s["dt_w_in"], 16)
                sp.dma_start(crows[0:24, :], d["state_conv"][0].rearrange("b j n -> (b j) n")).then_inc(s["conv_in"], 16)
                sp.dma_start(srows[0:16, :], d["state_sc"][0].rearrange("b j n -> (b j) n")).then_inc(s["sc_in"], 16)

            @block.tensor
            def _(pe):
                pe.wait_ge(s["dt_lo"], 1)
                for k in range(KC):
                    feed.ready(pe, k)
                    for n, (p, q) in enumerate(((0, 0), (0, 1), (1, 0))):
                        m = nc.tensor.matmul(e.bank[4][0:SSD_HEADS, 0:T], wdts[p][:, k, :], feed.rhs(k)[q],
                                             start=n == 0 and k == 0, stop=n == 2 and k == KC - 1)
                m.then_inc(s["dt_done"], 1)
                pe.wait_ge(s["conv_in"], 16)
                pe.wait_ge(s["sc_in"], 16)
                tensor(pe)
                pe.wait_ge(s["dt_raw"], 1)
                for u, rows in units:
                    m = nc.tensor.transpose(e.bank[5][0:rows, 32 * u:32 * u + 32], dtt[:, 128 * u:128 * u + rows], e.ident[0:32, 0:32])
                m.then_inc(s["dt_turned"], 1)

            @block.gpsimd
            def _(pool):
                p_z.low(pool, end=NSPLIT)

            @block.scalar
            def _(act):
                act.wait_ge(s["dt_w_in"], 16)
                nc.scalar.activation(wdts[0][:], wdt, ACT.Copy).then_inc(s["dt_hi"], 1)
                feed.scalar(act, p_z)
                copies(act, 1)

            @block.vector
            def _(dve):
                v = nc.vector
                dve.wait_ge(s["dt_hi"], 1)
                v.tensor_tensor(wdts[1][:], wdt, wdts[0][:].bitcast(F32), ALU.subtract).then_inc(s["dt_lo"], 1)
                feed.vector(dve)
                dve.wait_ge(s["dt_done"], 1)
                v.tensor_copy(dtt, e.bank[4][0:SSD_HEADS, 0:T]).then_inc(s["dt_raw"], 1)
                copies(dve, 0)
                dve.wait_ge(s["dt_turned"], 1)
                v.tensor_copy(e.dt[:, 0:2, :], e.bank[5][:, 0:64].rearrange("p (u h) -> p u h", u=2)).then_inc(s["dt_out"], 1)
                v.tensor_copy(e.dt[0:TSA, 2, :], e.bank[5][0:TSA, 64:96]).then_inc(s["dt_out"], 1)


def conv_projections(e, p_z, p_xbc, p_sc, rhs, tail):
    nc = e.nc
    with ExitStack() as ctx:
        sb = lambda n, sh: ctx.enter_context(nc.sbuf_tensor(n, sh, F32))
        t = ctx.enter_context(stage(nc, "conv", ["step", "silu_done"]))
        xpp = [sb(f"conv_pad{i}", [128, CW - 1 + TP]) for i in range(2)]
        xps = [sb(f"conv_pad_s{i}", [128, NB, CW - 1 + TS]) for i in range(2)]
        acc = [sb(f"conv_acc{i}", [128, T]) for i in range(2)]
        CONV_STEPS = 12
        conv0 = 2
        with nc.Block() as block:
            @block.sync
            def _(sp):
                p_z.later_loads(sp)
                p_xbc.first_loads(sp)
                p_xbc.later_loads(sp)
                p_sc.first_loads(sp)

            @block.tensor
            def _(pe):
                for p in (p_z, p_xbc):
                    p.matmuls(pe, rhs)

            @block.gpsimd
            def _(pool):
                p_z.low(pool, NSPLIT)
                p_xbc.low(pool, end=p_xbc.slots + NSPLIT)

            @block.scalar
            def _(act):
                act.sem_inc(t["silu_done"], 2)

                def z_tile(i, j):
                    p_z.wait_tile(act, i, j)
                    nc.scalar.activation(e.zs[:, ds(4 * i + j, 1), :], e.bank[j][:, 0:T].unsqueeze(1), ACT.Silu).then_inc(e.bank_free, 1)

                def conv_tile(i, j):
                    act.wait_ge(t["step"], i * (4 * CONV_STEPS) + (conv0 + j * CONV_STEPS + 10))
                    nc.scalar.activation(e.xbc[:, ds(4 * i + j, 1), :], acc[j % 2][:].unsqueeze(1), ACT.Silu,
                                         bias=e.vb[:, ds(4 * i + (VB_CB + j), 1)]).then_inc(t["silu_done"], 1)

                p_z.act_loop(act, z_tile, more=True)

                with act.Fori(0, p_xbc.iters) as i:
                    for j in range(NSLOT):
                        p_xbc.high(act, i, j + NSPLIT)
                        conv_tile(i, j)

            @block.vector
            def _(dve):
                v = nc.vector
                v.memset(xpp[0][:, 0:CW - 1], 0.0).then_inc(t["step"], 1)
                v.memset(xpp[1][:, 0:CW - 1], 0.0).then_inc(t["step"], 1)
                p_xbc.take_over(dve)
                with dve.Fori(0, p_xbc.iters) as i:
                    for j in range(4):
                        n = [conv0 + j * CONV_STEPS]

                        def step(ins):
                            ins.then_inc(t["step"], 1)
                            n[0] += 1

                        def settled(k=0):
                            dve.wait_ge(t["step"], i * (4 * CONV_STEPS) + (n[0] - k))

                        xp, xs, y = xpp[j % 2], xps[j % 2], acc[j % 2]
                        ys = y[:, TP:T].rearrange("p (b t) -> p b t", b=NB)
                        p_xbc.wait_tile(dve, i, j)
                        step(v.tensor_copy(xp[:, 3:3 + TP], e.bank[j][:, 0:TP]))
                        v.tensor_copy(xs[:, :, 3:11], e.bank[j][:, TP:T].rearrange("p (b t) -> p b t", b=NB)).then_inc(e.bank_free, 1)
                        step(v.tensor_scalar(xs[:, :, 0:3], tail[:, ds(4 * i + j, 1), 3:27].rearrange("p c (b t) -> p (c b) t", b=NB),
                                             1.0, None, ALU.mult))
                        settled()
                        dve.wait_ge(t["silu_done"], i * 4 + (j + 1))
                        for k in range(CW):
                            wk = e.vb[:, ds(4 * i + (VB_CW + k * CCH + j), 1)]
                            if k == 0:
                                step(v.tensor_scalar(y[:, 0:TP], xp[:, 0:TP], wk, None, ALU.mult))
                                step(v.tensor_scalar(ys, xs[:, :, 0:TS], wk, None, ALU.mult))
                            else:
                                settled(1)
                                step(v.scalar_tensor_tensor(y[:, 0:TP], xp[:, k:k + TP], wk, y[:, 0:TP], ALU.mult, ALU.add))
                                settled(1)
                                step(v.scalar_tensor_tensor(ys, xs[:, :, k:k + TS], wk, ys, ALU.mult, ALU.add))
                        step(v.tensor_scalar(tail[:, ds(4 * i + j, 1), 0:3], xp[:, TP:TP + 3].unsqueeze(1), 1.0, None, ALU.mult))
                        step(v.tensor_scalar(tail[:, ds(4 * i + j, 1), 3:27].rearrange("p c (b t) -> p (c b) t", b=NB),
                                             xs[:, :, TS:TS + 3], 1.0, None, ALU.mult))
                        assert n[0] == conv0 + (j + 1) * CONV_STEPS


def short_conv_projection(e, p_sc, nxt, rhs, sctail):
    nc = e.nc
    with ExitStack() as ctx:
        sb = lambda n, sh: ctx.enter_context(nc.sbuf_tensor(n, sh, F32))
        t = ctx.enter_context(stage(nc, "sc", ["step"]))
        xp = sb("sc_pad", [128, SCW - 1 + TP])
        xs = sb("sc_pad_s", [128, NB, SCW - 1 + TS])
        part = [sb(f"sc_part{i}", [128, T]) for i in range(3)]
        SC_STEPS = 13
        sc0 = 1
        with nc.Block() as block:
            @block.sync
            def _(sp):
                p_sc.later_loads(sp)
                nxt.first_loads(sp)

            @block.tensor
            def _(pe):
                p_sc.matmuls(pe, rhs)

            @block.gpsimd
            def _(pool):
                p_sc.low(pool, NSPLIT)

            @block.scalar
            def _(act):
                def tile(i, j):
                    p_sc.wait_tile(act, i, j)
                    if j == 0:
                        act.wait_ge(t["step"], i * SC_STEPS + sc0)
                    if j == 3:
                        act.wait_ge(t["step"], i * SC_STEPS + (sc0 + 3))
                    nc.scalar.activation(part[1 if j == 3 else j][:], e.bank[j][:, 0:T],
                                         ACT.Silu if j == 3 else ACT.Copy).then_inc(e.bank_free, 1)

                p_sc.take_over(act)
                p_sc.act_loop(act, tile)

            @block.vector
            def _(dve):
                v = nc.vector
                v.memset(xp[:, 0:SCW - 1], 0.0).then_inc(t["step"], 1)
                y = part[2]
                ys = y[:, TP:T].rearrange("p (b t) -> p b t", b=NB)
                with dve.Fori(0, p_sc.iters) as i:
                    n = [sc0]

                    def step(ins):
                        ins.then_inc(t["step"], 1)
                        n[0] += 1

                    def settled(k=0):
                        dve.wait_ge(t["step"], i * SC_STEPS + (n[0] - k))

                    fp = lambda a: a[:, 0:TP]
                    fs = lambda a: a[:, TP:T].rearrange("p (b t) -> p b t", b=NB)
                    step(v.tensor_scalar(xs[:, :, 0:2], sctail[:, ds(i, 1), 2:18].rearrange("p c (b t) -> p (c b) t", b=NB),
                                         1.0, None, ALU.mult))
                    dve.wait_ge(e.bank_free, i * 4 + (NSLOT + p_sc.tile0 + 3))
                    step(v.tensor_tensor(xp[:, 2:2 + TP], fp(part[1]), fp(part[2]), ALU.mult))
                    step(v.tensor_tensor(xs[:, :, 2:10], fs(part[1]), fs(part[2]), ALU.mult))
                    settled()
                    for k in range(SCW):
                        wk = e.vc[:, ds(i + k * KC, 1)]
                        if k == 0:
                            step(v.tensor_scalar(y[:, 0:TP], xp[:, 0:TP], wk, None, ALU.mult))
                            step(v.tensor_scalar(ys, xs[:, :, 0:TS], wk, None, ALU.mult))
                        else:
                            settled(1)
                            step(v.scalar_tensor_tensor(y[:, 0:TP], xp[:, k:k + TP], wk, y[:, 0:TP], ALU.mult, ALU.add))
                            settled(1)
                            step(v.scalar_tensor_tensor(ys, xs[:, :, k:k + TS], wk, ys, ALU.mult, ALU.add))
                    step(v.tensor_scalar(sctail[:, ds(i, 1), 0:2], xp[:, TP:TP + 2].unsqueeze(1), 1.0, None, ALU.mult))
                    step(v.tensor_scalar(sctail[:, ds(i, 1), 2:18].rearrange("p c (b t) -> p (c b) t", b=NB),
                                         xs[:, :, TS:TS + 2], 1.0, None, ALU.mult))
                    settled(2)
                    step(v.tensor_tensor(y[:], y[:], part[0][:], ALU.mult))
                    settled()
                    dve.wait_ge(e.bank_free, i * 4 + (NSLOT + p_sc.tile0 + 4))
                    step(v.tensor_tensor(e.ysc[:, ds(i, 1), :], y[:].unsqueeze(1), part[1][:].unsqueeze(1), ALU.mult))
                    assert n[0] == sc0 + SC_STEPS


def store_tails(e, ctx, tail, sctail):
    nc, d = e.nc, e.d
    sb = lambda n, sh: ctx.enter_context(nc.sbuf_tensor(n, sh, F32))
    crows = sb("conv_tail_rows", [27, CONV_CH])
    srows = sb("sc_tail_rows", [18, D])
    stored = ctx.enter_context(stage(nc, "tails_out", ["stored"]))["stored"]
    c2 = ExitStack()
    s = c2.enter_context(stage(nc, "tails", ["turned", "evac_v", "evac_s"]))
    fills = [([(128 * a, tail[:, c + a, :], 128, 27) for a in range(4)], 27, 512, crows[:, 128 * c:128 * c + 512])
             for c in range(0, CCH, 4)]
    fills += [([(128 * a, sctail[:, c + a, :], 128, 18) for a in range(4)], 18, 512, srows[:, 128 * c:128 * c + 512])
              for c in range(0, KC, 4)]
    tensor, copies = transposes(e, s, fills)
    with nc.Block() as block:
        block.tensor(tensor)
        block.vector(lambda eng: copies(eng, 0))
        block.scalar(lambda eng: copies(eng, 1))

        @block.sync
        def _(sp):
            sp.wait_ge(s["evac_v"], 5)
            sp.wait_ge(s["evac_s"], 5)
            sp.dma_start(d["conv_prompt_o"][0, 0], crows[0:3, :]).then_inc(stored, 16)
            sp.dma_start(d["conv_sample_o"][0].rearrange("b j n -> (b j) n"), crows[3:27, :]).then_inc(stored, 16)
            sp.dma_start(d["sc_prompt_o"][0, 0], srows[0:2, :]).then_inc(stored, 16)
            sp.dma_start(d["sc_sample_o"][0].rearrange("b j n -> (b j) n"), srows[2:18, :]).then_inc(stored, 16)
    c2.close()
    return stored


class Softplus:
    sems = ["rows_in", "step", "minus_abs", "exped", "a_head", "a_ready"]

    def __init__(self, e, ctx, z):
        self.e, self.z = e, z
        self.s = ctx.enter_context(stage(e.nc, "softplus", self.sems))
        sb = lambda n, sh: ctx.enter_context(e.nc.sbuf_tensor(n, sh, F32))
        self.head = sb("head_rows", [128, 2, SSD_HEADS])
        self.x, self.u, self.q, self.w = [sb(f"softplus_{n}", [128, 3, SSD_HEADS]) for n in "xuqw"]

    def sync(self, sp):
        d, s = self.e.d, self.s
        sp.dma_start(self.head[:, 0, :], d["ev_dt_bias"][0:1, :].partition_broadcast(128)).then_inc(s["rows_in"], 16)
        sp.dma_start(self.head[:, 1, :], d["ev_a_log"][0:1, :].partition_broadcast(128)).then_inc(s["rows_in"], 16)

    def scalar(self, act):
        s, a = self.s, self.e.nc.scalar.activation
        act.wait_ge(s["rows_in"], 32)
        a(self.head[:, 1, :], self.head[:, 1, :], ACT.Exp).then_inc(s["a_head"], 1)
        act.wait_ge(s["minus_abs"], 1)
        a(self.u[:], self.u[:], ACT.Exp).then_inc(s["exped"], 1)

    def vector(self, dve):
        e, s, v = self.e, self.s, self.e.nc.vector
        x, u, q, w = self.x, self.u, self.q, self.w
        n = [0]

        def step(ins):
            ins.then_inc(s["step"], 1)
            n[0] += 1
            dve.wait_ge(s["step"], n[0])

        bias = self.head[:, 0:1, :].to_broadcast([128, 3, SSD_HEADS])
        dve.wait_ge(s["rows_in"], 32)
        step(v.memset(x[:], 0.0))
        step(v.tensor_copy(x[:, 0:2, :], e.dt[:, 0:2, :]))
        step(v.tensor_copy(x[0:TSA, 2, :], e.dt[0:TSA, 2, :]))
        step(v.tensor_tensor(x[:], x[:], bias, ALU.add))
        v.scalar_tensor_tensor(u[:], x[:], -1.0, x[:], ALU.mult, ALU.min).then_inc(s["minus_abs"], 1)
        dve.wait_ge(s["exped"], 1)
        step(v.tensor_scalar(w[:], u[:], 2.0, None, ALU.add))
        step(v.reciprocal(w[:], w[:]))
        step(v.tensor_tensor(u[:], u[:], w[:], ALU.mult))
        step(v.tensor_tensor(w[:], u[:], u[:], ALU.mult))
        step(v.tensor_scalar(q[:], w[:], 1.0 / 17, None, ALU.mult))
        for k in (15, 13, 11, 9, 7, 5, 3):
            step(v.scalar_tensor_tensor(q[:], q[:], 1.0 / k, w[:], ALU.add, ALU.mult))
        step(v.scalar_tensor_tensor(q[:], q[:], 1.0, u[:], ALU.add, ALU.mult))
        step(v.tensor_scalar(q[:], q[:], 2.0, None, ALU.mult))
        step(v.scalar_tensor_tensor(e.dt, x[:], 0.0, q[:], ALU.max, ALU.add))
        dve.wait_ge(s["a_head"], 1)
        v.scalar_tensor_tensor(self.z.a, e.dt, -1.0, self.head[:, 1:2, :].to_broadcast([128, 3, SSD_HEADS]),
                               ALU.mult, ALU.mult).then_inc(s["a_ready"], 1)


def s0_rows(state):
    return state[0].rearrange("b h p n -> b (h p) n").rearrange("b (t q) n -> q b t n", q=128)


def ssd_steps(e, z):
    nc, d = e.nc, e.d
    with ExitStack() as ctx:
        sb = lambda n, sh: ctx.enter_context(nc.sbuf_tensor(n, sh, F32))
        s = ctx.enter_context(stage(nc, "steps", ["rows_in", "step", "sums_ready", "small_ready", "sums_out", "decays"]))
        dcol = sb("d_skip_col", [SSD_HEADS, 1])
        r = sb("scan_totals", [128, 3, SSD_HEADS])
        with nc.Block() as block:
            @block.sync
            def _(sp):
                sp.dma_start(z.selhp[0:32, :], d["c_selhp"]).then_inc(s["rows_in"], 16)
                sp.dma_start(dcol[:], d["ev_d_skip"].rearrange("a h -> h a")).then_inc(s["rows_in"], 16)
                for b in range(S0_RING - 1):
                    sp.dma_start(z.s0[b][:], s0_rows(d["state_ssm"])[:, b]).then_inc(z.s0_in[f"in{b}"], 16)

            @block.vector
            def _(dve):
                v = nc.vector
                n = [0]

                def step(ins):
                    ins.then_inc(s["step"], 1)
                    n[0] += 1
                    dve.wait_ge(s["step"], n[0])

                step(v.memset(z.acs[:], 0.0))
                step(v.memset(r[:], 0.0))
                dve.wait_ge(s["sums_ready"], 1)
                for k, dst in ((0, z.acs), (1, r)):
                    src = e.bank[0][:, 96 * k:96 * k + 96].rearrange("p (u h) -> p u h", u=3)
                    step(v.tensor_copy(dst[:, 0:2, :], src[:, 0:2, :]))
                    step(v.tensor_copy(dst[0:TSA, 2, :], src[0:TSA, 2, :]))
                step(v.tensor_copy(z.acst[:], e.bank[1][0:32, 0:T]))
                v.tensor_tensor(z.dec[:], r[:], z.acs[:], ALU.subtract).then_inc(s["sums_out"], 1)
                dve.wait_ge(s["small_ready"], 1)
                step(v.tensor_copy(z.dhp[:], e.bank[2][:, 0:KC]))
                step(v.tensor_copy(z.etot_hp[:], e.bank[2][:, 16:144].rearrange("p (t b) -> p t b", t=KC)))

            @block.scalar
            def _(act):
                a = nc.scalar.activation
                act.wait_ge(s["sums_out"], 1)
                a(z.eacst[:], z.acst[:], ACT.Exp).then_inc(s["decays"], 1)
                a(z.dec[:], z.dec[:], ACT.Exp).then_inc(s["decays"], 1)
                a(z.etot[:], r[:], ACT.Exp).then_inc(s["decays"], 1)

            @block.tensor
            def _(pe):
                mm = nc.tensor.matmul
                for u_ in range(3):
                    n, tri, blk = unit_masks(e, u_)
                    h = slice(32 * u_, 32 * u_ + 32)
                    mm(e.bank[0][0:n, 32 * u_:32 * u_ + 32], tri, z.a[0:n, u_, :], start=True, stop=True)
                    mm(e.bank[0][0:n, 96 + 32 * u_:128 + 32 * u_], blk, z.a[0:n, u_, :], start=True, stop=True)
                    m = mm(e.bank[1][0:32, 128 * u_:128 * u_ + n], z.a[0:n, u_, :], tri, start=True, stop=True)
                m.then_inc(s["sums_ready"], 1)
                pe.wait_ge(s["rows_in"], 32)
                pe.wait_ge(s["decays"], 1)
                for t in range(KC):
                    sel = z.selhp[0:32, 128 * t:128 * t + 128]
                    mm(e.bank[2][:, t:t + 1], sel, dcol[:], start=True, stop=True)
                    m = mm(e.bank[2][:, 16 + 8 * t:24 + 8 * t], sel, z.eacst[:, TP + TS - 1:T:TS], start=True, stop=True)
                m.then_inc(s["small_ready"], 1)


def unit_masks(e, u):
    if u < 2:
        return 128, e.const[:, C_TRIP:C_TRIP + 128], e.ones
    return TSA, e.const[0:TSA, C_TRIS:C_TRIS + TSA], e.const[0:TSA, C_BLKS:C_BLKS + TSA]


def unit_tokens(e, z, u):
    nc = e.nc
    n = unit_masks(e, u)[0]
    tok = slice(128 * u, 128 * u + n)
    with ExitStack() as ctx:
        s = ctx.enter_context(stage(nc, f"tokens{u}", ["turned", "scaled", "decayed", "b_out"]))
        with nc.Block() as block:
            @block.tensor
            def _(pe):
                for f in range(5):
                    for a in range(4):
                        m = nc.tensor.transpose(e.bank[f][0:n, 128 * a:128 * a + 128], e.xbc[:, 4 * f + a, tok], e.ident)
                    m.then_inc(s["turned"], 1)

            @block.vector
            def _(dve):
                for f in range(4):
                    dve.wait_ge(s["turned"], f + 1)
                    v3 = lambda a: a[0:n, :].rearrange("p (h q) -> p h q", h=8)
                    nc.vector.tensor_tensor(v3(z.xr[:, 512 * f:512 * f + 512]), v3(e.bank[f][:, :]),
                                            e.dt[0:n, u, 8 * f:8 * f + 8].unsqueeze(2).to_broadcast([n, 8, HD]),
                                            ALU.mult).then_inc(s["scaled"], 1)
                for f in range(4):
                    v3 = lambda a: a[0:n, :].rearrange("p (h q) -> p h q", h=8)
                    dve.wait_ge(s["scaled"], f + 1)
                    nc.vector.tensor_tensor(v3(z.xd[:, 512 * f:512 * f + 512]), v3(z.xr[:, 512 * f:512 * f + 512]),
                                            z.dec[0:n, u, 8 * f:8 * f + 8].unsqueeze(2).to_broadcast([n, 8, HD]),
                                            ALU.mult).then_inc(s["decayed"], 1)

            @block.scalar
            def _(act):
                act.wait_ge(s["turned"], 5)
                nc.scalar.activation(z.btok[0:n, :], e.bank[4][0:n, :], ACT.Copy).then_inc(s["b_out"], 1)


def unit_groups(e, z, u):
    nc = e.nc
    n, tri, _ = unit_masks(e, u)
    tok = slice(128 * u, 128 * u + n)
    has_in = u > 0
    with ExitStack() as ctx:
        s = ctx.enter_context(stage(nc, f"unit{u}", ["cb_ready", "cb_out", "spread", "diff", "exped", "weights", "within",
                                                     "decay_ready", "decay_out", "incoming", "state_ready", "state_step",
                                                     "state_out", "joined", "y_out"]))
        cbm = ctx.enter_context(nc.sbuf_tensor(f"cbm{u}", [128, 128], F32))
        mx = [[ctx.enter_context(nc.sbuf_tensor(f"mx{u}_{g}_{q}", [128, 4, 128], F32)) for q in range(2)] for g in range(2)]
        es = ctx.enter_context(nc.sbuf_tensor(f"es{u}", [128, 4, 128], F32))
        b3 = lambda i: e.bank[i][:, 0:4 * n].rearrange("p (a l) -> p a l", a=4)
        with nc.Block() as block:
            @block.tensor
            def _(pe):
                mm = nc.tensor.matmul

                def outputs(g):
                    for q in range(2):
                        pe.wait_ge(s["weights"], 2 * g + q + 1)
                        if q == 0 and g:
                            pe.wait_ge(s["joined" if has_in else "y_out"], g if has_in else 4 * g)
                        for hh in range(4):
                            h = 8 * g + 4 * q + hh
                            p0, t = 64 * (h % 2), 2 * q + hh // 2
                            m = mm(e.bank[3][p0:p0 + 64, t * n:t * n + n], z.xr[0:n, HD * h:HD * h + HD],
                                   mx[g % 2][q][0:n, hh, 0:n], start=True, stop=True)
                    m.then_inc(s["within"], 1)

                def spread(g):
                    if g:
                        pe.wait_ge(s["cb_out"], g)
                    mm(e.bank[0][0:n, 0:n], e.xbc[:, 16 + g, tok], e.xbc[:, 20 + g, tok],
                       start=True, stop=True).then_inc(s["cb_ready"], 1)
                    for q in range(2):
                        if g:
                            pe.wait_ge(s["diff"], 2 * g - 1 + q)
                        for hh in range(4):
                            h = 8 * g + 4 * q + hh
                            m = mm(e.bank[1 + q][0:n, hh * n:hh * n + n], e.ident[0:32, h:h + 1].to_broadcast([32, n]),
                                   z.acst[:, tok], start=True, stop=True)
                        m.then_inc(s["spread"], 1)

                spread(0)
                for g in range(5):
                    if g:
                        outputs(g - 1)
                    if g < 4:
                        if has_in:
                            if g:
                                pe.wait_ge(s["decay_out"], g)
                            for a in range(4):
                                m = mm(b3(5)[:, a, :], z.selhp[0:32, 128 * (4 * g + a):128 * (4 * g + a) + 128],
                                       z.eacst[:, tok], start=True, stop=True)
                            m.then_inc(s["decay_ready"], 1)
                        if g < 3:
                            spread(g + 1)
                        if u == 1:
                            if g:
                                pe.wait_ge(s["joined"], g)
                            for a in range(4):
                                t = 4 * g + a
                                m = mm(b3(4)[:, a, :], z.st[:, 128 * t:128 * t + 128], e.xbc[:, 20 + g, tok], start=True, stop=True)
                            m.then_inc(s["incoming"], 1)
                        if u < 2:
                            if g:
                                pe.wait_ge(s["state_out"], g)
                            mm(e.bank[6][:, 0:512], z.btok[0:n, 128 * g:128 * g + 128], z.xd[0:n, 512 * g:512 * g + 512],
                               start=True, stop=True).then_inc(s["state_ready"], 1)

            @block.scalar
            def _(act):
                for g in range(4):
                    for q in range(2):
                        act.wait_ge(s["diff"], 2 * g + q + 1)
                        m = mx[g % 2][q][0:n, :, 0:n]
                        nc.scalar.activation(m, m, ACT.Exp).then_inc(s["exped"], 1)
                    if has_in:
                        act.wait_ge(s["decay_ready"], g + 1)
                        if g:
                            act.wait_ge(s["y_out"], 4 * g)
                        nc.scalar.activation(es[:, :, 0:n], b3(5), ACT.Copy).then_inc(s["decay_out"], 1)

            @block.vector
            def _(dve):
                v = nc.vector

                def join(g):
                    dve.wait_ge(s["within"], g + 1)
                    y, src = es[:, :, 0:n], b3(3)
                    if has_in:
                        dve.wait_ge(s["decay_out"], g + 1)
                        if u == 1:
                            dve.wait_ge(s["incoming"], g + 1)
                            off = b3(4)
                        else:
                            off = z.yoff[:, 4 * g:4 * g + 4, :]
                        v.tensor_tensor(y, y, off, ALU.mult).then_inc(s["state_step"], 1)
                        dve.wait_ge(s["state_step"], joins(g))
                        v.tensor_tensor(y, y, b3(3), ALU.add).then_inc(s["joined"], 1)
                        dve.wait_ge(s["joined"], g + 1)
                        src = y
                    for a in range(4):
                        t = 4 * g + a
                        x = e.xbc[:, t, tok]
                        v.scalar_tensor_tensor(x, x, z.dhp[:, t:t + 1], src[:, a, :], ALU.mult, ALU.add).then_inc(s["y_out"], 1)
                    if u < 2:
                        dve.wait_ge(s["state_ready"], g + 1)
                        st = z.st[:, 512 * g:512 * g + 512]
                        if u == 0:
                            v.tensor_copy(st, e.bank[6][:, 0:512]).then_inc(s["state_out"], 1)
                        else:
                            st3 = st.rearrange("p (h q) -> p h q", h=8)
                            v.tensor_tensor(st3, st3, z.etot[:, 1, 8 * g:8 * g + 8].unsqueeze(2).to_broadcast([128, 8, HD]),
                                            ALU.mult).then_inc(s["state_step"], 1)
                            dve.wait_ge(s["state_step"], joins(g) + 1)
                            v.tensor_tensor(st, st, e.bank[6][:, 0:512], ALU.add).then_inc(s["state_out"], 1)

                joins = lambda g: (2 * g if u == 1 else g) + 1
                for g in range(5):
                    if g < 4:
                        dve.wait_ge(s["cb_ready"], g + 1)
                        if g:
                            dve.wait_ge(s["weights"], 2 * g)
                        v.tensor_tensor(cbm[0:n, 0:n], e.bank[0][0:n, 0:n], tri, ALU.mult).then_inc(s["cb_out"], 1)
                        for q in range(2):
                            dve.wait_ge(s["spread"], 2 * g + q + 1)
                            if g >= 2:
                                dve.wait_ge(s["within"], g - 1)
                            for hh in range(4):
                                h = 8 * g + 4 * q + hh
                                m = v.tensor_scalar(mx[g % 2][q][0:n, hh, 0:n], e.bank[1 + q][0:n, hh * n:hh * n + n],
                                                    z.acs[0:n, u, h:h + 1], 0.0, ALU.subtract, ALU.min)
                            m.then_inc(s["diff"], 1)
                        dve.wait_ge(s["cb_out"], g + 1)
                        for q in range(2):
                            dve.wait_ge(s["exped"], 2 * g + q + 1)
                            m = mx[g % 2][q][0:n, :, 0:n]
                            v.tensor_tensor(m, m, cbm[0:n, 0:n].unsqueeze(1).to_broadcast([n, 4, n]), ALU.mult).then_inc(s["weights"], 1)
                    if g:
                        join(g - 1)


def sample_states(e, z):
    nc, d = e.nc, e.d
    RING = S0_RING
    with ExitStack() as ctx:
        names = ["turned", "turn_out_v", "turn_out_s", "y_rows", "y_rows_out", "y_turned", "yoff_out", "b_masked", "new_ready", "new_out"]
        s = ctx.enter_context(stage(nc, "sstate", names + [f"stored{i}" for i in range(RING)]))
        sb = lambda n, sh: ctx.enter_context(nc.sbuf_tensor(n, sh, F32))
        s0 = z.s0
        s0t = z.st[:].rearrange("p (t n) -> p t n", t=KC)
        bmk = sb("b_masked", [TSA, 512])
        yrows = sb("state_y_rows", [128, 512])
        src, dst = s0_rows(d["state_ssm"]), s0_rows(d["ssm_sample_o"])
        with nc.Block() as block:
            @block.sync
            def _(sp):
                for b in range(RING - 1, NB):
                    if b >= RING:
                        sp.wait_ge(s[f"stored{b % RING}"], 16 * (b // RING))
                    elif b == RING - 1:
                        sp.wait_ge(z.state_stored, 16)
                    sp.dma_start(s0[b % RING][:], src[:, b]).then_inc(z.s0_in[f"in{b % RING}"], 16)

            @block.gpsimd
            def _(pool):
                for b in range(NB):
                    pool.wait_ge(s["new_out"], KC * (b + 1))
                    pool.dma_start(dst[:, b], s0[b % RING][:]).then_inc(s[f"stored{b % RING}"], 16)
                pool.wait_ge(z.tails_stored, 16 * 4)
                for i in range(RING):
                    pool.wait_ge(s[f"stored{i}"], 16 * len(range(i, NB, RING)))

            @block.tensor
            def _(pe):
                mm = nc.tensor.matmul

                def turn_y(b):
                    pe.wait_ge(s["y_rows_out"], b + 1)
                    if b:
                        pe.wait_ge(s["yoff_out"], b)
                    for a in range(4):
                        m = nc.tensor.transpose(e.bank[7][:, 128 * a:128 * a + 128], yrows[:, 128 * a:128 * a + 128], e.ident)
                    m.then_inc(s["y_turned"], 1)

                for b in range(NB):
                    st = s0[b % RING]
                    pe.wait_ge(z.s0_in[f"in{b % RING}"], 16 * (b // RING + 1))
                    for f in range(4):
                        if b:
                            pe.wait_ge(s["turn_out_s" if f % 2 else "turn_out_v"], 2 * (b - 1) + f // 2 + 1)
                        for a in range(4):
                            m = nc.tensor.transpose(e.bank[f][:, 128 * a:128 * a + 128], st[:, 4 * f + a, :], e.ident)
                        m.then_inc(s["turned"], 1)
                    if b:
                        turn_y(b - 1)
                    pe.wait_ge(s["b_masked"], b + 1)
                    for g in range(GROUPS):
                        k = 4 * b + g
                        if k >= 2:
                            pe.wait_ge(s["new_out"], 4 * (k - 1))
                        for a in range(4):
                            t = 4 * g + a
                            m = mm(e.bank[5 + g % 2][:, 128 * a:128 * a + 128], z.xd[0:TSA, 128 * t:128 * t + 128],
                                   bmk[:, 128 * g:128 * g + 128], start=True, stop=True)
                        m.then_inc(s["new_ready"], 1)
                    pe.wait_ge(s["turn_out_v"], 2 * (b + 1))
                    pe.wait_ge(s["turn_out_s"], 2 * (b + 1))
                    for g in range(GROUPS):
                        c0 = TP + 32 * (b // 4)
                        m = mm(e.bank[4][32 * g:32 * g + 32, :], e.xbc[:, 20 + g, c0:c0 + 32],
                               s0t[:, 4 * g:4 * g + 4, :].rearrange("p t n -> p (t n)"), start=True, stop=True)
                    m.then_inc(s["y_rows"], 1)
                turn_y(NB - 1)

            @block.scalar
            def _(act):
                def y_out(b):
                    act.wait_ge(s["y_turned"], b + 1)
                    y = e.bank[7][:].rearrange("p (a g l) -> p a g l", a=4, g=GROUPS)
                    l0 = TS * (b % 4)
                    nc.scalar.activation(z.yoff[:, :, TS * b:TS * b + TS].rearrange("p (g a) l -> p a g l", g=GROUPS),
                                         y[:, :, :, l0:l0 + TS], ACT.Copy).then_inc(s["yoff_out"], 1)

                for b in range(NB):
                    for f in (1, 3):
                        act.wait_ge(s["turned"], 4 * b + f + 1)
                        if b:
                            act.wait_ge(s["y_rows"], b)
                        nc.scalar.activation(s0t[:, 4 * f:4 * f + 4, :], e.bank[f][:].rearrange("p (a l) -> p a l", a=4), ACT.Copy).then_inc(s["turn_out_s"], 1)
                    if b:
                        y_out(b - 1)
                    act.wait_ge(s["y_rows"], b + 1)
                    nc.scalar.activation(yrows[:], e.bank[4][:], ACT.Copy).then_inc(s["y_rows_out"], 1)
                y_out(NB - 1)

            @block.vector
            def _(dve):
                v = nc.vector
                for b in range(NB):
                    if b:
                        dve.wait_ge(s["new_ready"], 4 * b)
                    v.tensor_scalar(bmk[:], z.btok[0:TSA, :], e.const[0:TSA, C_BM + b:C_BM + b + 1], None, ALU.mult).then_inc(s["b_masked"], 1)
                    for f in (0, 2):
                        dve.wait_ge(s["turned"], 4 * b + f + 1)
                        if b:
                            dve.wait_ge(s["y_rows"], b)
                        v.tensor_copy(s0t[:, 4 * f:4 * f + 4, :], e.bank[f][:].rearrange("p (a l) -> p a l", a=4)).then_inc(s["turn_out_v"], 1)
                    for g in range(GROUPS):
                        dve.wait_ge(s["new_ready"], 4 * b + g + 1)
                        for a in range(4):
                            t = 4 * g + a
                            x = s0[b % RING][:, t, :]
                            v.scalar_tensor_tensor(x, x, z.etot_hp[:, t, b:b + 1], e.bank[5 + g % 2][:, 128 * a:128 * a + 128],
                                                   ALU.mult, ALU.add).then_inc(s["new_out"], 1)


def prompt_state_out(e, z):
    nc, d = e.nc, e.d
    with ExitStack() as ctx:
        s = ctx.enter_context(stage(nc, "pstate", ["turned", "evac_v", "evac_s"]))
        out = z.state_rows
        fills = [([(128 * a, z.st[:, 128 * (4 * f + a):128 * (4 * f + a) + 128], 128, 128) for a in range(4)], 128, 512,
                  out[:, 4 * f:4 * f + 4, :]) for f in range(4)]
        tensor, copies = transposes(e, s, fills)
        with nc.Block() as block:
            block.tensor(tensor)
            block.vector(lambda eng: copies(eng, 0))
            block.scalar(lambda eng: copies(eng, 1))

            @block.sync
            def _(sp):
                sp.wait_ge(s["evac_v"], 2)
                sp.wait_ge(s["evac_s"], 2)
                sp.dma_start(d["ssm_prompt_o"][0, 0].rearrange("h p n -> (h p) n").rearrange("(t q) n -> q t n", q=128),
                               out[:]).then_inc(z.state_stored, 16)


@contextmanager
def gated_group_norm(e, dst):
    nc = e.nc
    with ExitStack() as ctx:
        r = ctx.enter_context(nc.sbuf_tensor("group_r", [128, GROUPS, T], F32))
        with ExitStack() as c2:
            s = c2.enter_context(stage(nc, "gnorm", ["gated", "squared", "summed", "var", "std", "rstd"]))
            sq = c2.enter_context(nc.sbuf_tensor("group_sq", [128, 8, T], F32))
            with nc.Block() as block:
                @block.vector
                def _(dve):
                    v = nc.vector

                    def variance(g):
                        dve.wait_ge(s["summed"], g + 1)
                        v.tensor_scalar(r[:, g, :], e.bank[g][:, 0:T], 1.0 / 512, EPS, ALU.mult, ALU.add).then_inc(s["var"], 1)

                    def inverse(g):
                        dve.wait_ge(s["std"], g + 1)
                        v.reciprocal(r[:, g, :], r[:, g, :]).then_inc(s["rstd"], 1)

                    for g in range(GROUPS):
                        for c in range(4 * g, 4 * g + 4, 2):
                            x = e.xbc[:, c:c + 2, :]
                            v.tensor_tensor(x, x, e.zs[:, c:c + 2, :], ALU.mult).then_inc(s["gated"], 1)
                        if g >= 2:
                            variance(g - 2)
                        if g == 3:
                            inverse(0)
                    variance(2)
                    inverse(1)
                    variance(3)
                    inverse(2)
                    inverse(3)

                @block.scalar
                def _(act):
                    def root(g):
                        act.wait_ge(s["var"], g + 1)
                        nc.scalar.activation(r[:, g, :], r[:, g, :], ACT.Sqrt).then_inc(s["std"], 1)

                    for c in range(0, KC, 2):
                        act.wait_ge(s["gated"], c // 2 + 1)
                        if c >= 8:
                            act.wait_ge(s["summed"], c // 4 - 1)
                        nc.scalar.activation(sq[:, c % 8:c % 8 + 2, :], e.xbc[:, c:c + 2, :], ACT.Square).then_inc(s["squared"], 1)
                    for g in range(GROUPS):
                        root(g)

                @block.tensor
                def _(pe):
                    for c in range(KC):
                        if c % 2 == 0:
                            pe.wait_ge(s["squared"], c // 2 + 1)
                        m = nc.tensor.matmul(e.bank[c // 4][:, 0:T], e.ones, sq[:, c % 8, :], start=c % 4 == 0, stop=c % 4 == 3)
                        if c % 4 == 3:
                            m.then_inc(s["summed"], 1)
        t = ctx.enter_context(stage(nc, "gfeed", Feed.sems))
        y = lambda c: e.xbc[:, c, :]
        make = lambda c: nc.vector.scalar_tensor_tensor(y(c), y(c), e.va[:, VA_EV + c:VA_EV + c + 1], r[:, c // 4, :], ALU.mult, ALU.mult)
        yield Feed(e, t, dst, KC, y, make)


class Scan:
    pass


def ssd(e, z, tails_stored):
    with ExitStack() as ctx:
        sb = lambda n, sh: ctx.enter_context(e.nc.sbuf_tensor(n, sh, F32))
        z.acs, z.dec, z.etot = [sb(f"scan_{n}", [128, 3, SSD_HEADS]) for n in ("acs", "dec", "etot")]
        z.acst, z.eacst = sb("scan_acst", [32, T]), sb("scan_eacst", [32, T])
        z.dhp, z.etot_hp = sb("scan_dhp", [128, KC]), sb("scan_etot_hp", [128, KC, NB])
        z.xr, z.st = sb("scan_xr", [128, D]), sb("scan_state", [128, D])
        z.selhp = sb("selhp", [32, 2048])
        z.state_rows = sb("pstate_rows", [128, KC, 128])
        z.state_stored = ctx.enter_context(stage(e.nc, "pstate_out", ["stored"]))["stored"]
        z.xd, z.btok = sb("scan_xd", [128, D]), sb("scan_btok", [128, 512])
        z.s0 = [*[sb(f"s0_{i}", [128, KC, 128]) for i in range(S0_RING - 1)], z.state_rows]
        z.s0_in = ctx.enter_context(stage(e.nc, "s0", [f"in{i}" for i in range(S0_RING)]))
        ssd_steps(e, z)
        for u in range(2):
            unit_tokens(e, z, u)
            unit_groups(e, z, u)
        prompt_state_out(e, z)
        unit_tokens(e, z, 2)
        z.yoff = sb("scan_yoff", [128, KC, TSA])
        z.tails_stored = tails_stored
        sample_states(e, z)
        unit_groups(e, z, 2)


def add_projection(e, p, feed, nxt=None, beside=None, squares=None):
    nc = e.nc
    with ExitStack() as ctx:
        if squares is not None:
            s = ctx.enter_context(stage(nc, f"squares{p.slot0}", ["zeroed", "squared", "added"]))
            sq = [ctx.enter_context(nc.sbuf_tensor(f"squares{p.slot0}_{i}", [128, p.tps, T], F32)) for i in range(2)]
        tiles = lambda i, j: e.xt[:, ds((NSLOT * i + j) * p.tps, p.tps), :]
        with nc.Block() as block:
            @block.sync
            def _(sp):
                if beside:
                    beside.sync(sp)
                p.later_loads(sp)
                if nxt:
                    nxt.first_loads(sp)

            @block.tensor
            def _(pe):
                p.matmuls(pe, feed.rhs, feed.ready)

            @block.gpsimd
            def _(pool):
                p.low(pool)

            @block.scalar
            def _(act):
                def square(i, j):
                    if squares is None:
                        return
                    act.wait_ge(e.bank_free, i * (NSLOT * p.tps) + (NSLOT + p.tile0 + (j + 1) * p.tps))
                    act.wait_ge(s["added"], i * (NSLOT * p.tps) + (j * p.tps + 1))
                    nc.scalar.activation(sq[j % 2][:], tiles(i, j), ACT.Square).then_inc(s["squared"], 1)

                if squares is not None:
                    act.sem_inc(s["squared"], 1)
                feed.scalar(act, p)
                if beside:
                    beside.scalar(act)
                p.act_loop(act, square)

            @block.vector
            def _(dve):
                def add(i, j):
                    dve.wait_ge(s["squared"], i * NSLOT + (j + 1))
                    for k in range(p.tps):
                        dve.wait_ge(s["added"], i * (NSLOT * p.tps) + (j * p.tps + k + 1))
                        nc.vector.tensor_tensor(squares, squares, sq[(j + 1) % 2][:, k, :], ALU.add).then_inc(s["added"], 1)

                if squares is not None:
                    nc.vector.memset(sq[1][:], 0.0).then_inc(s["zeroed"], 1)
                    dve.wait_ge(s["zeroed"], 1)
                    nc.vector.memset(squares, 0.0).then_inc(s["added"], 1)
                feed.vector(dve)
                if beside:
                    beside.vector(dve)
                p.take_over(dve)

                def body(i):
                    for j in range(NSLOT * p.tps):
                        p.wait_tile(dve, i, j)
                        y = e.xt[:, ds(NSLOT * p.tps * i + j, 1), :]
                        nc.vector.tensor_tensor(y, y, e.bank[j % NSLOT][:, 0:T].unsqueeze(1), ALU.add).then_inc(e.bank_free, 1)
                        if squares is not None and j % p.tps == p.tps - 1:
                            add(i, j // p.tps)
                p.loop(dve, body)
                if squares is not None:
                    add(p.iters, 0)


def prompt_attention(e, label, heads, qt, kt, v, gated, bias=None, sync=None):
    nc = e.nc
    with ExitStack() as ctx:
        s = ctx.enter_context(stage(nc, label, ["scores", "biased", "negmax", "exped", "recips", "probs", "turned",
                                                "turn_out", "out_ready", "out"]))
        sb = lambda n, sh: [ctx.enter_context(nc.sbuf_tensor(f"{label}_{n}{i}", sh, F32)) for i in range(2)]
        p, pt = sb("p", [128, 2, TP]), sb("pt", [128, 2, TP])
        nm, den, rec = sb("negmax", [128, 2]), sb("den", [128, 2]), sb("rec", [128, 2])
        sc = lambda u: e.bank[u % 2][:].rearrange("p (r k) -> p r k", r=2)
        with nc.Block() as block:
            if sync:
                block.sync(sync)

            @block.tensor
            def _(pe):
                mm = nc.tensor.matmul

                def scores(u):
                    if u >= 2:
                        if bias:
                            pe.wait_ge(s["biased"], u - 1)
                        else:
                            pe.wait_ge(s["exped"], 2 * (u - 1))
                    for r in range(2):
                        m = mm(sc(u)[:, r, :], qt(u)[:, 128 * r:128 * r + 128], kt(u), start=True, stop=True)
                    m.then_inc(s["scores"], 1)

                scores(0)
                for u in range(heads + 2):
                    if u + 1 < heads:
                        scores(u + 1)
                    if u >= 2:
                        w = u - 2
                        pe.wait_ge(s["turn_out"], w + 1)
                        if w >= 2:
                            pe.wait_ge(s["out"], w - 1)
                        for k in range(2):
                            m = mm(e.bank[4 + w % 2][:, 0:TP], v(w, k), pt[w % 2][:, k, :], start=k == 0, stop=k == 1)
                        m.then_inc(s["out_ready"], 1)
                    if 1 <= u <= heads:
                        w = u - 1
                        pe.wait_ge(s["probs"], 2 * (w + 1))
                        if w >= 2:
                            pe.wait_ge(s["turn_out"], w - 1)
                        for k in range(2):
                            for r in range(2):
                                m = nc.tensor.transpose(e.bank[2 + w % 2][:, 128 * (2 * k + r):128 * (2 * k + r) + 128],
                                                        p[w % 2][:, r, 128 * k:128 * k + 128], e.ident)
                        m.then_inc(s["turned"], 1)

            @block.scalar
            def _(act):
                for u in range(heads + 1):
                    if u < heads:
                        act.wait_ge(s["negmax"], u + 1)
                        if u >= 2:
                            act.wait_ge(s["recips"], u - 1)
                            act.wait_ge(s["turned"], u - 1)
                        for r in range(2):
                            src = p[u % 2][:, r, :] if bias else sc(u)[:, r, :]
                            nc.scalar.activation(p[u % 2][:, r, :], src, ACT.Exp, bias=nm[u % 2][:, r:r + 1],
                                                 accum_out=den[u % 2][:, r:r + 1]).then_inc(s["exped"], 1)
                    if u >= 1:
                        w = u - 1
                        act.wait_ge(s["turned"], w + 1)
                        if w >= 2:
                            act.wait_ge(s["out_ready"], w - 1)
                        nc.scalar.activation(pt[w % 2][:].rearrange("p k q -> p (k q)"), e.bank[2 + w % 2][:], ACT.Copy).then_inc(s["turn_out"], 1)

            @block.vector
            def _(dve):
                v_ = nc.vector
                for u in range(heads + 2):
                    if u < heads:
                        dve.wait_ge(s["scores"], u + 1)
                        src = sc(u)
                        if bias:
                            table, slope = bias(u)
                            if u >= 2:
                                dve.wait_ge(s["turned"], u - 1)
                            v_.scalar_tensor_tensor(p[u % 2][:], table, slope, sc(u), ALU.mult, ALU.add).then_inc(s["biased"], 1)
                            dve.wait_ge(s["biased"], u + 1)
                            src = p[u % 2][:]
                        if u >= 2:
                            dve.wait_ge(s["exped"], 2 * (u - 1))
                        v_.tensor_reduce(nm[u % 2][:], src, AX.X, ALU.max, negate=True).then_inc(s["negmax"], 1)
                    if 1 <= u <= heads:
                        w = u - 1
                        dve.wait_ge(s["exped"], 2 * (w + 1))
                        v_.reciprocal(rec[w % 2][:], den[w % 2][:]).then_inc(s["recips"], 1)
                        dve.wait_ge(s["recips"], w + 1)
                        for r in range(2):
                            x = p[w % 2][:, r, :]
                            v_.tensor_scalar(x, x, rec[w % 2][:, r:r + 1], None, ALU.mult).then_inc(s["probs"], 1)
                    if u >= 2:
                        w = u - 2
                        dve.wait_ge(s["out_ready"], w + 1)
                        v_.tensor_tensor(gated(w), gated(w), e.bank[4 + w % 2][:, 0:TP], ALU.mult).then_inc(s["out"], 1)


def cross_sample(e, layer, qt, gt, kr, vr):
    nc, d = e.nc, e.d
    L = f"xs{layer}"
    with ExitStack() as ctx:
        s = ctx.enter_context(stage(nc, L, ["mask_in", "v_in", "masked", "turned", "kt_v", "kt_s",
                                            "scores", "negmax", "exped", "recips", "probs", "p_turned", "p_out", "used",
                                            "out_ready", "rows_v", "rows_s", "out_turned", "out"]))
        sb = lambda n, sh: ctx.enter_context(nc.sbuf_tensor(f"{L}_{n}", sh, F32))
        mask = sb("mask", [128, NB, TSA])
        vr = [*vr, *[sb(f"vrows{i}", [128, 2, 512]) for i in range(len(vr), NB)]]
        kt = [sb(f"kt{i}", [128, CAH, NM]) for i in range(2)]
        qm = [sb(f"qm{i}", [128, CAH, TSA]) for i in range(2)]
        p, pt = sb("p", [128, 2, NM]), sb("pt", [128, 2, 2, 128])
        orows = sb("orows", [128, 2, 512])
        nm, den, rec = sb("negmax", [128, 2]), sb("den", [128, 2]), sb("rec", [128, 2])
        rows = lambda a: a.rearrange("(t p) h n -> p t (h n)", p=128)
        with nc.Block() as block:
            @block.sync
            def _(sp):
                sp.dma_start(mask[:], d["c_qmask"].rearrange("p (b t) -> p b t", b=NB)).then_inc(s["mask_in"], 16)
                for b in range(CROSS_V_AHEAD, NB):
                    sp.dma_start(vr[b][:], rows(d["cache_mem_v"][layer, b])).then_inc(s["v_in"], 16)

            @block.tensor
            def _(pe):
                mm = nc.tensor.matmul
                pe.wait_ge(e.cross_in, e.cross_loads(layer))
                for b in range(NB + 1):
                    if b < NB:
                        for t in range(2):
                            if b:
                                pe.wait_ge(s["kt_s" if t else "kt_v"], b)
                            for h in range(CAH):
                                m = nc.tensor.transpose(e.bank[t][:, 128 * h:128 * h + 128], kr[b][:, t, 128 * h:128 * h + 128], e.ident)
                            m.then_inc(s["turned"], 1)
                    if b:
                        c = b - 1
                        pe.wait_ge(s["kt_v"], b)
                        pe.wait_ge(s["kt_s"], b)
                        pe.wait_ge(s["masked"], b)
                        for h in range(CAH):
                            p0 = 64 * (h % 2)
                            m = mm(e.bank[2 + h // 2][p0:p0 + 64, 0:NM], qm[c % 2][:, h, :], kt[c % 2][:, h, :],
                                   start=c == 0, stop=c == NB - 1)
                        m.then_inc(s["scores"], 1)
                pe.wait_ge(s["probs"], 2)
                for t in range(2):
                    for r in range(2):
                        m = nc.tensor.transpose(e.bank[4][:, 128 * (2 * t + r):128 * (2 * t + r) + 128], p[:, r, 128 * t:128 * t + 128], e.ident)
                m.then_inc(s["p_turned"], 1)
                pe.wait_ge(s["p_out"], 1)
                for b in range(NB):
                    if b == CROSS_V_AHEAD:
                        pe.wait_ge(s["v_in"], 16 * (NB - CROSS_V_AHEAD))
                    for t in range(2):
                        for h in range(CAH):
                            c0 = 64 * (h % 2) + 32 * (b // 4)
                            m = mm(e.bank[5 + b // 4][32 * h:32 * h + 32, 128 * (b % 4):128 * (b % 4) + 128], pt[:, t, h // 2, c0:c0 + 32],
                                   vr[b][:, t, 128 * h:128 * h + 128], start=t == 0, stop=t == 1, skip_group_check=True)
                    m.then_inc(s["used"], 1)
                for half in range(2):
                    pe.wait_ge(s["rows_s" if half else "rows_v"], 1)
                    for a in range(4):
                        m = nc.tensor.transpose(e.bank[2 * half][:, 128 * a:128 * a + 128], orows[:, half, 128 * a:128 * a + 128], e.ident)
                    m.then_inc(s["out_turned"], 1)

            @block.scalar
            def _(act):
                for b in range(NB):
                    act.wait_ge(s["turned"], 2 * b + 2)
                    if b >= 2:
                        act.wait_ge(s["scores"], b - 1)
                    nc.scalar.activation(kt[b % 2][:, :, 128:256], e.bank[1][:].rearrange("p (h m) -> p h m", h=CAH), ACT.Copy).then_inc(s["kt_s"], 1)
                act.wait_ge(s["negmax"], 2)
                for r in range(2):
                    nc.scalar.activation(p[:, r, :], e.bank[2 + r][:, 0:NM], ACT.Exp, bias=nm[:, r:r + 1],
                                         accum_out=den[:, r:r + 1]).then_inc(s["exped"], 1)
                act.wait_ge(s["p_turned"], 1)
                nc.scalar.activation(pt[:].rearrange("p t r q -> p (t r q)"), e.bank[4][:], ACT.Copy).then_inc(s["p_out"], 1)
                act.wait_ge(s["used"], NB)
                nc.scalar.activation(orows[:, 1, :], e.bank[6][:], ACT.Copy).then_inc(s["rows_s"], 1)

            @block.vector
            def _(dve):
                v = nc.vector
                dve.wait_ge(s["mask_in"], 16)
                for b in range(NB):
                    if b >= 2:
                        dve.wait_ge(s["scores"], b - 1)
                    v.tensor_tensor(qm[b % 2][:], qt[:, :, TP:T], mask[:, b:b + 1, :].to_broadcast([128, CAH, TSA]), ALU.mult).then_inc(s["masked"], 1)
                    dve.wait_ge(s["turned"], 2 * b + 1)
                    v.tensor_copy(kt[b % 2][:, :, 0:128], e.bank[0][:].rearrange("p (h m) -> p h m", h=CAH)).then_inc(s["kt_v"], 1)
                dve.wait_ge(s["scores"], NB)
                for r in range(2):
                    v.tensor_reduce(nm[:, r:r + 1], e.bank[2 + r][:, 0:NM], AX.X, ALU.max, negate=True).then_inc(s["negmax"], 1)
                dve.wait_ge(s["exped"], 2)
                v.reciprocal(rec[:], den[:]).then_inc(s["recips"], 1)
                dve.wait_ge(s["recips"], 1)
                for r in range(2):
                    v.tensor_scalar(p[:, r, :], p[:, r, :], rec[:, r:r + 1], None, ALU.mult).then_inc(s["probs"], 1)
                dve.wait_ge(s["used"], NB // 2)
                v.tensor_copy(orows[:, 0, :], e.bank[5][:]).then_inc(s["rows_v"], 1)
                for b in range(NB):
                    if b % 4 == 0:
                        dve.wait_ge(s["out_turned"], b // 4 + 1)
                    g = gt[:, :, TP + TS * b:TP + TS * b + TS]
                    o = e.bank[2 * (b // 4)][:, 128 * (b % 4):128 * (b % 4) + 128].rearrange("p (h q) -> p h q", h=CAH)
                    v.tensor_tensor(g, g, o[:, :, TS * (b % 4):TS * (b % 4) + TS], ALU.mult).then_inc(s["out"], 1)


def cross_attention(e, layer, p_q, p_out, nxt):
    nc, d = e.nc, e.d
    rows = lambda a: a.rearrange("(t p) h n -> p t (h n)", p=128)
    with ExitStack() as ctx:
        sb = lambda n, sh: ctx.enter_context(nc.sbuf_tensor(f"x{layer}_{n}", sh, F32))
        qt, gt = sb("q", [128, CAH, T]), sb("g", [128, CAH, T])
        with ExitStack() as c2:
            sb2 = lambda n, sh: c2.enter_context(nc.sbuf_tensor(f"x{layer}_{n}", sh, F32))
            km, vm = sb2("km", [128, CAH, NM]), sb2("vm", [128, 2, 512])
            kr = [sb2(f"krows{i}", [128, 2, 512]) for i in range(NB)]
            vr = [sb2(f"vrows{i}", [128, 2, 512]) for i in range(CROSS_V_AHEAD)]
            kmr = vr[-1]
            with ExitStack() as c3:
                x = c3.enter_context(split_buffers(e, f"xq{layer}", KC))
                feed = c3.enter_context(normed(e, f"norm_cross{layer}", e.xt, T, VA_CROSS + KC * layer, x, squares=e.squares))
                s = c3.enter_context(stage(nc, f"xproj{layer}", ["turned", "km_v"]))
                with nc.Block() as block:
                    @block.sync
                    def _(sp):
                        sp.dma_start(kmr[:], rows(d["mem_k_o"][layer, 0])).then_inc(e.cross_in, 16)
                        sp.dma_start(vm[:], rows(d["mem_v_o"][layer, 0])).then_inc(e.cross_in, 16)
                        p_q.later_loads(sp)
                        for b in range(NB):
                            sp.dma_start(kr[b][:], rows(d["cache_mem_k"][layer, b])).then_inc(e.cross_in, 16)
                            if b < CROSS_V_AHEAD - 1:
                                sp.dma_start(vr[b][:], rows(d["cache_mem_v"][layer, b])).then_inc(e.cross_in, 16)
                        p_out.first_loads(sp)
                        sp.wait_ge(s["turned"], 2)
                        sp.dma_start(kmr[:], rows(d["cache_mem_v"][layer, CROSS_V_AHEAD - 1])).then_inc(e.cross_in, 16)

                    @block.tensor
                    def _(pe):
                        p_q.matmuls(pe, feed.rhs, feed.ready)
                        pe.wait_ge(e.cross_in, e.cross_loads(layer) - 16)
                        for t in range(2):
                            for h in range(CAH):
                                m = nc.tensor.transpose(e.bank[4 + t][:, 128 * h:128 * h + 128], kmr[:, t, 128 * h:128 * h + 128], e.ident)
                            m.then_inc(s["turned"], 1)

                    @block.gpsimd
                    def _(pool):
                        p_q.low(pool)

                    @block.vector
                    def _(dve):
                        feed.vector(dve)
                        for t in range(2):
                            dve.wait_ge(s["turned"], t + 1)
                            nc.vector.tensor_copy(km[:, :, 128 * t:128 * t + 128], e.bank[4 + t][:].rearrange("p (h m) -> p h m", h=CAH)).then_inc(s["km_v"], 1)

                    @block.scalar
                    def _(act):
                        def query(i, j):
                            p_q.wait_tile(act, i, j)
                            nc.scalar.activation(qt[:, j, :], e.bank[j][:, 0:T], ACT.Copy, scale=QSCALE).then_inc(e.bank_free, 1)

                        def gate(i, j):
                            p_q.wait_tile(act, i, j)
                            nc.scalar.activation(gt[:, j, :], e.bank[j][:, 0:T], ACT.Silu).then_inc(e.bank_free, 1)

                        p_q.take_over(act)
                        feed.scalar(act, p_q)
                        for i in range(2):
                            for j in range(NSLOT):
                                (gate if i else query)(i, j)
                                if i == 0 or j < NSPLIT:
                                    p_q.high(act, i, j + NSPLIT)
            prompt_attention(e, f"xp{layer}", CAH, lambda h: qt[:, h, 0:TP], lambda h: km[:, h, :],
                             lambda h, m: vm[:, m, 128 * h:128 * h + 128], lambda h: gt[:, h, 0:TP])
            cross_sample(e, layer, qt, gt, kr, vr)
        x = ctx.enter_context(split_buffers(e, f"xo{layer}", CAH))
        s = ctx.enter_context(stage(nc, f"xout{layer}", Feed.sems))
        add_projection(e, p_out, Feed(e, s, x, CAH, lambda c: gt[:, c, :]), nxt, squares=e.squares)


class Pages:
    QUAD = 4

    def __init__(self, e, ctx):
        self.e = e
        self.s = ctx.enter_context(stage(e.nc, "pages", ["pages_in"] + [f"{k}_in{i}" for k in "kv" for i in range(NPG // self.QUAD)]))
        self.table = ctx.enter_context(e.nc.sbuf_tensor("page_table", [1, NB * NPG], I32))
        self.krows = ctx.enter_context(e.nc.sbuf_tensor("key_pages", [128, NPG, 512], F32))
        self.vrows = e.w[:].rearrange("p j (g c) -> p (j g) c", c=512)

    def load(self, eng, kind, b, g, free=None):
        src = self.e.d[f"cache_{kind}"][0].rearrange("n t h c -> n t (h c)")
        dst = self.krows if kind == "k" else self.vrows
        page = eng.value_load(self.table[0:1, ds(b * NPG + g, 1)], min_val=0, max_val=src.shape[0] - 1)
        if free:
            eng.wait_ge(*free)
        eng.dma_start(dst[:, g:g + 1, :], src[ds(page, 1)].rearrange("n t c -> t n c")).then_inc(self.s[f"{kind}_in{g // self.QUAD}"], 16)

    def first(self, sp):
        sp.dma_start(self.table[:], self.e.d["page_table"].rearrange("b n -> (b n)").unsqueeze(0)).then_inc(self.s["pages_in"], 16)
        sp.wait_ge(self.s["pages_in"], 16)
        for g in range(NPG):
            self.load(sp, "k", 0, g)


def moba_sample(e, pages, qt, kt_new, v_new, gt, nxt):
    nc, d = e.nc, e.d
    names = ["zeroed", "tables_in", "q_ready", "k_turned", "kt_out", "scores", "own_scores", "step", "biases",
             "exped", "recips", "p_turned", "pt_v", "pt_s", "v_used", "o_ready", "o_rows", "o_turned", "o_out"]
    QUAD, HALF = Pages.QUAD, NPG // 2
    with ExitStack() as ctx:
        s = ctx.enter_context(stage(nc, "ms", names))
        sb = lambda n, sh, dt=F32: ctx.enter_context(nc.sbuf_tensor(f"ms_{n}", sh, dt))
        past, own = sb("past", [128, PAST]), sb("own", [128, NB, TSA])
        krows, vrows = pages.krows, pages.vrows
        kt = sb("kt", [128, KVH, PAST])
        qb = sb("q", [128, AH, TS])
        gate, rank, drop = sb("gate", [128, NBLK]), sb("rank", [128, NBLK]), sb("drop", [128, NBLK + 1])
        top, dropped, bias, den = [sb(n, [128, NBLK + 1]) for n in ("top", "dropped", "bias", "den")]
        orows = sb("orows", [128, DH])
        above, tied = sb("above", [128, NBLK, NBLK]), sb("tied", [128, NBLK, NBLK])
        nm, den1, rec = sb("negmax", [128, 1]), sb("den_sum", [128, 1]), sb("rec", [128, 1])
        NP = PAST + TSA
        p, pt = sb("p", [128, NP]), sb("pt", [128, (NPG + 1) * 128])
        STEPS = 25
        with nc.Block() as block:
            @block.sync
            def _(sp):
                sp.dma_start(past[:], d["c_past"]).then_inc(s["tables_in"], 16)
                sp.dma_start(own[:], d["c_own"].rearrange("p (b t) -> p b t", b=NB)).then_inc(s["tables_in"], 16)
                with sp.Fori(0, NB - 1) as b:
                    for g in range(NPG):
                        pages.load(sp, "k", b + 1, g, (s["k_turned"], b * NPG + (NPG + g + 1)))
                sp.wait_ge(s["v_used"], NPG + NB * NPG)
                nxt.first_loads(sp)

            @block.gpsimd
            def _(pool):
                with pool.Fori(0, NB) as b:
                    for g in range(NPG):
                        pages.load(pool, "v", b, g, (s["v_used"], b * NPG + (g + 1)))

            @block.tensor
            def _(pe):
                mm = nc.tensor.matmul
                pe.sem_inc(s["k_turned"], NPG)
                pe.sem_inc(s["v_used"], NPG)

                def turn(b, g):
                    if g % QUAD == 0:
                        pe.wait_ge(pages.s[f"k_in{g // QUAD}"], b * 64 + 64)
                    if g >= 2 or not isinstance(b, int):
                        pe.wait_ge(s["kt_out"], b * NPG + (g - 1))
                    for h in range(KVH):
                        m = nc.tensor.transpose(e.bank[g % 2][:, 128 * h:128 * h + 128], krows[:, g, 128 * h:128 * h + 128], e.ident)
                    m.then_inc(s["k_turned"], 1)

                def scores(b, q):
                    pe.wait_ge(s["kt_out"], b * NPG + QUAD * (q + 1))
                    for h in range(KVH):
                        m = mm(e.bank[4 + q][32 * h:32 * h + 32, :], qb[:, 4 * h:4 * h + 4, :].rearrange("p g t -> p (g t)"),
                               kt[:, h, 512 * q:512 * q + 512], start=True, stop=True)
                    m.then_inc(s["scores"], 1)

                def first_scores(b):
                    pe.wait_ge(s["q_ready"], b + 1)
                    scores(b, 0)
                    scores(b, 1)

                def turn_probs(b, f):
                    pe.wait_ge(s["exped"], b * 9 + (2 * f + 3))
                    for a in range(4):
                        m = nc.tensor.transpose(e.bank[4 + f][:, 128 * a:128 * a + 128], p[:, 512 * f + 128 * a:512 * f + 128 * a + 128], e.ident)
                    m.then_inc(s["p_turned"], 1)
                    if f == 0:
                        nc.tensor.transpose(e.bank[3][0:TSA, 0:128], p[:, PAST:NP], e.ident).then_inc(s["p_turned"], 1)

                def values(b, f):
                    if f < 3:
                        pe.wait_ge(s["pt_v"], b * 4 + (f + 2 if f else 1))
                    else:
                        pe.wait_ge(s["pt_s"], b + 1)
                    pe.wait_ge(pages.s[f"v_in{f}"], b * 64 + 64)
                    for g in range(QUAD * f, QUAD * f + QUAD):
                        for h in range(KVH):
                            m = mm(e.bank[2][32 * h:32 * h + 32, 128:256], pt[:, 128 * g + 32 * h:128 * g + 32 * h + 32],
                                   vrows[:, g, 128 * h:128 * h + 128], start=g == 0, stop=False, skip_group_check=True)
                        m.then_inc(s["v_used"], 1)

                def batch(b, last):
                    for g in range(HALF, NPG):
                        turn(b, g)
                        if g % QUAD == QUAD - 1:
                            scores(b, g // QUAD)
                    for h in range(KVH):
                        m = mm(e.bank[2][32 * h:32 * h + 32, 0:TSA], qb[:, 4 * h:4 * h + 4, :].rearrange("p g t -> p (g t)"),
                               kt_new[:, h, TP:T], start=True, stop=True)
                    m.then_inc(s["own_scores"], 1)
                    if not last:
                        for g in range(HALF):
                            turn(b + 1, g)
                    turn_probs(b, 0)
                    turn_probs(b, 1)
                    values(b, 0)
                    turn_probs(b, 2)
                    values(b, 1)
                    turn_probs(b, 3)
                    values(b, 2)
                    values(b, 3)
                    for h in range(KVH):
                        m = mm(e.bank[2][32 * h:32 * h + 32, 128:256], pt[0:TSA, 128 * NPG + 32 * h:128 * NPG + 32 * h + 32],
                               v_new[0:TSA, 128 * h:128 * h + 128], start=False, stop=True, skip_group_check=True)
                    m.then_inc(s["o_ready"], 1)
                    if not last:
                        first_scores(b + 1)
                    pe.wait_ge(s["o_rows"], b + 1)
                    nc.tensor.transpose(e.bank[3][:, 128:256], orows[:], e.ident).then_inc(s["o_turned"], 1)

                for g in range(HALF):
                    turn(0, g)
                first_scores(0)
                with pe.Fori(0, NB - 1) as b:
                    batch(b, False)
                batch(NB - 1, True)

            @block.scalar
            def _(act):
                def evacuate(b, g):
                    act.wait_ge(s["k_turned"], b * NPG + (g + 1 + NPG))
                    nc.scalar.activation(kt[:, :, 128 * g:128 * g + 128], e.bank[g % 2][:].rearrange("p (h t) -> p h t", h=KVH),
                                         ACT.Copy).then_inc(s["kt_out"], 1)

                def batch(b, last):
                    for g in range(HALF, NPG):
                        evacuate(b, g)
                    if not last:
                        for g in range(HALF):
                            evacuate(b + 1, g)
                    act.wait_ge(s["biases"], b + 1)
                    for k in (NBLK, *range(NBLK)):
                        x = p[:, BLK * k:BLK * k + (BLK if k < NBLK else TSA)]
                        nc.scalar.activation(x, x, ACT.Exp, bias=bias[:, k:k + 1], accum_out=den[:, k:k + 1]).then_inc(s["exped"], 1)
                    act.wait_ge(s["p_turned"], b * 5 + 5)
                    nc.scalar.activation(pt[:, 1536:2048], e.bank[7][:], ACT.Copy).then_inc(s["pt_s"], 1)

                for g in range(HALF):
                    evacuate(0, g)
                with act.Fori(0, NB - 1) as b:
                    batch(b, False)
                batch(NB - 1, True)

            @block.vector
            def _(dve):
                v = nc.vector

                def batch(b, last):
                    n = [0]

                    def step(ins):
                        ins.then_inc(s["step"], 1)
                        n[0] += 1

                    def settled():
                        dve.wait_ge(s["step"], b * STEPS + n[0])

                    def past_scores(q):
                        dve.wait_ge(s["scores"], b * 4 + (q + 1))
                        step(v.tensor_reduce(gate[:, 2 * q:2 * q + 2], e.bank[4 + q][:].rearrange("p (a k) -> p a k", a=2), AX.X, ALU.add))
                        step(v.tensor_tensor(p[:, 512 * q:512 * q + 512], e.bank[4 + q][:], past[:, 512 * q:512 * q + 512], ALU.add))
                        settled()
                        step(v.tensor_reduce(top[:, 2 * q:2 * q + 2], p[:, 512 * q:512 * q + 512].rearrange("p (a k) -> p a k", a=2), AX.X, ALU.max))

                    for q in range(4):
                        past_scores(q)
                    dve.wait_ge(s["own_scores"], b + 1)
                    step(v.tensor_tensor(p[:, PAST:NP].unsqueeze(1), e.bank[2][:, 0:TSA].unsqueeze(1), own[:, ds(b, 1), :], ALU.add))
                    settled()
                    step(v.tensor_reduce(top[:, NBLK:NBLK + 1], p[:, PAST:NP], AX.X, ALU.max))
                    gi = gate[:].unsqueeze(1).to_broadcast([128, NBLK, NBLK])
                    gj = gate[:].unsqueeze(2).to_broadcast([128, NBLK, NBLK])
                    step(v.tensor_tensor(above[:], gi, gj, ALU.is_gt))
                    step(v.tensor_tensor(tied[:], gi, gj, ALU.is_equal))
                    settled()
                    step(v.tensor_tensor(tied[:], tied[:], e.const[:, C_TIE:C_TIE + 64].rearrange("p (j i) -> p j i", j=NBLK), ALU.mult))
                    settled()
                    step(v.tensor_tensor(above[:], above[:], tied[:], ALU.add))
                    settled()
                    step(v.tensor_reduce(rank[:], above[:], AX.X, ALU.add))
                    settled()
                    step(v.tensor_scalar(drop[:, 0:NBLK], rank[:], TOPK - 0.5, NEG, ALU.is_gt, ALU.mult))
                    settled()
                    step(v.tensor_scalar(rank[:], gate[:], 0.5 * NEG * BLK, NEG, ALU.is_le, ALU.mult))
                    settled()
                    step(v.tensor_tensor(drop[:, 0:NBLK], drop[:, 0:NBLK], rank[:], ALU.add))
                    settled()
                    step(v.tensor_tensor(dropped[:], top[:], drop[:], ALU.add))
                    settled()
                    step(v.tensor_reduce(nm[:], dropped[:], AX.X, ALU.max, negate=True))
                    settled()
                    v.tensor_scalar(bias[:], drop[:], nm[:], None, ALU.add).then_inc(s["biases"], 1)
                    for f in range(3):
                        dve.wait_ge(s["p_turned"], b * 5 + (f + 2 if f else 1))
                        v.tensor_copy(pt[:, 512 * f:512 * f + 512], e.bank[4 + f][:]).then_inc(s["pt_v"], 1)
                        if f == 0:
                            dve.wait_ge(s["p_turned"], b * 5 + 2)
                            v.tensor_copy(pt[0:TSA, 128 * NPG:128 * NPG + 128], e.bank[3][0:TSA, 0:128]).then_inc(s["pt_v"], 1)
                    dve.wait_ge(s["exped"], b * 9 + 9)
                    step(v.tensor_reduce(den1[:], den[:], AX.X, ALU.add))
                    settled()
                    v.reciprocal(rec[:], den1[:]).then_inc(s["recips"], 1)
                    if not last:
                        v.tensor_copy(qb[:], qt[:, :, ds(b * TS + (TP + TS), TS)]).then_inc(s["q_ready"], 1)
                    dve.wait_ge(s["recips"], b + 1)
                    dve.wait_ge(s["o_ready"], b + 1)
                    v.tensor_scalar(orows[:], e.bank[2][:, 128:256], rec[:], None, ALU.mult).then_inc(s["o_rows"], 1)
                    dve.wait_ge(s["o_turned"], b + 1)
                    go = gt[:, :, ds(b * TS + TP, TS)]
                    v.tensor_tensor(go, go, e.bank[3][:, 128:256].rearrange("p (h t) -> p h t", h=AH), ALU.mult).then_inc(s["o_out"], 1)
                    assert n[0] == STEPS, n

                v.tensor_copy(qb[:], qt[:, :, TP:TP + TS]).then_inc(s["q_ready"], 1)
                v.memset(drop[:, NBLK:NBLK + 1], 0.0).then_inc(s["zeroed"], 1)
                dve.wait_ge(s["zeroed"], 1)
                dve.wait_ge(s["tables_in"], 32)
                with dve.Fori(0, NB - 1) as b:
                    batch(b, False)
                batch(NB - 1, True)


def moba(e, p_in, p_out, nxt):
    nc, d = e.nc, e.d
    with ExitStack() as ctx:
        sb = lambda n, sh: ctx.enter_context(nc.sbuf_tensor(n, sh, F32))
        qt, kt, gt = sb("m_q", [128, AH, T]), sb("m_k", [128, KVH, T]), sb("m_g", [128, AH, T])
        vrows = sb("m_vrows", [128, 3, 512])
        with ExitStack() as c2:
            vt = c2.enter_context(nc.sbuf_tensor("m_v", [128, KVH, T], F32))
            krows = c2.enter_context(nc.sbuf_tensor("m_krows", [128, 3, 512], F32))
            with split_buffers(e, "odd", KC) as x, normed(e, "norm_mix1", e.xt, T, VA_MIX + KC, x, squares=e.squares) as feed:
                with nc.Block() as block:
                    @block.sync
                    def _(sp):
                        p_in.later_loads(sp)

                    @block.tensor
                    def _(pe):
                        p_in.matmuls(pe, feed.rhs, feed.ready)

                    block.vector(feed.vector)

                    @block.gpsimd
                    def _(pool):
                        p_in.low(pool)

                    @block.scalar
                    def _(act):
                        def tile(i, j, dst, func, scale=1.0):
                            p_in.wait_tile(act, i, j)
                            nc.scalar.activation(dst, e.bank[j][:, 0:T].unsqueeze(1), func, scale=scale).then_inc(e.bank_free, 1)
                            if not (isinstance(i, int) and i == p_in.iters - 1 and j >= NSLOT - NSPLIT):
                                p_in.high(act, i, j + NSPLIT)

                        p_in.take_over(act)
                        feed.scalar(act, p_in)
                        with act.Fori(0, 4) as i:
                            for j in range(4):
                                tile(i, j, qt[:, ds(4 * i + j, 1), :], ACT.Copy, QSCALE)
                        for i, dst in ((4, kt), (5, vt)):
                            for j in range(4):
                                tile(i, j, dst[:, j:j + 1, :], ACT.Copy)
                        with act.Fori(0, 3) as i:
                            for j in range(4):
                                tile(i + 6, j, gt[:, ds(4 * i + j, 1), :], ACT.Silu)
                        for j in range(4):
                            tile(9, j, gt[:, 12 + j:13 + j, :], ACT.Silu)
            s = c2.enter_context(stage(nc, "mrows", ["turned", "evac_v", "evac_s", "stored"]))
            fills = []
            for src, dst in ((kt, krows), (vt, vrows)):
                for u in range(3):
                    n = 128 if u < 2 else TSA
                    fills.append(([(128 * h, src[:, h, 128 * u:128 * u + n], 128, n) for h in range(KVH)], n, 512, dst[0:n, u, :]))
            tensor, copies = transposes(e, s, fills)
            with nc.Block() as block:
                block.tensor(tensor)
                block.vector(lambda eng: copies(eng, 0))
                block.scalar(lambda eng: copies(eng, 1))

                @block.gpsimd
                def _(pool):
                    pool.wait_ge(s["evac_v"], 3)
                    pool.wait_ge(s["evac_s"], 3)
                    for n, r in (("k", krows), ("v", vrows)):
                        pool.dma_start(d[f"{n}_prompt_o"][0, 0].rearrange("(t p) h c -> p t (h c)", p=128), r[:, 0:2, :]).then_inc(s["stored"], 16)
                        pool.dma_start(d[f"{n}_sample_o"][0].rearrange("b t h c -> (b t) (h c)"), r[0:TSA, 2, :]).then_inc(s["stored"], 16)
                    pool.wait_ge(s["stored"], 64)
        pctx = ctx.enter_context(ExitStack())
        pages = Pages(e, pctx)
        with ExitStack() as c2:
            dist = c2.enter_context(nc.sbuf_tensor("m_dist", [128, 2, TP], F32))
            s = c2.enter_context(stage(nc, "mdist", ["dist_in"]))
            with nc.Block() as block:
                @block.sync
                def _(sp):
                    sp.dma_start(dist[:], d["c_dist"].rearrange("p (r k) -> p r k", r=2)).then_inc(s["dist_in"], 16)
                    sp.wait_ge(s["dist_in"], 16)
            prompt_attention(e, "mp", AH, lambda h: qt[:, h, 0:TP], lambda h: kt[:, h // G4, 0:TP],
                             lambda h, m: vrows[:, m, 128 * (h // G4):128 * (h // G4) + 128], lambda h: gt[:, h, 0:TP],
                             bias=lambda h: (dist[:], e.const[:, C_SLOPE + h:C_SLOPE + h + 1]), sync=pages.first)
        moba_sample(e, pages, qt, kt, vrows[:, 2, :], gt, p_out)
        pctx.close()
        x = ctx.enter_context(split_buffers(e, "odd_out", KC))
        s = ctx.enter_context(stage(nc, "mout", Feed.sems))
        add_projection(e, p_out, Feed(e, s, x, KC, lambda c: gt[:, c, :]), nxt, squares=e.squares)


def final(e):
    nc, d = e.nc, e.d
    with ExitStack() as ctx:
        s = ctx.enter_context(stage(nc, "final", ["normed", "turned", "evac_v", "evac_s", "stored"]))
        r = ctx.enter_context(nc.sbuf_tensor("final_r", [128, T], F32))
        norm_sums(e, "norm_final", e.xt, T, r, e.squares)
        rows = ctx.enter_context(nc.sbuf_tensor("y_rows", [128, 3, D], F32))
        fills = []
        for c in range(0, KC, 4):
            for u in range(3):
                n = 128 if u < 2 else TSA
                fills.append(([(128 * a, e.xt[:, c + a, 128 * u:128 * u + n], 128, n) for a in range(4)], n, 512, rows[0:n, u, 128 * c:128 * c + 512]))
        tensor, copies = transposes(e, s, fills, {3 * g: [("normed", 4 * g + 4)] for g in range(4)})
        with nc.Block() as block:
            block.tensor(tensor)

            @block.vector
            def _(dve):
                for c in range(KC):
                    x = e.xt[:, c, :]
                    nc.vector.scalar_tensor_tensor(x, x, e.va[:, VA_FIN + c:VA_FIN + c + 1], r[:], ALU.mult, ALU.mult).then_inc(s["normed"], 1)
                copies(dve, 0)
            block.scalar(lambda eng: copies(eng, 1))

            @block.sync
            def _(sp):
                for g in range(4):
                    done = 3 * g + 3
                    sp.wait_ge(s["evac_v"], (done + 1) // 2)
                    sp.wait_ge(s["evac_s"], done // 2)
                    cs = slice(512 * g, 512 * g + 512)
                    sp.dma_start(d["y_prompt_o"][0].rearrange("(u p) n -> p u n", p=128)[:, :, cs], rows[:, 0:2, cs]).then_inc(s["stored"], 16)
                    sp.dma_start(d["y_sample_o"].rearrange("b t n -> (b t) n")[:, cs], rows[0:TSA, 2, cs]).then_inc(s["stored"], 16)
                sp.wait_ge(s["stored"], 16 * 8)


def build(nc, d):
    e = Trunk(nc, d)
    with ExitStack() as ctx:
        sb = lambda n, sh: ctx.enter_context(nc.sbuf_tensor(n, sh, F32))
        e.const = sb("const", [128, C_N])
        e.ident = e.const[:, C_ID:C_ID + 128]
        e.ones = e.const[:, C_ONE:C_ONE + 128]
        e.va, e.vb, e.vc = sb("va", [128, VA_N]), sb("vb", [128, VB_N]), sb("vc", [128, VC_N])
        e.w = sb("w_slots", [128, NSLOT, KC * 128])
        e.xt = sb("xt", [128, KC, T])
        token_sums = sb("squares", [128, T])
        e.squares = token_sums[:]
        by_unit = lambda k: token_sums[:, 96 * k:96 * k + 96].rearrange("p (u h) -> p u h", u=3)
        e.bank = [ctx.enter_context(nc.psum_tensor(f"bank{i}", [128, 512], F32)) for i in range(8)]
        sem = lambda n: ctx.enter_context(nc.semaphore(n))
        e.pe_event, e.bank_free, e.w_hi, e.w_lo = [sem(n) for n in ("pe_event", "bank_free", "w_hi", "w_lo")]
        e.cross_in = sem("cross_in")
        e.cross_loads = lambda layer: (layer + 1) * 16 * (2 + NB + CROSS_V_AHEAD)
        e.w_landed = [sem(f"w_landed{j}") for j in range(NSLOT)]

        w_ev = d["ev_w_in"][0]
        p_kv = [Proj(e, columns(d["ca_w_kv"][l]), 8, ntok=NM) for l in range(2)]
        p_z = Proj(e, columns(w_ev, OFF_Z), 16)
        p_xbc = Proj(e, columns(w_ev, OFF_XBC), CCH)
        p_sc = Proj(e, sc_columns(w_ev), 64)
        p_evy, p_evs = [Proj(e, columns(d["ev_w_out"][0][D * i:D * i + D, :]), 16) for i in (1, 0)][::-1]
        p_xq, p_xo = [None, None], [None, None]
        p_xq[0] = Proj(e, columns(d["ca_w_q"][0]), 8)
        p_xo[0] = Proj(e, wide_columns(d["ca_w_out"][0]), 16, kch=CAH, tiles_per_slot=4)
        p_od = Proj(e, columns(d["od_w_in"][0]), 40)
        p_odo = Proj(e, columns(d["od_w_out"][0]), 16)
        p_xq[1] = Proj(e, columns(d["ca_w_q"][1]), 8)
        p_xo[1] = Proj(e, wide_columns(d["ca_w_out"][1]), 16, kch=CAH, tiles_per_slot=4)
        e.next_proj = p_kv[0]
        with ExitStack() as c2:
            e.memt = c2.enter_context(nc.sbuf_tensor("memt", [128, KC, NM], F32))
            setup(e)
            r = c2.enter_context(nc.sbuf_tensor("mem_r", [128, T], F32))
            norm_sums(e, "norm_mem", e.memt, NM, r)
            stored = c2.enter_context(stage(nc, "mem_out", ["stored"]))["stored"]
            for layer, nxt in enumerate((p_kv[1], p_z)):
                rows = c2.enter_context(nc.sbuf_tensor(f"mem{layer}_kvrows", [128, 2, 2, 512], F32))
                memory_kv(e, layer, p_kv[layer], nxt, r, rows, stored)
        with ExitStack() as c2:
            sb2 = lambda n, sh: c2.enter_context(nc.sbuf_tensor(n, sh, F32))
            e.zs, e.xbc = sb2("zs", [128, KC, T]), sb2("xbc", [128, CCH, T])
            z = Scan()
            e.dt, z.a = by_unit(0), by_unit(1)
            tail = sb2("conv_tail", [128, CCH, 27])
            sctail = sb2("sc_tail", [128, KC, 18])
            with nc.sbuf_tensor("ysc", [128, KC, T], F32) as e.ysc:
                even_projections(e, p_z, p_xbc, p_sc, p_evs, tail, sctail)
                with split_buffers(e, "sc_out", KC) as x:
                    with stage(nc, "sc_out", Feed.sems) as s, ExitStack() as c3:
                        add_projection(e, p_evs, Feed(e, s, x, KC, lambda c: e.ysc[:, c, :]), p_evy, beside=Softplus(e, c3, z))
            with ExitStack() as c3:
                stored = store_tails(e, c3, tail, sctail)
                ssd(e, z, stored)
            with split_buffers(e, "scan_out", KC) as x:
                with gated_group_norm(e, x) as feed:
                    add_projection(e, p_evy, feed, p_xq[0], squares=e.squares)
        cross_attention(e, 0, p_xq[0], p_xo[0], p_od)
        moba(e, p_od, p_odo, p_xq[1])
        cross_attention(e, 1, p_xq[1], p_xo[1], None)
        final(e)


_OUTS = [("y_prompt_o", (1, TP, D)), ("y_sample_o", (NB, TS, D)),
         ("k_prompt_o", (1, 1, TP, KVH, DH)), ("v_prompt_o", (1, 1, TP, KVH, DH)),
         ("conv_prompt_o", (1, 1, CW - 1, CONV_CH)), ("ssm_prompt_o", (1, 1, SSD_HEADS, HD, NST)),
         ("sc_prompt_o", (1, 1, SCW - 1, D)),
         ("mem_k_o", (2, 1, NM, CAH, DH)), ("mem_v_o", (2, 1, NM, CAH, DH)),
         ("k_sample_o", (1, NB, TS, KVH, DH)), ("v_sample_o", (1, NB, TS, KVH, DH)),
         ("conv_sample_o", (1, NB, CW - 1, CONV_CH)), ("ssm_sample_o", (1, NB, SSD_HEADS, HD, NST)),
         ("sc_sample_o", (1, NB, SCW - 1, D))]


def kernel(**inputs):
    import numpy as _np
    import concourse.bacc as _bacc
    from concourse.bass_utils import run_bass_kernel_spmd as _run

    nc = _bacc.Bacc("TRN2", target_bir_lowering=False, num_devices=1)
    arrays = {k: _np.ascontiguousarray(v) for k, v in inputs.items()}
    arrays.update(host_constants())
    d = {k: nc.dram_tensor(f"in_{k}", v.shape, mybir.dt.from_np(v.dtype), kind="ExternalInput").ap()
         for k, v in arrays.items()}
    for name, shape in _OUTS:
        d[name] = nc.dram_tensor(name, shape, F32, kind="ExternalOutput").ap()
    build(nc, d)
    r = _run(nc, [{f"in_{k}": v for k, v in arrays.items()}], core_ids=[0])
    return tuple(r.results[0][name] for name, _ in _OUTS)
```
